# Optimizing a Trainium2 kernel written in Bass

```python
import jax, jax.numpy as jnp
from jax import lax
import numpy as np

D_MODEL = 1024
BATCH = 1
SEQ = 256
DEPTH = 2

GRID_W = 64
CTX_LEN = 256
NA_HEADS = 8
NA_HEAD_DIM = 64
NA_WIDTH = NA_HEADS * NA_HEAD_DIM
NA_KR_MAX = 8
NA_KC = 16
SC_WIDTH = D_MODEL - NA_WIDTH
SC_CONV_W = 3
IN_WIDTH = 3 * NA_WIDTH + 3 * SC_WIDTH
CONF_CONV_W = 31
N_EXPERTS = 16
N_GROUPS = 4
EXPERTS_PER_GROUP = N_EXPERTS // N_GROUPS
TOP_K = 2
EXPERT_FF = 512

N_EVEN = (DEPTH + 1) // 2
N_ODD = DEPTH // 2
EPS = 1e-6

kernel_name = "hybrid_natten_shortconv_conformer_grouped_moe_dit"

def rms_norm(x, g):
    xf = x.astype(jnp.float32)
    y = xf * lax.rsqrt(jnp.mean(xf * xf, axis=-1, keepdims=True) + EPS)
    return (y * g.astype(jnp.float32)).astype(x.dtype)

def layer_norm(x, g, b):
    xf = x.astype(jnp.float32)
    mu = jnp.mean(xf, axis=-1, keepdims=True)
    var = jnp.mean(jnp.square(xf - mu), axis=-1, keepdims=True)
    y = (xf - mu) * lax.rsqrt(var + EPS) * g.astype(jnp.float32) + b.astype(jnp.float32)
    return y.astype(x.dtype)

def modulate(h, shift, scale):
    return h * (1 + scale) + shift

def depthwise_conv(x, w):
    k, ch = w.shape
    return lax.conv_general_dilated(
        x, w[:, None, :].astype(x.dtype), window_strides=(1,),
        padding=[((k - 1) // 2, k // 2)],
        dimension_numbers=("NWC", "WIO", "NWC"), feature_group_count=ch)

def split_heads(t):
    return t.reshape(t.shape[0], t.shape[1], NA_HEADS, NA_HEAD_DIM)

def neighbourhood_attention(q, k, v, k_ctx, v_ctx, rpb):
    b, s, h, dh = q.shape
    rows = s // GRID_W
    kr = min(NA_KR_MAX, rows)
    scale = dh ** -0.5
    qg = q.reshape(b, rows, GRID_W, h, dh)
    kg = k.reshape(b, rows, GRID_W, h, dh)
    vg = v.reshape(b, rows, GRID_W, h, dh)
    cols = np.arange(GRID_W)
    col_start = np.clip(cols - NA_KC // 2, 0, GRID_W - NA_KC)
    col_idx = col_start[:, None] + np.arange(NA_KC)[None, :]
    dc = col_idx - cols[:, None] + (NA_KC - 1)
    rpb_c = rpb.astype(jnp.float32)[:, :, dc]

    def row_block(r):
        rs = jnp.clip(r - kr // 2, 0, rows - kr)
        q_r = lax.dynamic_index_in_dim(qg, r, axis=1, keepdims=False)
        k_rows = lax.dynamic_slice_in_dim(kg, rs, kr, axis=1)
        v_rows = lax.dynamic_slice_in_dim(vg, rs, kr, axis=1)
        k_nb = k_rows[:, :, col_idx]
        v_nb = v_rows[:, :, col_idx]
        dr = rs + jnp.arange(kr) - r + (NA_KR_MAX - 1)
        bias = jnp.transpose(rpb_c[:, dr], (0, 2, 1, 3))
        s_loc = jnp.einsum("bwhd,brwkhd->bhwrk", q_r, k_nb).astype(jnp.float32) * scale + bias[None]
        s_loc = s_loc.reshape(b, h, GRID_W, kr * NA_KC)
        s_ctx = jnp.einsum("bwhd,blhd->bhwl", q_r, k_ctx).astype(jnp.float32) * scale
        p = jax.nn.softmax(jnp.concatenate([s_loc, s_ctx], axis=-1), axis=-1).astype(v.dtype)
        p_loc = p[..., :kr * NA_KC].reshape(b, h, GRID_W, kr, NA_KC)
        p_ctx = p[..., kr * NA_KC:]
        return (jnp.einsum("bhwrk,brwkhd->bwhd", p_loc, v_nb)
                + jnp.einsum("bhwl,blhd->bwhd", p_ctx, v_ctx))

    out = lax.map(row_block, jnp.arange(rows))
    return jnp.transpose(out, (1, 0, 2, 3, 4)).reshape(b, s, h * dh)

def context_attention(q, k, v):
    b, l, h, dh = q.shape
    s = jnp.einsum("blhd,bmhd->bhlm", q, k).astype(jnp.float32) * dh ** -0.5
    p = jax.nn.softmax(s, axis=-1).astype(v.dtype)
    return jnp.einsum("bhlm,bmhd->blhd", p, v).reshape(b, l, h * dh)

SPLITS = [NA_WIDTH, 2 * NA_WIDTH, 3 * NA_WIDTH, 3 * NA_WIDTH + SC_WIDTH, 3 * NA_WIDTH + 2 * SC_WIDTH]

def even_mixer(hx, hc, w_in, rpb, conv_w, w_out, ctx_live):
    q, k, v, gb, gc, hb = jnp.split(hx @ w_in, SPLITS, axis=-1)
    if ctx_live:
        qc, k_c, v_c, gbc, gcc, hbc = jnp.split(hc @ w_in, SPLITS, axis=-1)
    else:
        k_c, v_c = jnp.split(hc @ w_in[:, NA_WIDTH:3 * NA_WIDTH], 2, axis=-1)
    k_c, v_c = split_heads(k_c), split_heads(v_c)
    a_x = neighbourhood_attention(split_heads(q), split_heads(k), split_heads(v), k_c, v_c, rpb)
    b_x = gb * depthwise_conv(gc * hb, conv_w)
    y_x = jnp.concatenate([a_x, b_x], axis=-1) @ w_out
    if not ctx_live:
        return y_x, None
    a_c = context_attention(split_heads(qc), k_c, v_c)
    b_c = gbc * depthwise_conv(gcc * hbc, conv_w)
    y_c = jnp.concatenate([a_c, b_c], axis=-1) @ w_out
    return y_x, y_c

def conformer_conv(h, pw1_w, pw1_b, dw_w, dw_b, ln_g, ln_b, pw2_w, pw2_b):
    a, g = jnp.split(h @ pw1_w + pw1_b, 2, axis=-1)
    u = a * jax.nn.sigmoid(g)
    u = depthwise_conv(u, dw_w) + dw_b
    u = jax.nn.silu(layer_norm(u, ln_g, ln_b))
    return u @ pw2_w + pw2_b

def route(t, router_w, router_b):
    n = t.shape[0]
    scores = jax.nn.sigmoid((t @ router_w).astype(jnp.float32))
    sel = (scores + router_b.astype(jnp.float32)).reshape(n, N_GROUPS, EXPERTS_PER_GROUP)
    grp_score = jnp.sum(lax.top_k(sel, TOP_K)[0], axis=-1)
    g_star = jnp.argmax(grp_score, axis=-1)
    in_grp = jnp.take_along_axis(sel, g_star[:, None, None], axis=1)[:, 0]
    _, loc = lax.top_k(in_grp, TOP_K)
    idx = g_star[:, None] * EXPERTS_PER_GROUP + loc
    w = jnp.take_along_axis(scores, idx, axis=-1)
    w = w / jnp.sum(w, axis=-1, keepdims=True)
    return jnp.sum(jax.nn.one_hot(idx, N_EXPERTS, dtype=jnp.float32) * w[..., None], axis=1)

def moe_ffn(h, router_w, router_b, w1, w3, w2):
    shape = h.shape
    t = h.reshape(-1, shape[-1])
    gates = route(t, router_w, router_b).astype(t.dtype)
    out = jnp.zeros_like(t)
    for e in range(N_EXPERTS):
        y = (jax.nn.silu(t @ w1[e]) * (t @ w3[e])) @ w2[e]
        out = out + gates[:, e:e + 1] * y
    return out.reshape(shape)

def setup_inputs(seed: int = 0) -> dict:
    key = jax.random.key(seed)
    ks = iter(jax.random.split(key, 32))
    nrm = lambda shape, s: jax.random.normal(next(ks), shape, jnp.float32) * s
    d = D_MODEL
    return {
        "x": nrm((BATCH, SEQ, d), 1.0),
        "c": nrm((BATCH, d), 1.0),
        "ctx": nrm((BATCH, CTX_LEN, d), 1.0),
        "c_ctx": nrm((d,), 1.0),
        "norm1_g": 1.0 + nrm((DEPTH, d), 0.02),
        "norm2_g": 1.0 + nrm((DEPTH, d), 0.02),
        "w_mod": nrm((DEPTH, d, 6 * d), 0.5 * d ** -0.5),
        "b_mod": nrm((DEPTH, 6 * d), 0.02),
        "na_w_in": nrm((N_EVEN, d, IN_WIDTH), d ** -0.5),
        "na_rpb": nrm((N_EVEN, NA_HEADS, 2 * NA_KR_MAX - 1, 2 * NA_KC - 1), 0.02),
        "sc_conv_w": nrm((N_EVEN, SC_CONV_W, SC_WIDTH), SC_CONV_W ** -0.5),
        "ab_w_out": nrm((N_EVEN, d, d), d ** -0.5),
        "cf_pw1_w": nrm((N_ODD, d, 2 * d), d ** -0.5),
        "cf_pw1_b": nrm((N_ODD, 2 * d), 0.02),
        "cf_dw_w": nrm((N_ODD, CONF_CONV_W, d), CONF_CONV_W ** -0.5),
        "cf_dw_b": nrm((N_ODD, d), 0.02),
        "cf_ln_g": 1.0 + nrm((N_ODD, d), 0.02),
        "cf_ln_b": nrm((N_ODD, d), 0.02),
        "cf_pw2_w": nrm((N_ODD, d, d), d ** -0.5),
        "cf_pw2_b": nrm((N_ODD, d), 0.02),
        "router_w": nrm((d, N_EXPERTS), d ** -0.5),
        "router_b": nrm((N_EXPERTS,), 0.01),
        "moe_w1": nrm((DEPTH, N_EXPERTS, d, EXPERT_FF), d ** -0.5),
        "moe_w3": nrm((DEPTH, N_EXPERTS, d, EXPERT_FF), d ** -0.5),
        "moe_w2": nrm((DEPTH, N_EXPERTS, EXPERT_FF, d), EXPERT_FF ** -0.5),
        "final_g": 1.0 + nrm((d,), 0.02),
    }

def reference(x, c, ctx, c_ctx, norm1_g, norm2_g, w_mod, b_mod, na_w_in, na_rpb, sc_conv_w,
              ab_w_out, cf_pw1_w, cf_pw1_b, cf_dw_w, cf_dw_b, cf_ln_g, cf_ln_b, cf_pw2_w,
              cf_pw2_b, router_w, router_b, moe_w1, moe_w3, moe_w2, final_g):
    silu_c = jax.nn.silu(c)
    silu_cc = jax.nn.silu(c_ctx)
    cs = ctx
    for i in range(DEPTH):
        j = i // 2
        even = i % 2 == 0
        ctx_live = any(m % 2 == 0 for m in range(i + 1, DEPTH))
        mx = (silu_c @ w_mod[i] + b_mod[i])[:, None, :]
        sh1, sc1, g1, sh2, sc2, g2 = jnp.split(mx, 6, axis=-1)
        hx = modulate(rms_norm(x, norm1_g[i]), sh1, sc1)
        if even or ctx_live:
            mc = silu_cc @ w_mod[i] + b_mod[i]
            csh1, csc1, cg1, csh2, csc2, cg2 = jnp.split(mc, 6, axis=-1)
            hc = modulate(rms_norm(cs, norm1_g[i]), csh1, csc1)
        if even:
            y_x, y_c = even_mixer(hx, hc, na_w_in[j], na_rpb[j], sc_conv_w[j], ab_w_out[j], ctx_live)
        else:
            conf = (cf_pw1_w[j], cf_pw1_b[j], cf_dw_w[j], cf_dw_b[j], cf_ln_g[j], cf_ln_b[j],
                    cf_pw2_w[j], cf_pw2_b[j])
            y_x = conformer_conv(hx, *conf)
            y_c = conformer_conv(hc, *conf) if ctx_live else None
        x = x + g1 * y_x
        x = x + g2 * moe_ffn(modulate(rms_norm(x, norm2_g[i]), sh2, sc2),
                             router_w, router_b, moe_w1[i], moe_w3[i], moe_w2[i])
        if ctx_live:
            cs = cs + cg1 * y_c
            cs = cs + cg2 * moe_ffn(modulate(rms_norm(cs, norm2_g[i]), csh2, csc2),
                                    router_w, router_b, moe_w1[i], moe_w3[i], moe_w2[i])
    return rms_norm(x, final_g)


_drawn_inputs = setup_inputs


def setup_inputs(seed=0):
    import zlib

    import numpy as np

    out = dict(_drawn_inputs(seed))
    spreads = {}
    factors = {'na_rpb': 64.0,
     'cf_pw1_b': 5.407,
     'cf_ln_g': 16.992,
     'cf_ln_b': 7.218,
     'cf_pw2_b': 13.894,
     'final_g': 8.093}
    for name, (base, spread) in spreads.items():
        noise = np.random.default_rng([zlib.crc32(name.encode()), seed]).standard_normal(out[name].shape)
        drawn = base * np.exp(spread * noise) if base else spread * noise
        out[name] = __import__('jax').numpy.asarray(drawn.astype(out[name].dtype))
    for name, factor in factors.items():
        out[name] = (out[name] * factor).astype(out[name].dtype)
    return out
```

```python
from contextlib import ExitStack

import concourse.bass as bass
from concourse import mybir

F32 = mybir.dt.float32
F32R = mybir.dt.float32r
I32 = mybir.dt.int32
ALU = mybir.AluOpType
ACT = mybir.ActivationFunctionType
AX = mybir.AxisListType

P = 128
D = 1024
KC = D // P
SEQ = 256
CTX = 256
NT = SEQ // P
HALF = 512
GRID_W = 64
ROWS = SEQ // GRID_W
HEADS = 8
DH = 64
NA = HEADS * DH
KR_MAX = 8
KCOL = 16
SC = D - NA
TAPS = 31
PAD = (TAPS - 1) // 2
EXPERTS = 16
GROUPS = 4
PER_GROUP = EXPERTS // GROUPS
FF = 512
FC = FF // P
TILES = GROUPS + 1
EPS = 1e-6

UNIT = 1024
RAW = 8
SPL = 6
BLOCK = 256
DENSE = 2
W_EXPERT = 12
W_GROUP = PER_GROUP * W_EXPERT
MOD_BLOCK = 768
MOD_TURN = 2 * KC
MOD_AFTER = [2 + (12 * i) // 5 for i in range(MOD_TURN)]

C_ID, C_TRI, C_ROW, C_SLOT, C_MASK, C_PRIO = 0, P, 2 * P, 2 * P + TILES * P, 2 * P + TILES * P + TILES, 0
C_PRIO = C_MASK + GRID_W
C_FLIP = C_PRIO + GROUPS
C_N = C_FLIP + P
R_C, R_CC, R_CONV, R_PW1, R_DWB, R_LNG, R_LNB = 0, 8, 16, 28, 44, 52, 60
R_N = 68
PE_TAPS = 13

BA, BB, BY, BT, BX = (0, 2), (1, 3), 4, 6, 7


def expert_order():
    out = []
    for e in range(PER_GROUP):
        out += [(e, "w1"), (e, "w3")]
        if e:
            out.append((e - 1, "w2"))
    return out + [(PER_GROUP - 1, "w2")]


def first_stream():
    out = []

    def mod(v):
        out.extend(("mod", v, k) for k in range(KC))

    def w(name, c0, width):
        for c in range(c0, c0 + width, BLOCK):
            out.extend(("w", name, c, h) for h in range(DENSE))

    mod(0)
    mod(1)
    w("in", NA, NA)
    w("in", 2 * NA, NA)
    mod(2)
    mod(3)
    w("in", 0, NA)
    w("in", 3 * NA + SC, SC)
    mod(4)
    w("in", 3 * NA + 2 * SC, SC)
    w("in", 3 * NA, SC)
    mod(5)
    w("out", 0, D)
    return out


def second_stream():
    out = []
    for c in range(0, D, BLOCK):
        out.extend(("w", "pw1", c, h) for h in range(DENSE))
        out.extend(("w", "pw1", D + c, h) for h in range(DENSE))
    for c in range(0, D, BLOCK):
        out.extend(("w", "pw2", c, h) for h in range(DENSE))
    return out


FIRST = first_stream()
SECOND = second_stream()
W_FIRST = sum(u[0] == "w" for u in FIRST)
TURN_UNITS = (W_GROUP + MOD_TURN, W_GROUP)
MOE_U = (len(FIRST), len(FIRST) + GROUPS * TURN_UNITS[0] + len(SECOND))
MOE_W = (W_FIRST, W_FIRST + GROUPS * W_GROUP + len(SECOND))
SECOND_U = len(FIRST) + GROUPS * TURN_UNITS[0]
SECOND_W = W_FIRST + GROUPS * W_GROUP
assert TURN_UNITS[0] % RAW == 0 and TURN_UNITS[1] % RAW == 0 and W_GROUP % SPL == 0


def turn_stream(layer):
    out = []
    for j in range(W_GROUP):
        out.append(("w", j))
        if layer == 0:
            out.extend(("mod", i) for i in range(MOD_TURN) if MOD_AFTER[i] == j)
    assert len(out) == TURN_UNITS[layer]
    return out


TURN = (turn_stream(0), turn_stream(1))


def program(nc, x, c, ctx, c_ctx, norm1_g, norm2_g, w_mod, b_mod, na_w_in, na_rpb, sc_conv_w, ab_w_out,
            cf_pw1_w, cf_pw1_b, cf_dw_w, cf_dw_b, cf_ln_g, cf_ln_b, cf_pw2_w, cf_pw2_b, router_w, router_b,
            moe_w1, moe_w3, moe_w2, final_g, consts, bias_scratch, out):
    with ExitStack() as stack:
        def sb(name, shape, dt=F32):
            return stack.enter_context(nc.sbuf_tensor(name, shape, dt))

        def sem(name):
            return stack.enter_context(nc.semaphore(name))

        raw = sb("raw", [P, RAW, UNIT])
        whi = sb("whi", [P, SPL, UNIT], F32R)
        wlo = sb("wlo", [P, SPL, UNIT], F32R)
        xres = sb("xres", [P, NT, D])
        mods_at = nc.sbuf_base
        mods = sb("mods", [P, 6 * D])
        g2keep = sb("g2keep", [P, D])
        acc = sb("acc", [P, 2, UNIT])
        gB = sb("gB", [P, D])
        cst = sb("cst", [P, C_N])
        ones = sb("ones", [P, P])
        zero = sb("zero", [P, 1])
        cols = sb("cols", [P, R_N])
        dwT = sb("dwT", [P, KC, TAPS])
        rw = sb("rw", [P, KC, EXPERTS])
        rb = sb("rb", [P, EXPERTS])
        stat = sb("stat", [P, 3, 4])
        flag = sb("flag", [P, 2], I32)
        room = nc.sbuf_usable_end - nc.sbuf_base - 64
        arena = nc.sbuf_base + 31 & ~31
        sb("arena", [P, room // 4])

        def at(name, shape, kb, dt=F32, base=None):
            n = 4
            for s in shape[1:]:
                n *= s
            where = (arena if base is None else base) + int(kb * 1024)
            assert base is not None or int(kb * 1024) + n <= room, (name, kb, room)
            return nc.alloc_sbuf_tensor_at(name, shape, dt, offset=where)

        hThi = at("hThi", [P, 2, KC, SEQ], 0, F32R)
        hTlo = at("hTlo", [P, 2, KC, SEQ], 16, F32R)
        hx = at("hx", [P, NT, D], 32)
        hc = at("hc", [P, NT, D], 40)
        ctxt = at("ctxt", [P, NT, D], 52)
        cG = at("cG", [P, D], 60)
        ccB = at("ccB", [P, KC, P], 64)
        stage = at("stage", [R_N, P], 0)
        dwst = at("dwst", [TAPS, D], 1)
        brow = at("brow", [1, 2 * D], 5)
        rpbt = at("rpbt", [HEADS * 7, P], 13)
        kT = at("kT", [P, 4, SEQ + CTX], 32)
        vv = at("vv", [P, 4, NA], 40)
        qT = at("qT", [P, 4, SEQ], 48)
        gcT = at("gcT", [P, 4, SEQ], 52)
        ghp = at("ghp", [P, 4, SEQ + 2], 56)
        cvT = at("cvT", [P, 4, SEQ], 61)
        catHi = at("catHi", [P, KC, SEQ], 65, F32R)
        catLo = at("catLo", [P, KC, SEQ], 0, F32R, base=mods_at)
        prob = at("prob", [P, 2, 512], 8)
        bias = at("bias", [P, 2, NT, SEQ], 12)
        probT = at("probT", [P, 2, 4, P], 24)
        gated = at("gated", [P, 2, SEQ], 28)
        smx = at("smx", [P, 3, 2], 30)
        ytmp = at("ytmp", [P, 2, BLOCK], 30.5)
        hhi = at("hhi", [P, NT, D], 0, F32R)
        hlo = at("hlo", [P, NT, D], 8, F32R)
        htok = at("htok", [P, NT, D], 16)
        xghi = at("xghi", [P, KC, P], 16, F32R)
        xglo = at("xglo", [P, KC, P], 20, F32R)
        silu = at("silu", [P, 2, FF], 24)
        hid = at("hid", [P, FF], 28)
        hidThi = at("hidThi", [P, FC, P], 30, F32R)
        hidTlo = at("hidTlo", [P, FC, P], 32, F32R)
        yg = at("yg", [P, D], 34)
        yhi = at("yhi", [P, D], 38, F32R)
        ylo = at("ylo", [P, D], 42, F32R)
        pick = at("pick", [P, NT, TILES * P], 46, F32R)
        spread = at("spread", [P, SEQ], 51, F32R)
        posB = at("posB", [P, SEQ], 52)
        gslot = at("gslot", [P, TILES, EXPERTS], 53)
        gspill = at("gspill", [P, PER_GROUP], 53.5)
        diag = at("diag", [P, NT, P], 54)
        rt = at("rt", [P, 14, NT, EXPERTS], 55)
        gatehi = at("gatehi", [P, NT, EXPERTS], 57, F32R)
        gatelo = at("gatelo", [P, NT, EXPERTS], 57.25, F32R)
        hTr = at("hTr", [P, KC, SEQ], 60)
        xg32 = at("xg32", [P, KC, P], 60)
        spraw = at("spraw", [P, 2, HALF], 64)
        hidT32 = at("hidT32", [P, FC, P], 68)
        fThi = at("fThi", [P, KC, SEQ], 0, F32R)
        fTlo = at("fTlo", [P, KC, SEQ], 8, F32R)
        uT = at("uT", [P, KC, SEQ + 2 * PAD], 16)
        sq = at("sq", [P, KC, SEQ], 16)
        cT = at("cT", [P, KC, SEQ], 25)
        sg = at("sg", [P, 2, SEQ], 33)
        mB = at("mB", [P, SEQ], 35)
        rB = at("rB", [P, SEQ], 36)
        sThi = at("sThi", [P, KC, SEQ], 37, F32R)
        sTlo = at("sTlo", [P, KC, SEQ], 45, F32R)
        fh = at("fh", [P, NT, D], 53)
        sT = at("sT", [P, KC, SEQ], 53)
        pbB = at("pbB", [P, D], 61)
        dg = at("dg", [P, 4, P], 65)
        ytmp2 = at("ytmp2", [P, 2, BLOCK], 67)

        ps = stack.enter_context(nc.psum_tensor("ps", [P, 8, HALF], F32))

        ident = cst[:, C_ID:C_ID + P]

        consts_in = sem("consts_in")
        rows_in = sem("rows_in")
        x_in = sem("x_in")
        small_in = sem("small_in")
        pw2b_in = sem("pw2b_in")
        raw_in = [sem(f"raw_in{i}") for i in range(RAW)]
        w_rounded = sem("w_rounded")
        unit_done = sem("unit_done")
        w_used = sem("w_used")
        gb_in = sem("gb_in")
        g_folded = sem("g_folded")
        acc_clear = sem("acc_clear")
        acc_in = [sem("acc_in0"), sem("acc_in1")]
        mod_spread = sem("mod_spread")
        mod_copied = sem("mod_copied")
        ones_set = sem("ones_set")
        rows_T = sem("rows_T")
        cols_set = sem("cols_set")
        cc_set = sem("cc_set")
        ctx_unit = sem("ctx_unit")
        ctx_mod = sem("ctx_mod")
        squares = sem("squares")
        meansq = sem("meansq")
        root = sem("root")
        h_set = sem("h_set")
        h_T = sem("h_T")
        hT_rounded = sem("hT_rounded")
        hT_rest = sem("hT_rest")
        proj = sem("proj")
        proj_taken = sem("proj_taken")
        proj_vec = sem("proj_vec")
        b_set = sem("b_set")
        b_rounded = sem("b_rounded")
        rpb_set = sem("rpb_set")
        zero_set = sem("zero_set")
        rpb_in = sem("rpb_in")
        rpb_out = sem("rpb_out")
        bias_in = [sem("bias_in0"), sem("bias_in1")]
        bias_masked = sem("bias_masked")
        scores = sem("scores")
        biased = sem("biased")
        exped = sem("exped")
        normed = sem("normed")
        prob_T = sem("prob_T")
        probT_set = sem("probT_set")
        attended = sem("attended")
        a_rounded = sem("a_rounded")
        a_rest = sem("a_rest")
        x_mixed = sem("x_mixed")
        g2_kept = sem("g2_kept")
        vec = sem("vec")
        routed = sem("routed")
        route_pe = sem("route_pe")
        route_act = sem("route_act")
        flag_set = sem("flag_set")
        y_clear = sem("y_clear")
        gathered = sem("gathered")
        layer_out = sem("layer_out")
        xg_rounded = sem("xg_rounded")
        xg_rest = sem("xg_rest")
        silu_set = sem("silu_set")
        hid_set = sem("hid_set")
        hid_T = sem("hid_T")
        hidT_rounded = sem("hidT_rounded")
        hidT_rest = sem("hidT_rest")
        y_scaled = sem("y_scaled")
        y_rounded = sem("y_rounded")
        y_rest = sem("y_rest")
        scattered = sem("scattered")
        x_added = sem("x_added")
        gate_set = sem("gate_set")
        diag_set = sem("diag_set")
        diag_used = sem("diag_used")
        conv_set = sem("conv_set")
        ln_sum = sem("ln_sum")
        centred = sem("centred")
        sq_set = sem("sq_set")
        s_act = sem("s_act")
        s_rounded = sem("s_rounded")
        s_rest = sem("s_rest")
        out_set = sem("out_set")
        out_done = sem("out_done")
        sp = [{n: sem(f"spill_{n}{L}") for n in ("in0", "in1", "x", "used", "pe", "silu", "hid", "hT", "y",
                                               "yhi", "ylo", "add")} for L in range(2)]

        w_dram = {
            "in": na_w_in[0].rearrange("(k p) n -> p k n", p=P),
            "out": ab_w_out[0].rearrange("(k p) n -> p k n", p=P),
            "pw1": cf_pw1_w[0].rearrange("(k p) n -> p k n", p=P),
            "pw2": cf_pw2_w[0].rearrange("(k p) n -> p k n", p=P),
        }

        def dense(tile, n, h=None):
            return tile[:, n % (RAW if tile is raw else SPL), :].rearrange("p (k n) -> p k n", k=KC // DENSE)

        def moe_slot(tile, n):
            return tile[:, n % (RAW if tile is raw else SPL), :]

        def tile_done(eng, n):
            which, value = TILE_END[n]
            eng.wait_ge(proj if which == "proj" else w_used, value)

        block = stack.enter_context(nc.Block())

        @block.sync
        def _(eng):
            def free(u):
                if not isinstance(u, int) or u >= RAW:
                    eng.wait_ge(unit_done, u - RAW + 1)

            def load_dense(stream, u0):
                for i, unit in enumerate(stream):
                    u = u0 + i
                    free(u)
                    if unit[0] == "mod":
                        _, v, k = unit
                        eng.dma_start(raw[:, u % RAW, :], w_mod[0, k * P:(k + 1) * P, v * D:(v + 1) * D]) \
                           .then_inc(raw_in[u % RAW], 16)
                    else:
                        _, name, c0, h = unit
                        eng.dma_start(dense(raw, u), w_dram[name][:, 4 * h:4 * h + 4, c0:c0 + BLOCK]) \
                           .then_inc(raw_in[u % RAW], 16)

            def load_experts(L):
                order = expert_order()
                with eng.Fori(0, GROUPS) as g:
                    for pos, (kind, j) in enumerate(TURN[L]):
                        slot = (MOE_U[L] + pos) % RAW
                        free(g * TURN_UNITS[L] + (MOE_U[L] + pos))
                        if kind == "mod":
                            c0 = 2 * MOD_BLOCK * g + MOD_BLOCK * (j // KC)
                            eng.dma_start(raw[:, slot, 0:MOD_BLOCK],
                                          w_mod[1, (j % KC) * P:(j % KC + 1) * P, bass.ds(c0, MOD_BLOCK)]) \
                               .then_inc(raw_in[slot], 16)
                            continue
                        e, name = order[j // 4]
                        q = j % 4
                        table = {"w1": moe_w1, "w3": moe_w3, "w2": moe_w2}[name]
                        src = table[L, bass.ds(g * PER_GROUP + e, 1)]
                        if name == "w2":
                            src = src[0, q * P:(q + 1) * P, :]
                            dst = raw[:, slot, :]
                        else:
                            src = src[0].rearrange("(k p) n -> p k n", p=P)[:, 2 * q:2 * q + 2, :]
                            dst = raw[:, slot, :].rearrange("p (k n) -> p k n", k=2)
                        eng.dma_start(dst, src).then_inc(raw_in[slot], 16)

            def load_spill(L):
                s = sp[L]
                eng.wait_ge(flag_set, L + 1)
                over = eng.value_load(flag[0:1, 0:1], min_val=0, max_val=1)
                group = eng.value_load(flag[0:1, 1:2], min_val=0, max_val=GROUPS - 1)
                with eng.If(over > 0):
                    n = 0
                    for e in range(PER_GROUP):
                        for table in (moe_w1, moe_w3, moe_w2):
                            src = table[L, bass.ds(group * PER_GROUP + e, 1)][0]
                            for q in range(KC):
                                if n >= 2:
                                    eng.wait_ge(s["used"], n - 1)
                                if table is moe_w2:
                                    part = src[(q // 2) * P:(q // 2 + 1) * P, (q % 2) * HALF:(q % 2 + 1) * HALF]
                                else:
                                    part = src[q * P:(q + 1) * P, :]
                                if n < 2:
                                    eng.wait_ge(scattered, (L + 1) * 4 * (GROUPS + 1))
                                eng.dma_start(spraw[:, n % 2, :], part).then_inc(s[f"in{n % 2}"], 16)
                                n += 1
                with eng.Else():
                    eng.nop()
                eng.end_ifs()

            eng.dma_start(ctxt[:], ctx[0].rearrange("(t p) d -> p t d", p=P)).then_inc(x_in, 16)
            eng.dma_start(xres[:], x[0].rearrange("(t p) d -> p t d", p=P)).then_inc(x_in, 16)
            load_dense(FIRST, 0)
            load_experts(0)
            load_spill(0)
            load_dense(SECOND, SECOND_U)
            load_experts(1)
            load_spill(1)
            for t in range(NT):
                eng.wait_ge(out_set, t + 1)
                eng.dma_start(out[0, t * P:(t + 1) * P, :], fh[:, t, :]).then_inc(out_done, 16)
            eng.wait_ge(out_done, 16 * NT)

        @block.gpsimd
        def _(eng):
            nc.gpsimd.memset(ones[:], 1.0).then_inc(ones_set, 1)
            nc.gpsimd.memset(zero[:], 0.0).then_inc(zero_set, 1)
            nc.gpsimd.memset(rpbt[:], 0.0).then_inc(rpb_set, 1)

            def clear(b, slot, width, src, spread_before):
                if spread_before is not None:
                    eng.wait_ge(mod_spread, spread_before)
                nc.gpsimd.memset(acc[:, slot, 0:width], 0.0).then_inc(acc_clear, 1)
                eng.wait_ge(acc_clear, b + 1)
                eng.dma_start(acc[0:1, slot, 0:width], src).then_inc(acc_in[slot], 16)

            def load_g(n, src):
                if n:
                    eng.wait_ge(g_folded, n)
                eng.dma_start(gB[:], src.partition_broadcast(P)).then_inc(gb_in, 16)

            for b in range(2):
                clear(b, b, D, b_mod[0:1, b * D:(b + 1) * D], None)
            load_g(0, norm1_g[0])
            eng.wait_ge(rpb_set, 1)
            for h in range(HEADS):
                eng.dma_start(rpbt[h * 7:(h + 1) * 7, 48:48 + 2 * KCOL - 1], na_rpb[0, h, 4:11, :]).then_inc(rpb_in, 16)
            eng.wait_ge(rpb_in, 16 * HEADS)
            eng.dma_start(bias_scratch, rpbt[:]).then_inc(rpb_out, 16)
            for b in range(2, 6):
                clear(b, b % 2, D, b_mod[0:1, b * D:(b + 1) * D], 2 * (b - 1))
                if b == 2:
                    load_g(1, norm2_g[0])
            eng.wait_ge(rpb_out, 16)
            for h in range(HEADS):
                if h == 0:
                    tile_done(eng, 11)
                if h >= 2:
                    eng.wait_ge(scores, 2 * (h - 1))
                for t in range(NT):
                    for half in range(2):
                        r = 2 * t + half
                        src = bass.AP(tensor=bias_scratch.tensor, offset=(h * 7 + 3 - r) * P,
                                      ap=[[1, GRID_W], [P, ROWS], [1, GRID_W]])
                        dst = bias[half * GRID_W:(half + 1) * GRID_W, h % 2, t, :].rearrange("p (r c) -> p r c", r=ROWS)
                        eng.dma_start(dst, src).then_inc(bias_in[h % 2], 16)
                eng.wait_ge(bias_in[h % 2], 64 * (h // 2 + 1))
                full = bias[:, h % 2].rearrange("p t (r c) -> p (t r) c", r=ROWS)
                mask = cst[:, C_MASK:C_MASK + GRID_W].unsqueeze(1).broadcast_to([P, NT * ROWS, GRID_W])
                nc.gpsimd.tensor_tensor(full, full, mask, ALU.add).then_inc(bias_masked, 1)
            load_g(2, norm1_g[1])
            eng.wait_ge(zero_set, 1)
            with eng.Fori(0, GROUPS) as g:
                for s in range(2):
                    b = 6 + s
                    eng.wait_ge(mod_spread, g * 4 + 2 * (b - 1))
                    none = zero[:].broadcast_to([P, MOD_BLOCK])
                    nc.gpsimd.tensor_tensor(acc[:, s, 0:MOD_BLOCK], none, none, ALU.add).then_inc(acc_clear, 1)
                    eng.wait_ge(acc_clear, g * 2 + (b + 1))
                    eng.dma_start(acc[0:1, s, 0:MOD_BLOCK], b_mod[1:2, bass.ds(2 * MOD_BLOCK * g + MOD_BLOCK * s, MOD_BLOCK)]) \
                       .then_inc(acc_in[s], 16)
            eng.wait_ge(h_T, 13)
            eng.dma_start(pbB[:], cf_pw2_b[0].partition_broadcast(P)).then_inc(pw2b_in, 16)
            load_g(3, norm2_g[1])
            load_g(4, final_g)
            for s in acc_in:
                eng.wait_ge(s, 16 * (3 + GROUPS))
            eng.wait_ge(gb_in, 16 * 5)

        @block.scalar
        def _(eng):
            A = nc.scalar

            def round_dense(u, n):
                eng.wait_ge(raw_in[u % RAW], 16 * (u // RAW + 1))
                if n >= SPL:
                    eng.wait_ge(w_used, n - SPL + 1)
                A.copy(whi[:, n % SPL, :], raw[:, u % RAW, :]).then_inc(w_rounded, 1)

            def round_turn(L, g, pos, j):
                u = MOE_U[L] + pos
                eng.wait_ge(raw_in[u % RAW], g * (16 * TURN_UNITS[L] // RAW) + 16 * (u // RAW + 1))
                eng.wait_ge(w_used, g * W_GROUP + (MOE_W[L] + j - SPL + 1))
                A.copy(whi[:, (MOE_W[L] + j) % SPL, :], raw[:, u % RAW, :]).then_inc(w_rounded, 1)

            def copy_mod(b):
                for i in range(2):
                    eng.wait_ge(mod_spread, 2 * b + i + 1)
                    A.copy(mods[:, b * D + i * HALF:b * D + (i + 1) * HALF], ps[:, 6 + i, :]).then_inc(mod_copied, 1)

            def norm(n, srcs, dsts):
                for i, (s, d) in enumerate(zip(srcs, dsts)):
                    A.activation(d, s, ACT.Square, accum_out=stat[:, 0, i:i + 1]).then_inc(squares, 1)
                eng.wait_ge(meansq, n)
                A.activation(stat[:, 2, 0:len(srcs)], stat[:, 1, 0:len(srcs)], ACT.Sqrt).then_inc(root, 1)

            units = [(u, unit) for u, unit in enumerate(FIRST)]
            dense_units = [u for u, unit in units if unit[0] == "w"]
            pending = iter(list(enumerate(dense_units)))

            def round_upto(k):
                for n, u in pending_list[:]:
                    if n < k:
                        round_dense(u, n)
                        pending_list.remove((n, u))
            pending_list = list(pending)

            eng.dma_start(cst[:], consts).then_inc(consts_in, 16)
            eng.dma_start(stage[R_C:R_C + 8, :], c.rearrange("a (k p) -> (a k) p", p=P)).then_inc(rows_in, 16)
            eng.dma_start(stage[R_CC:R_CC + 8, :], c_ctx.rearrange("(k p) -> k p", p=P)).then_inc(rows_in, 16)
            eng.dma_start(brow[0:1, :], b_mod[0:1, 0:2 * D]).then_inc(rows_in, 16)
            eng.dma_start(stage[R_CONV:R_CONV + 12, :], sc_conv_w[0].rearrange("t (k p) -> (t k) p", p=P)).then_inc(rows_in, 16)
            eng.dma_start(stage[R_PW1:R_PW1 + 16, :], cf_pw1_b[0].rearrange("(k p) -> k p", p=P)).then_inc(rows_in, 16)
            eng.dma_start(stage[R_DWB:R_DWB + 8, :], cf_dw_b[0].rearrange("(k p) -> k p", p=P)).then_inc(rows_in, 16)
            eng.dma_start(stage[R_LNG:R_LNG + 8, :], cf_ln_g[0].rearrange("(k p) -> k p", p=P)).then_inc(rows_in, 16)
            eng.dma_start(stage[R_LNB:R_LNB + 8, :], cf_ln_b[0].rearrange("(k p) -> k p", p=P)).then_inc(rows_in, 16)
            eng.dma_start(dwst[:], cf_dw_w[0]).then_inc(rows_in, 16)
            eng.dma_start(rw[:], router_w.rearrange("(k p) n -> p k n", p=P)).then_inc(small_in, 16)
            eng.dma_start(rb[:], router_b.partition_broadcast(P)).then_inc(small_in, 16)
            eng.wait_ge(rows_T, 1)
            A.activation(cols[:, 0:16], ps[:, 6, 0:16], ACT.Silu).then_inc(cols_set, 1)
            A.copy(cols[:, 16:R_N], ps[:, 6, 16:R_N]).then_inc(cols_set, 1)
            eng.wait_ge(rows_T, 2)
            A.copy(dwT[:].rearrange("p k t -> p (k t)"), ps[:, 7, 0:KC * TAPS]).then_inc(cols_set, 1)
            eng.wait_ge(cols_set, 3)
            eng.wait_ge(ones_set, 1)
            for k in range(KC):
                A.activation(ccB[:, k, :], ones[:], ACT.Copy, scale=cols[:, R_CC + k:R_CC + k + 1]).then_inc(cc_set, 1)
            eng.wait_ge(x_in, 32)
            norm(1, [xres[:, 0], xres[:, 1], ctxt[:, 0], ctxt[:, 1]], [hx[:, 0], hx[:, 1], hc[:, 0], hc[:, 1]])
            copy_mod(0)
            copy_mod(1)
            round_upto(6)
            eng.wait_ge(rpb_out, 16)
            for i in range(4):
                for a in range(2):
                    n = 2 * i + a
                    eng.wait_ge(h_T, n + 1)
                    A.copy(hThi[:, i // 2, 4 * a:4 * a + 4, (i % 2) * P:(i % 2 + 1) * P],
                           ps[:, n, :].rearrange("p (k n) -> p k n", k=4)).then_inc(hT_rounded, 1)
            for n in range(4):
                tile_done(eng, n)
                A.copy(kT[:, n, :], ps[:, n % 4, :]).then_inc(proj_taken, 1)
                if n % 2 == 1:
                    round_upto(6 + n + 1)
            for n in range(8):
                blk, tile = n // 4, n % 4
                tile_done(eng, 4 + n)
                A.copy(vv[:, tile, blk * BLOCK:(blk + 1) * BLOCK], ps[:, n % 4, 0:BLOCK]).then_inc(proj_taken, 1)
                if n % 4 == 3:
                    round_upto(10 + 2 * (blk + 1))
            copy_mod(2)
            copy_mod(3)
            for n in range(4):
                tile_done(eng, 12 + n)
                A.mul(qT[:, n, :], ps[:, n % 4, 0:SEQ], float(DH) ** -0.5).then_inc(proj_taken, 1)
                if n % 2 == 1:
                    round_upto(14 + n + 1)
            for n in range(4):
                tile_done(eng, 16 + n)
                A.copy(gcT[:, n, :], ps[:, n % 4, 0:SEQ]).then_inc(proj_taken, 1)
                if n % 2 == 1:
                    round_upto(18 + n + 1)
            copy_mod(4)
            round_upto(24)
            for n in range(4):
                eng.wait_ge(b_set, n + 1)
                A.copy(catHi[:, 4 + n, :], gated[:, n % 2, :]).then_inc(b_rounded, 1)
            for n in range(16 + 1):
                if n < 16:
                    eng.wait_ge(biased, n + 1)
                    if n >= 2:
                        eng.wait_ge(prob_T, n - 1)
                    A.activation(prob[:, n % 2, :], ps[:, 4 + n % 2, :], ACT.Exp, bias=smx[:, 0, n % 2:n % 2 + 1],
                                 accum_out=smx[:, 1, n % 2:n % 2 + 1]).then_inc(exped, 1)
                if n >= 1:
                    m = n - 1
                    eng.wait_ge(prob_T, m + 1)
                    if m >= 2:
                        eng.wait_ge(attended, m - 1)
                    A.copy(probT[:, m % 2], ps[:, m % 2, :].rearrange("p (k n) -> p k n", k=4)).then_inc(probT_set, 1)
                    if m % 4 == 3:
                        hp = m // 4
                        eng.wait_ge(attended, m + 1)
                        A.copy(catHi[:, hp, :], ps[:, 2 + hp % 2, 0:SEQ]).then_inc(a_rounded, 1)
            copy_mod(5)
            round_upto(len(dense_units))

            def experts(L):
                eng.wait_ge(x_mixed, (L + 1) * 8)
                if L == 0:
                    eng.wait_ge(mod_copied, 12)
                    A.copy(g2keep[:], mods[:, 5 * D:6 * D]).then_inc(g2_kept, 1)
                else:
                    A.copy(g2keep[:], mods[:, 5 * D:6 * D]).then_inc(g2_kept, 1)
                norm(2 + 2 * L, [xres[:, 0], xres[:, 1]], [htok[:, 0], htok[:, 1]])
                for t in range(NT):
                    for a in range(2):
                        n = 8 + 8 * L + 2 * t + a
                        eng.wait_ge(h_T, n + 1)
                        A.copy(hTr[:, 4 * a:4 * a + 4, t * P:(t + 1) * P],
                               ps[:, 2 * t + a, :].rearrange("p (k n) -> p k n", k=4)).then_inc(hT_rounded, 1)
                for t in range(NT):
                    eng.wait_ge(h_set, 4 + 4 * L + t + 1)
                    A.copy(hhi[:, t, :], htok[:, t, :]).then_inc(route_act, 1)
                eng.wait_ge(route_pe, 4 * L + 1)
                A.activation(rt[:, 0].rearrange("p t n -> p (t n)"), ps[:, BX, 0:NT * EXPERTS], ACT.Sigmoid) \
                 .then_inc(route_act, 1)
                eng.wait_ge(routed, 2 * L + 1)
                A.copy(gatehi[:], rt[:, 10]).then_inc(route_act, 1)
                eng.wait_ge(route_pe, 4 * L + 3)
                A.copy(posB[:], ps[:, BT, 0:SEQ]).then_inc(route_act, 1)
                eng.wait_ge(route_pe, 4 * L + 4)
                A.copy(gslot[:].rearrange("p t n -> p (t n)"), ps[:, BX, 0:TILES * EXPERTS]).then_inc(route_act, 1)
                eng.wait_ge(gathered, 5 * L + 1)
                for a in range(2):
                    A.copy(xghi[:, 4 * a:4 * a + 4, :], ps[:, a, :].rearrange("p (k n) -> p k n", k=4)).then_inc(xg_rounded, 1)

                def silu_of(g, e):
                    eng.wait_ge(w_used, g * W_GROUP + (MOE_W[L] + W13[e] + 4))
                    A.activation(silu[:, e % 2, :], ps[:, BA[e % 2], :], ACT.Silu).then_inc(silu_set, 1)

                def hidT_round(g, e):
                    eng.wait_ge(hid_T, g * PER_GROUP + (16 * L + e + 1))
                    A.copy(hidThi[:], ps[:, BT, :].rearrange("p (k n) -> p k n", k=4)).then_inc(hidT_rounded, 1)

                def y_round(g):
                    eng.wait_ge(y_scaled, g + (5 * L + 1))
                    A.copy(yhi[:], yg[:]).then_inc(y_rounded, 1)

                def mod_piece(g, s, i):
                    eng.wait_ge(mod_spread, g * 4 + (12 + 2 * s + i + 1))
                    w = MOD_BLOCK // 2
                    A.copy(mods[:, bass.ds(2 * MOD_BLOCK * g + (MOD_BLOCK * s + i * w), w)], ps[:, BX, 0:w]).then_inc(mod_copied, 1)

                with eng.Fori(0, GROUPS) as g:
                    j = -1
                    for pos, (kind, jj) in enumerate(TURN[L]):
                        if kind == "mod":
                            continue
                        j = jj
                        if j == 6:
                            y_round(g)
                        for e in range(PER_GROUP):
                            if j == W13[e] + 4 + 5:
                                silu_of(g, e)
                            if j == HID_T[e] + 6:
                                hidT_round(g, e)
                        if L == 0:
                            if j == MOD_PE[0] + 6:
                                mod_piece(g, 0, 0)
                            if j == MOD_PE[1] + 6:
                                mod_piece(g, 0, 1)
                            if j == MOD_PE[2] + 6:
                                mod_piece(g, 1, 0)
                        round_turn(L, g, pos, j)
                    hidT_round(g, PER_GROUP - 1)
                    eng.wait_ge(gathered, g + (5 * L + 2))
                    for a in range(2):
                        A.copy(xghi[:, 4 * a:4 * a + 4, :], ps[:, a, :].rearrange("p (k n) -> p k n", k=4)).then_inc(xg_rounded, 1)
                    if L == 0:
                        mod_piece(g, 1, 1)
                y_round(GROUPS)
                s = sp[L]
                eng.wait_ge(flag_set, L + 1)
                over = eng.value_load(flag[0:1, 0:1], min_val=0, max_val=1)
                with eng.If(over > 0):
                    for e in range(PER_GROUP):
                        eng.wait_ge(s["used"], 24 * e + KC)
                        A.activation(silu[:, 0, :], ps[:, BA[0], :], ACT.Silu).then_inc(s["silu"], 1)
                        eng.wait_ge(s["pe"], e + 1)
                        A.copy(hidT32[:], ps[:, BT, :].rearrange("p (k n) -> p k n", k=4)).then_inc(s["hT"], 1)
                    eng.wait_ge(s["y"], 1)
                    A.copy(yhi[:], yg[:]).then_inc(s["yhi"], 1)
                with eng.Else():
                    eng.nop()
                eng.end_ifs()

            experts(0)

            eng.wait_ge(layer_out, 1)
            norm(3, [xres[:, 0], xres[:, 1]], [fh[:, 0], fh[:, 1]])
            second = [("w", SECOND_U + i, SECOND_W + i) for i in range(len(SECOND))]

            def round_second(k):
                while second and second[0][2] - SECOND_W < k:
                    _, u, n = second.pop(0)
                    round_dense(u, n)
            round_second(6)
            for t in range(NT):
                for a in range(2):
                    n = 12 + 2 * t + a
                    eng.wait_ge(h_T, n + 1)
                    A.copy(fThi[:, 4 * a:4 * a + 4, t * P:(t + 1) * P],
                           ps[:, 2 * t + a, :].rearrange("p (k n) -> p k n", k=4)).then_inc(hT_rounded, 1)
            nd = 0

            def diags(ch):
                nonlocal nd
                for tap in range(PE_TAPS):
                    if nd >= 4:
                        eng.wait_ge(diag_used, nd - 3)
                    A.activation(dg[:, nd % 4, :], ident, ACT.Copy, scale=dwT[:, ch, tap:tap + 1]).then_inc(diag_set, 1)
                    nd += 1

            for j in range(4):
                for m in range(2):
                    ch = 2 * j + m
                    tile_done(eng, PROJ["pw1"] + 4 * j + 2 + m)
                    if ch >= 2:
                        eng.wait_ge(gate_set, ch - 1)
                    A.activation(sg[:, ch % 2, :], ps[:, 2 + m, 0:SEQ], ACT.Sigmoid,
                                 bias=cols[:, R_PW1 + 8 + ch:R_PW1 + 9 + ch]).then_inc(proj_taken, 1)
                round_second(4 * (j + 1) + 6)
                for m in range(2):
                    diags(2 * j + m)
            round_second(len(SECOND) - 2)
            eng.wait_ge(centred, 1)
            for a in range(2):
                A.activation(sq[:, 4 * a:4 * a + 4, :].rearrange("p k n -> p (k n)"),
                             cT[:, 4 * a:4 * a + 4, :].rearrange("p k n -> p (k n)"), ACT.Square).then_inc(sq_set, 1)
            eng.wait_ge(centred, 2)
            A.activation(rB[:], mB[:], ACT.Sqrt).then_inc(root, 1)
            for ch in range(KC):
                if ch % 2 == 0:
                    eng.wait_ge(centred, 3 + ch // 2)
                A.activation(sT[:, ch, :], cT[:, ch, :], ACT.Silu, bias=cols[:, R_LNB + ch:R_LNB + ch + 1],
                             scale=cols[:, R_LNG + ch:R_LNG + ch + 1]).then_inc(s_act, 1)
                eng.wait_ge(s_act, ch + 1)
                A.copy(sThi[:, ch, :], sT[:, ch, :]).then_inc(s_rounded, 1)
            round_second(len(SECOND))
            experts(1)
            eng.wait_ge(layer_out, 2)
            norm(5, [xres[:, 0], xres[:, 1]], [fh[:, 0], fh[:, 1]])

        @block.vector
        def _(eng):
            V = nc.vector
            own = [0]

            def link(ins):
                own[0] += 1
                ins.then_inc(vec, 1)
                eng.wait_ge(vec, own[0])

            def rest_dense(u, n):
                eng.wait_ge(w_rounded, n + 1)
                V.tensor_tensor(wlo[:, n % SPL, :], raw[:, u % RAW, :], whi[:, n % SPL, :], ALU.subtract).then_inc(unit_done, 1)

            def sum_mod(u, b, k, ctx_too):
                eng.wait_ge(raw_in[u % RAW], 16 * (u // RAW + 1))
                if k == 0:
                    eng.wait_ge(acc_in[b % 2], 16 * (b // 2 + 1))
                else:
                    eng.wait_ge(unit_done, u)
                if ctx_too:
                    eng.wait_ge(ctx_unit, u + 1)
                V.scalar_tensor_tensor(out=acc[:, b % 2, :], in0=raw[:, u % RAW, :], scalar=cols[:, R_C + k:R_C + k + 1],
                                       in1=acc[:, b % 2, :], op0=ALU.mult, op1=ALU.add).then_inc(unit_done, 1)

            todo = [(u, unit) for u, unit in enumerate(FIRST)]
            nw = [0]

            def stream(count_w=None, mod=None):
                while todo:
                    u, unit = todo[0]
                    if unit[0] == "w":
                        if count_w is None or nw[0] >= count_w:
                            return
                        rest_dense(u, nw[0])
                        nw[0] += 1
                    else:
                        if mod is None or unit[1] > mod:
                            return
                        sum_mod(u, unit[1], unit[2], unit[1] < 2)
                    todo.pop(0)

            def mean_eps(n, count):
                eng.wait_ge(squares, n)
                V.tensor_scalar(stat[:, 1, 0:count], stat[:, 0, 0:count], 1.0 / D, EPS, ALU.mult, ALU.add).then_inc(meansq, 1)

            def inv_root(n, count):
                eng.wait_ge(root, n)
                link(V.reciprocal(stat[:, 0, 0:count], stat[:, 2, 0:count]))

            def fold_gain(scale, n):
                eng.wait_ge(gb_in, 16 * n)
                V.scalar_tensor_tensor(out=scale, in0=scale, scalar=1.0, in1=gB[:], op0=ALU.add, op1=ALU.mult).then_inc(g_folded, 1)
                eng.wait_ge(g_folded, n)

            def modulated(dst, src, i, gain, shift):
                link(V.scalar_tensor_tensor(out=dst, in0=src, scalar=stat[:, 0, i:i + 1], in1=gain, op0=ALU.mult, op1=ALU.mult))
                V.tensor_tensor(dst, dst, shift, ALU.add).then_inc(h_set, 1)

            eng.wait_ge(cols_set, 2)
            mean_eps(4, 4)
            stream(mod=1)
            inv_root(1, 4)
            eng.wait_ge(ctx_mod, 2)
            eng.wait_ge(gb_in, 16)
            link(V.scalar_tensor_tensor(out=cG[:].rearrange("p (a n) -> p a n", a=2), in0=ps[:, 2:4, :], scalar=1.0,
                                        in1=gB[:].rearrange("p (a n) -> p a n", a=2), op0=ALU.add, op1=ALU.mult))
            for t in range(NT):
                modulated(hc[:, t, :].rearrange("p (a n) -> p a n", a=2), ctxt[:, t, :].rearrange("p (a n) -> p a n", a=2),
                          2 + t, cG[:].rearrange("p (a n) -> p a n", a=2), ps[:, 0:2, :])
            eng.wait_ge(mod_copied, 4)
            fold_gain(mods[:, D:2 * D], 1)
            for t in range(NT):
                modulated(hx[:, t, :], xres[:, t, :], t, mods[:, D:2 * D], mods[:, 0:D])
            stream(count_w=6)
            for i in range(4):
                for a in range(2):
                    n = 2 * i + a
                    eng.wait_ge(hT_rounded, n + 1)
                    hi = hThi[:, i // 2, 4 * a:4 * a + 4, (i % 2) * P:(i % 2 + 1) * P]
                    lo = hTlo[:, i // 2, 4 * a:4 * a + 4, (i % 2) * P:(i % 2 + 1) * P]
                    V.tensor_tensor(lo, ps[:, n, :].rearrange("p (k n) -> p k n", k=4), hi, ALU.subtract).then_inc(hT_rest, 1)

            def room(n):
                if n > SPL:
                    eng.wait_ge(w_used, n - SPL)

            def stream_w(k):
                while nw[0] < k:
                    room(nw[0] + 1)
                    stream(count_w=nw[0] + 1)

            stream_w(8)
            stream(mod=3)
            stream_w(16)
            stream(mod=4)
            link(V.memset(ghp[:, :, 0:1], 0.0))
            link(V.memset(ghp[:, :, SEQ + 1:SEQ + 2], 0.0))
            for n in range(4):
                if n % 2 == 0:
                    stream_w(18 + n)
                tile_done(eng, 20 + n)
                eng.wait_ge(proj_taken, 16 + n + 1)
                V.tensor_tensor(ghp[:, n, 1:SEQ + 1], ps[:, n % 4, 0:SEQ], gcT[:, n, :], ALU.mult).then_inc(proj_vec, 1)
            for n in range(4):
                if n % 2 == 0:
                    stream_w(22 + n)
                eng.wait_ge(proj_vec, n + 1)
                for tap in range(3):
                    w = cols[:, R_CONV + 4 * tap + n:R_CONV + 4 * tap + n + 1]
                    src = ghp[:, n, tap:tap + SEQ]
                    if tap == 0:
                        link(V.tensor_scalar(cvT[:, n, :], src, w, None, ALU.mult))
                    else:
                        link(V.scalar_tensor_tensor(out=cvT[:, n, :], in0=src, scalar=w, in1=cvT[:, n, :], op0=ALU.mult, op1=ALU.add))
            for n in range(4):
                tile_done(eng, 24 + n)
                if n >= 2:
                    eng.wait_ge(b_rounded, n - 1)
                V.tensor_tensor(gated[:, n % 2, :], ps[:, n % 4, 0:SEQ], cvT[:, n, :], ALU.mult).then_inc(b_set, 1)
                eng.wait_ge(b_rounded, n + 1)
                V.tensor_tensor(catLo[:, 4 + n, :], gated[:, n % 2, :], catHi[:, 4 + n, :], ALU.subtract).then_inc(proj_vec, 1)
            for n in range(16 + 1):
                if n < 16:
                    h, t = n // 2, n % 2
                    eng.wait_ge(scores, n + 1)
                    V.tensor_reduce(smx[:, 0, n % 2:n % 2 + 1], ps[:, 4 + n % 2, :], AX.X, ALU.max, negate=True).then_inc(biased, 1)
                if n >= 1:
                    m = n - 1
                    eng.wait_ge(exped, m + 1)
                    link(V.reciprocal(smx[:, 2, m % 2:m % 2 + 1], smx[:, 1, m % 2:m % 2 + 1]))
                    V.tensor_scalar(prob[:, m % 2, :], prob[:, m % 2, :], smx[:, 2, m % 2:m % 2 + 1], None, ALU.mult).then_inc(normed, 1)
                    if m % 4 == 3 and m >= 4:
                        hp = m // 4 - 1
                        eng.wait_ge(a_rounded, hp + 1)
                        V.tensor_tensor(catLo[:, hp, :], ps[:, 2 + hp % 2, 0:SEQ], catHi[:, hp, :], ALU.subtract).then_inc(a_rest, 1)
                if n == 3:
                    stream(mod=5)
            eng.wait_ge(a_rounded, 4)
            V.tensor_tensor(catLo[:, 3, :], ps[:, 3, 0:SEQ], catHi[:, 3, :], ALU.subtract).then_inc(a_rest, 1)
            stream_w(30)

            def mix(n, base, gate, tmp, extra=None):
                blk, t = n // 2, n % 2
                cols_ = slice(blk * BLOCK, (blk + 1) * BLOCK)
                tile_done(eng, base + n)
                src = ps[:, n % 4, 0:BLOCK]
                if extra is not None:
                    link(V.tensor_tensor(tmp[:, n % 2, :], src, extra[:, cols_], ALU.add))
                    src = tmp[:, n % 2, :]
                link(V.tensor_tensor(tmp[:, n % 2, :], src, gate[:, cols_], ALU.mult))
                V.tensor_tensor(xres[:, t, cols_], xres[:, t, cols_], tmp[:, n % 2, :], ALU.add).then_inc(x_mixed, 1)

            g1 = mods[:, 2 * D:3 * D]
            for n in range(8):
                if n in (2, 4):
                    stream_w(30 + n - (n == 4) * 2)
                mix(n, PROJ["out"], g1, ytmp)
            assert not todo, todo

            def experts(L):
                mean_eps([6, 10][L], 2)
                inv_root([2, 5][L], 2)
                eng.wait_ge(x_mixed, 8 * (L + 1))
                fold_gain(mods[:, 4 * D:5 * D], [2, 4][L])
                for t in range(NT):
                    modulated(htok[:, t, :], xres[:, t, :], t, mods[:, 4 * D:5 * D], mods[:, 3 * D:4 * D])
                for t in range(NT):
                    eng.wait_ge(route_act, 6 * L + t + 1)
                    V.tensor_tensor(hlo[:, t, :], htok[:, t, :], hhi[:, t, :], ALU.subtract).then_inc(vec, 1)
                    own[0] += 1
                (SCO, SEL, PAIR, GRP, EQ, W4, ONE, RANK, T1, GSEL, GATE, POS, RR, T2) = range(14)

                def r(i, n=EXPERTS):
                    return rt[:, i, :, 0:n]

                def grp(i):
                    return rt[:, i].rearrange("p t (g e) -> p t g e", e=PER_GROUP)

                link(V.memset(rt[:, RANK], 0.0))
                eng.wait_ge(route_act, 6 * L + 3)
                eng.wait_ge(small_in, 32)
                link(V.tensor_tensor(r(SEL), r(SCO), rb[:].unsqueeze(1).broadcast_to([P, NT, EXPERTS]), ALU.add))
                sel = grp(SEL)
                pair, p2 = grp(PAIR), grp(T2)
                for d_ in range(1, PER_GROUP):
                    n = PER_GROUP - d_
                    o = pair[:, :, :, 0:3] if d_ == 1 else p2[:, :, :, 0:2] if d_ == 2 else p2[:, :, :, 2:3]
                    link(V.tensor_tensor(o, sel[:, :, :, 0:n], sel[:, :, :, d_:], ALU.add))
                link(V.tensor_tensor(pair[:, :, :, 0:3], pair[:, :, :, 0:3], p2[:, :, :, 0:3], ALU.max))
                link(V.tensor_reduce(r(GRP, GROUPS), pair[:, :, :, 0:3], AX.X, ALU.max))
                link(V.tensor_reduce(r(EQ, 1), r(GRP, GROUPS), AX.X, ALU.max))
                link(V.tensor_tensor(r(W4, GROUPS), r(GRP, GROUPS), r(EQ, 1).broadcast_to([P, NT, GROUPS]), ALU.is_equal))
                prio = cst[:, C_PRIO:C_PRIO + GROUPS].unsqueeze(1).broadcast_to([P, NT, GROUPS])
                link(V.tensor_tensor(r(W4, GROUPS), r(W4, GROUPS), prio, ALU.mult))
                link(V.tensor_reduce(r(EQ, 1), r(W4, GROUPS), AX.X, ALU.max))
                link(V.tensor_tensor(r(ONE, GROUPS), r(W4, GROUPS), r(EQ, 1).broadcast_to([P, NT, GROUPS]), ALU.is_equal))
                rank = grp(RANK)
                for d_ in range(1, PER_GROUP):
                    n = PER_GROUP - d_
                    a, b = sel[:, :, :, 0:n], sel[:, :, :, d_:]
                    link(V.tensor_tensor(p2[:, :, :, 0:n], b, a, ALU.is_gt))
                    link(V.tensor_tensor(rank[:, :, :, 0:n], rank[:, :, :, 0:n], p2[:, :, :, 0:n], ALU.add))
                    link(V.tensor_tensor(p2[:, :, :, 0:n], a, b, ALU.is_ge))
                    link(V.tensor_tensor(rank[:, :, :, d_:], rank[:, :, :, d_:], p2[:, :, :, 0:n], ALU.add))
                link(V.tensor_scalar(r(GSEL), r(RANK), 1.5, None, ALU.is_lt))
                one_b = rt[:, ONE, :, 0:GROUPS].unsqueeze(3).broadcast_to([P, NT, GROUPS, PER_GROUP])
                link(V.tensor_tensor(grp(GSEL), grp(GSEL), one_b, ALU.mult))
                link(V.tensor_tensor(r(T1), r(GSEL), r(SCO), ALU.mult))
                link(V.tensor_reduce(r(T2, 1), r(T1), AX.X, ALU.add))
                link(V.reciprocal(r(EQ, 1), r(T2, 1)))
                V.tensor_tensor(r(GATE), r(T1), r(EQ, 1).broadcast_to([P, NT, EXPERTS]), ALU.mult).then_inc(routed, 1)
                eng.wait_ge(route_pe, 4 * L + 2)
                cnt = ps[:, BX, 64:64 + 3 * GROUPS]
                link(V.tensor_tensor(r(T1, GROUPS), cnt[:, 0:2 * GROUPS].rearrange("p (t g) -> p t g", t=NT), r(ONE, GROUPS), ALU.mult))
                link(V.tensor_reduce(r(POS, 1), r(T1, GROUPS), AX.X, ALU.add))
                link(V.tensor_tensor(r(T1, GROUPS), r(ONE, GROUPS), prio, ALU.mult))
                link(V.tensor_reduce(r(T2, 1), r(T1, GROUPS), AX.X, ALU.add))
                link(V.tensor_scalar(r(T2, 1), r(T2, 1), -float(P), float(P * GROUPS), ALU.mult, ALU.add))
                link(V.tensor_scalar(r(W4, 1), r(POS, 1), P - 0.5, None, ALU.is_gt))
                link(V.tensor_scalar(r(T1, 1), r(T2, 1), -1.0, float(P * GROUPS - P), ALU.mult, ALU.add))
                link(V.tensor_tensor(r(T1, 1), r(T1, 1), r(W4, 1), ALU.mult))
                link(V.tensor_tensor(r(T2, 1), r(T2, 1), r(T1, 1), ALU.add))
                link(V.tensor_tensor(r(POS, 1), r(POS, 1), r(T2, 1), ALU.add))
                for t in range(NT):
                    link(V.tensor_scalar(diag[:, t, :], ident, rt[:, POS, t, 0:1], None, ALU.mult))
                link(V.tensor_scalar(rt[:, RR, 0, 0:GROUPS], cnt[:, 2 * GROUPS:3 * GROUPS], P + 0.5, None, ALU.is_gt))
                link(V.tensor_reduce(rt[:, RR, 1, 0:1], rt[:, RR, 0, 0:GROUPS], AX.X, ALU.add))
                link(V.tensor_tensor(rt[:, RR, 0, 4:8], rt[:, RR, 0, 0:GROUPS], cst[:, C_PRIO:C_PRIO + GROUPS], ALU.mult))
                link(V.tensor_reduce(rt[:, RR, 1, 1:2], rt[:, RR, 0, 4:8], AX.X, ALU.add))
                link(V.tensor_scalar(rt[:, RR, 1, 2:3], rt[:, RR, 1, 0:1], float(GROUPS), None, ALU.mult))
                link(V.tensor_tensor(rt[:, RR, 1, 1:2], rt[:, RR, 1, 2:3], rt[:, RR, 1, 1:2], ALU.subtract))
                V.tensor_copy(flag[:], rt[:, RR, 1, 0:2]).then_inc(flag_set, 1)
                eng.wait_ge(route_act, 6 * L + 4)
                for t in range(NT):
                    link(V.tensor_scalar(pick[:, t, :], cst[:, C_ROW:C_ROW + TILES * P], rt[:, POS, t, 0:1], None, ALU.is_equal))
                V.tensor_tensor(gatelo[:], rt[:, GATE], gatehi[:], ALU.subtract).then_inc(routed, 1)
                V.memset(spread[:].bitcast(F32), 0.0).then_inc(y_clear, 1)
                V.memset(ps[:, BY:BY + 2, :], 0.0).then_inc(y_clear, 1)
                eng.wait_ge(route_act, 6 * L + 6)
                link(V.tensor_reduce(gspill[:], gslot[:, GROUPS, :].rearrange("p (g e) -> p e g", e=PER_GROUP), AX.X, ALU.add))
                eng.wait_ge(y_clear, 2 * L + 2)
                for a in range(2):
                    eng.wait_ge(xg_rounded, 10 * L + a + 1)
                    V.tensor_tensor(xglo[:, 4 * a:4 * a + 4, :], ps[:, a, :].rearrange("p (k n) -> p k n", k=4),
                                    xghi[:, 4 * a:4 * a + 4, :], ALU.subtract).then_inc(xg_rest, 1)

                def rest_turn(g, pos, j):
                    u, n = MOE_U[L] + pos, MOE_W[L] + j
                    eng.wait_ge(w_rounded, g * W_GROUP + (n + 1))
                    V.tensor_tensor(wlo[:, n % SPL, :], raw[:, u % RAW, :], whi[:, n % SPL, :], ALU.subtract).then_inc(unit_done, 1)

                def mod_turn(g, pos, i):
                    u, s, k = MOE_U[L] + pos, i // KC, i % KC
                    eng.wait_ge(raw_in[u % RAW], g * (16 * TURN_UNITS[L] // RAW) + 16 * (u // RAW + 1))
                    if k == 0:
                        eng.wait_ge(acc_in[s], g * 16 + 16 * 4)
                    else:
                        eng.wait_ge(unit_done, g * TURN_UNITS[L] + (MOE_U[L] + MOD_POS[i - 1] + 1))
                    V.scalar_tensor_tensor(out=acc[:, s, 0:MOD_BLOCK], in0=raw[:, u % RAW, 0:MOD_BLOCK],
                                           scalar=cols[:, R_C + k:R_C + k + 1], in1=acc[:, s, 0:MOD_BLOCK],
                                           op0=ALU.mult, op1=ALU.add).then_inc(unit_done, 1)

                def y_scale(g):
                    eng.wait_ge(w_used, g * W_GROUP + MOE_W[L])
                    V.tensor_tensor(yg[:].rearrange("p (a n) -> p a n", a=2), ps[:, BY:BY + 2, :],
                                    g2keep[:].rearrange("p (a n) -> p a n", a=2), ALU.mult).then_inc(y_scaled, 1)

                def y_remainder(g):
                    eng.wait_ge(y_rounded, g + (5 * L + 1))
                    V.tensor_tensor(ylo[:], yg[:], yhi[:], ALU.subtract).then_inc(y_rest, 1)

                def x_add(g, i):
                    t, half = i // 2, i % 2
                    eng.wait_ge(scattered, g * 4 + (20 * L + i + 1))
                    dst = xres[:, t, half * HALF:(half + 1) * HALF]
                    V.tensor_tensor(dst, dst, ps[:, BX, :], ALU.add).then_inc(x_added, 1)

                def set_spread(g):
                    V.tensor_scalar(spread[:], posB[:], cst[:, bass.ds(g + C_SLOT, 1)] if not isinstance(g, int)
                                    else cst[:, C_SLOT + g:C_SLOT + g + 1], None, ALU.is_equal).then_inc(vec, 1)

                def hid_mul(g, e):
                    eng.wait_ge(silu_set, g * PER_GROUP + (16 * L + e + 1))
                    eng.wait_ge(w_used, g * W_GROUP + (MOE_W[L] + W13[e] + 8))
                    gate = gslot[:].rearrange("p t n -> p (t n)")[:, bass.ds(g * (EXPERTS + PER_GROUP) + e, 1)]
                    V.scalar_tensor_tensor(out=hid[:], in0=silu[:, e % 2, :], scalar=gate, in1=ps[:, BB[e % 2], :],
                                           op0=ALU.mult, op1=ALU.mult).then_inc(hid_set, 1)

                def hidT_remainder(g, e):
                    eng.wait_ge(hidT_rounded, g * PER_GROUP + (16 * L + e + 1))
                    V.tensor_tensor(hidTlo[:], ps[:, BT, :].rearrange("p (k n) -> p k n", k=4), hidThi[:], ALU.subtract) \
                     .then_inc(hidT_rest, 1)

                eng.wait_ge(g2_kept, L + 1)
                own0 = own[0]
                with eng.Fori(0, GROUPS) as g:
                    for pos, (kind, j) in enumerate(TURN[L]):
                        if kind == "mod":
                            mod_turn(g, pos, j)
                            continue
                        if j == 5:
                            y_scale(g)
                        if j == 7:
                            y_remainder(g)
                        for e in range(PER_GROUP):
                            if j == W13[e] + 8 + 5:
                                hid_mul(g, e)
                            if j == HID_T[e] + 6:
                                hidT_remainder(g, e)
                        for i in range(4):
                            if j == SCATTER[i] + 6:
                                x_add(g, i)
                        if j == SCATTER[3] + 6:
                            set_spread(g)
                        rest_turn(g, pos, j)
                    hidT_remainder(g, PER_GROUP - 1)
                    for a in range(2):
                        eng.wait_ge(xg_rounded, g * 2 + (10 * L + 3 + a))
                        V.tensor_tensor(xglo[:, 4 * a:4 * a + 4, :], ps[:, a, :].rearrange("p (k n) -> p k n", k=4),
                                        xghi[:, 4 * a:4 * a + 4, :], ALU.subtract).then_inc(xg_rest, 1)
                own[0] = own0 + GROUPS
                y_scale(GROUPS)
                y_remainder(GROUPS)
                for i in range(4):
                    x_add(GROUPS, i)
                s = sp[L]
                eng.wait_ge(flag_set, L + 1)
                over = eng.value_load(flag[0:1, 0:1], min_val=0, max_val=1)
                with eng.If(over > 0):
                    V.tensor_tensor(xg32[:], xghi[:], xglo[:], ALU.add).then_inc(s["x"], 1)
                    V.tensor_scalar(spread[:], posB[:], cst[:, C_SLOT + GROUPS:C_SLOT + GROUPS + 1], None, ALU.is_equal).then_inc(s["x"], 1)
                    for e in range(PER_GROUP):
                        eng.wait_ge(s["silu"], e + 1)
                        eng.wait_ge(s["used"], 24 * e + 16)
                        V.scalar_tensor_tensor(out=hid[:], in0=silu[:, 0, :], scalar=gspill[:, e:e + 1], in1=ps[:, BB[0], :],
                                               op0=ALU.mult, op1=ALU.mult).then_inc(s["hid"], 1)
                    eng.wait_ge(s["used"], 24 * PER_GROUP)
                    V.tensor_tensor(yg[:].rearrange("p (a n) -> p a n", a=2), ps[:, BY:BY + 2, :],
                                    g2keep[:].rearrange("p (a n) -> p a n", a=2), ALU.mult).then_inc(s["y"], 1)
                    eng.wait_ge(s["yhi"], 1)
                    V.tensor_tensor(ylo[:], yg[:], yhi[:], ALU.subtract).then_inc(s["ylo"], 1)
                    for i in range(4):
                        t, half = i // 2, i % 2
                        eng.wait_ge(s["pe"], PER_GROUP + i + 1)
                        dst = xres[:, t, half * HALF:(half + 1) * HALF]
                        V.tensor_tensor(dst, dst, ps[:, BX, :], ALU.add).then_inc(s["add"], 1)
                    eng.wait_ge(s["add"], 4)
                with eng.Else():
                    eng.nop()
                eng.end_ifs()
                eng.wait_ge(x_added, 20 * (L + 1))
                V.memset(stat[:, 1, :], 0.0).then_inc(layer_out, 1)

            experts(0)

            mean_eps(8, 2)
            inv_root(3, 2)
            eng.wait_ge(mod_copied, 12 + 4 * GROUPS)
            fold_gain(mods[:, D:2 * D], 3)
            for t in range(NT):
                modulated(fh[:, t, :], xres[:, t, :], t, mods[:, D:2 * D], mods[:, 0:D])
            second = [(SECOND_U + i, SECOND_W + i) for i in range(len(SECOND))]

            def rest_second(k):
                while second and second[0][1] - SECOND_W < k:
                    u, n = second.pop(0)
                    rest_dense(u, n)
            rest_second(6)
            for t in range(NT):
                for a in range(2):
                    n = 12 + 2 * t + a
                    eng.wait_ge(hT_rounded, n + 1)
                    hi = fThi[:, 4 * a:4 * a + 4, t * P:(t + 1) * P]
                    lo = fTlo[:, 4 * a:4 * a + 4, t * P:(t + 1) * P]
                    V.tensor_tensor(lo, ps[:, 2 * t + a, :].rearrange("p (k n) -> p k n", k=4), hi, ALU.subtract).then_inc(hT_rest, 1)
            link(V.memset(uT[:, :, 0:PAD], 0.0))
            link(V.memset(uT[:, :, PAD + SEQ:], 0.0))

            def conv(ch):
                eng.wait_ge(gate_set, ch + 1)
                for tap in range(PE_TAPS, TAPS):
                    src, w = uT[:, ch, tap:tap + SEQ], dwT[:, ch, tap:tap + 1]
                    if tap == PE_TAPS:
                        link(V.tensor_scalar(cT[:, ch, :], src, w, cols[:, R_DWB + ch:R_DWB + ch + 1], ALU.mult, ALU.add))
                    else:
                        link(V.scalar_tensor_tensor(out=cT[:, ch, :], in0=src, scalar=w, in1=cT[:, ch, :], op0=ALU.mult, op1=ALU.add))
                eng.wait_ge(diag_used, PE_TAPS * (ch + 1))
                V.tensor_tensor(cT[:, ch, :], cT[:, ch, :], ps[:, 4 + ch % 2, 0:SEQ], ALU.add).then_inc(conv_set, 1)

            for j in range(4):
                for m in range(2):
                    ch = 2 * j + m
                    eng.wait_ge(proj_taken, 20 + ch + 1)
                    V.scalar_tensor_tensor(out=uT[:, ch, PAD:PAD + SEQ], in0=ps[:, m, 0:SEQ],
                                           scalar=cols[:, R_PW1 + ch:R_PW1 + ch + 1], in1=sg[:, ch % 2, :],
                                           op0=ALU.add, op1=ALU.mult).then_inc(gate_set, 1)
                rest_second(4 * (j + 1) + 6)
                for m in range(2):
                    conv(2 * j + m)
            rest_second(len(SECOND) - 2)
            flat = lambda tile, a: tile[:, 4 * a:4 * a + 4, :]
            eng.wait_ge(ln_sum, 1)
            link(V.tensor_scalar(mB[:], ps[:, BT, 0:SEQ], 1.0 / D, None, ALU.mult))
            V.tensor_tensor(cT[:], cT[:], mB[:].unsqueeze(1).broadcast_to([P, KC, SEQ]), ALU.subtract).then_inc(centred, 1)
            eng.wait_ge(centred, 1)
            eng.wait_ge(ln_sum, 2)
            V.tensor_scalar(mB[:], ps[:, BX, 0:SEQ], 1.0 / D, EPS, ALU.mult, ALU.add).then_inc(centred, 1)
            eng.wait_ge(root, 4)
            link(V.reciprocal(mB[:], rB[:]))
            for q in range(4):
                V.tensor_tensor(cT[:, 2 * q:2 * q + 2, :], cT[:, 2 * q:2 * q + 2, :],
                                mB[:].unsqueeze(1).broadcast_to([P, 2, SEQ]), ALU.mult).then_inc(centred, 1)
            for ch in range(KC):
                eng.wait_ge(s_rounded, ch + 1)
                V.tensor_tensor(sTlo[:, ch, :], sT[:, ch, :], sThi[:, ch, :], ALU.subtract).then_inc(s_rest, 1)
            eng.wait_ge(pw2b_in, 16)
            for n in range(8):
                if n == 2:
                    rest_second(len(SECOND))
                mix(n, PROJ["pw2"], mods[:, 2 * D:3 * D], ytmp2, pbB)
            experts(1)
            mean_eps(12, 2)
            inv_root(6, 2)
            eng.wait_ge(gb_in, 16 * 5)
            for t in range(NT):
                V.scalar_tensor_tensor(out=fh[:, t, :], in0=xres[:, t, :], scalar=stat[:, 0, t:t + 1], in1=gB[:],
                                       op0=ALU.mult, op1=ALU.mult).then_inc(out_set, 1)

        @block.tensor
        def _(eng):
            T = nc.tensor

            def three(dst, lhi, llo, rhi, rlo, first, last):
                T.matmul(dst, lhi, rhi, start=first, stop=False)
                T.matmul(dst, llo, rhi, start=False, stop=False)
                return T.matmul(dst, lhi, rlo, start=False, stop=last)

            def spread_mod(b):
                if b == 0:
                    eng.wait_ge(cols_set, 3)
                else:
                    eng.wait_ge(mod_copied, 2 * b)
                last_u = max(u for u, unit in enumerate(FIRST) if unit[0] == "mod" and unit[1] == b)
                eng.wait_ge(unit_done, last_u + 1)
                for i in range(2):
                    T.matmul(ps[:, 6 + i, :], ones[:], acc[:, b % 2, i * HALF:(i + 1) * HALF], start=True, stop=True).then_inc(mod_spread, 1)

            eng.wait_ge(consts_in, 16)
            eng.wait_ge(rows_in, 16 * 9)
            T.transpose(ps[:, 6, 0:R_N], stage[:], cst[0:R_N, C_ID:C_ID + R_N]).then_inc(rows_T, 1)
            for k in range(KC):
                ins = T.transpose(ps[:, 7, k * TAPS:(k + 1) * TAPS], dwst[:, k * P:(k + 1) * P], cst[0:TAPS, C_ID:C_ID + TAPS])
            ins.then_inc(rows_T, 1)
            eng.wait_ge(cc_set, KC)
            for b in range(2):
                for k in range(KC):
                    u = KC * b + k
                    eng.wait_ge(raw_in[u % RAW], 16 * (u // RAW + 1))
                    for i in range(2):
                        cols_ = slice(b * D + i * HALF, b * D + (i + 1) * HALF)
                        ins = T.matmul(ps[:, 2 * b + i, :], ccB[:, k, :], raw[:, u % RAW, i * HALF:(i + 1) * HALF],
                                       start=(k == 0), stop=False)
                    ins.then_inc(ctx_unit, 1)
                for i in range(2):
                    ins = T.matmul(ps[:, 2 * b + i, :], ones[0:1, :], brow[0:1, b * D + i * HALF:b * D + (i + 1) * HALF],
                                   start=False, stop=True)
                ins.then_inc(ctx_mod, 1)
                spread_mod(b)
            order = [(hx, 0), (hx, 1), (hc, 0), (hc, 1)]
            eng.wait_ge(h_set, 4)
            eng.wait_ge(mod_copied, 4)
            for i, (src, t) in enumerate(order):
                for a in range(2):
                    for k in range(4):
                        ins = T.transpose(ps[:, 2 * i + a, k * P:(k + 1) * P], src[:, t, (4 * a + k) * P:(4 * a + k + 1) * P], ident)
                    ins.then_inc(h_T, 1)
            nw = [0]
            nproj = [0]
            w_unit = [u for u, unit in enumerate(FIRST) if unit[0] == "w"] + [SECOND_U + i for i in range(len(SECOND))]
            base_w = [0]

            def have(n):
                u = w_unit[n]
                eng.wait_ge(unit_done, u + 1)

            def project(kind, n0, u_list, dst, left, right, done_unit):
                for k in range(KC):
                    ins = three(dst, left(k, 0), left(k, 1), right(k, 0), right(k, 1), k == 0, k == KC - 1)
                    if done_unit and k == KC // 2 - 1:
                        ins.then_inc(w_used, 1)
                return ins

            def wpart(n0, k, part, c0, width):
                tile = (whi, wlo)[part]
                return dense(tile, n0 + k // 4)[:, k % 4, c0:c0 + width]

            def release(n_before, kind="act"):
                pass

            def weights_left(n0, width_tok, acts, bank, m, done):
                dst = ps[:, bank, 0:width_tok]
                for k in range(KC):
                    T.matmul(dst, wpart(n0, k, 0, m * P, P), acts(k, 0), start=(k == 0), stop=False)
                    T.matmul(dst, wpart(n0, k, 0, m * P, P), acts(k, 1), start=False, stop=False)
                    ins = T.matmul(dst, wpart(n0, k, 1, m * P, P), acts(k, 0), start=False, stop=(k == KC - 1))
                    if done and k == 3:
                        ins.then_inc(w_used, 1)
                return ins

            def finish(ins, last):
                ins.then_inc(w_used if last else proj, 1)
                nproj[0] += 1

            def xc(k, part):
                return (hThi, hTlo)[part][:, :, k, :]

            def xonly(k, part):
                return (hThi, hTlo)[part][:, 0, k, :]

            def block_left(acts, width_tok, banks, free):
                n0 = nw[0]
                have(n0 + 1)
                for m in range(2):
                    free(nproj[0])
                    dst = ps[:, banks[nproj[0] % len(banks)], 0:width_tok]
                    if width_tok > HALF // 2:
                        dst = dst.rearrange("p (a n) -> p a n", a=2)
                    for k in range(KC):
                        T.matmul(dst, wpart(n0, k, 0, m * P, P), acts(k, 0), start=(k == 0), stop=False)
                        i2 = T.matmul(dst, wpart(n0, k, 1, m * P, P), acts(k, 0), start=False, stop=False)
                        i3 = T.matmul(dst, wpart(n0, k, 0, m * P, P), acts(k, 1), start=False, stop=(k == KC - 1))
                        if m == 1 and k == 3:
                            i3.then_inc(w_used, 1)
                    finish(i3, m == 1)
                nw[0] += DENSE

            def block_right(acts, tiles, banks, free):
                n0 = nw[0]
                have(n0 + 1)
                for i, t in enumerate(tiles):
                    free(nproj[0])
                    dst = ps[:, banks[nproj[0] % len(banks)], 0:BLOCK]
                    for k in range(KC):
                        T.matmul(dst, acts(k, 0, t), wpart(n0, k, 0, 0, BLOCK), start=(k == 0), stop=False)
                        T.matmul(dst, acts(k, 0, t), wpart(n0, k, 1, 0, BLOCK), start=False, stop=False)
                        i3 = T.matmul(dst, acts(k, 1, t), wpart(n0, k, 0, 0, BLOCK), start=False, stop=(k == KC - 1))
                        if i == len(tiles) - 1 and k == 3:
                            i3.then_inc(w_used, 1)
                    finish(i3, i == len(tiles) - 1)
                nw[0] += DENSE

            four = [0, 1, 2, 3]
            eng.wait_ge(hT_rest, 8)

            def after_copy(n):
                if n >= 4:
                    eng.wait_ge(proj_taken, n - 3)

            for _ in range(2):
                block_left(xc, SEQ + CTX, four, after_copy)
            for _ in range(2):
                block_right(lambda k, part, t: (hThi, hTlo)[part][:, t // 2, k, (t % 2) * P:(t % 2 + 1) * P],
                            range(4), four, after_copy)
            spread_mod(2)
            spread_mod(3)
            eng.wait_ge(mod_copied, 8)
            for _ in range(2):
                block_left(xonly, SEQ, four, after_copy)
            for _ in range(2):
                block_left(xonly, SEQ, four, after_copy)
            spread_mod(4)
            eng.wait_ge(mod_copied, 10)
            for _ in range(2):
                block_left(xonly, SEQ, four, after_copy)

            def after_hb(n):
                eng.wait_ge(proj_vec, n - 24 + 1)

            for _ in range(2):
                block_left(xonly, SEQ, four, after_hb)
            assert nproj[0] == PROJ["out"]

            def score(n):
                h, t = n // 2, n % 2
                lo = (h % 2) * DH
                if n >= 2:
                    eng.wait_ge(exped, n - 1)
                T.matmul(ps[:, 4 + n % 2, :], qT[lo:lo + DH, h // 2, t * P:(t + 1) * P], kT[lo:lo + DH, h // 2, :],
                         start=True, stop=False)
                eng.wait_ge(bias_masked, h + 1)
                T.matmul(ps[:, 4 + n % 2, 0:SEQ], cst[:, C_FLIP:C_FLIP + P], bias[:, h % 2, t, :],
                         start=False, stop=True).then_inc(scores, 1)

            eng.wait_ge(proj_vec, 8)
            eng.wait_ge(proj_taken, 16)
            score(0)
            score(1)
            for n in range(16):
                h, t = n // 2, n % 2
                eng.wait_ge(normed, n + 1)
                if n >= 2:
                    eng.wait_ge(probT_set, n - 1)
                for q in range(4):
                    ins = T.transpose(ps[:, n % 2, q * P:(q + 1) * P], prob[:, n % 2, q * P:(q + 1) * P], ident)
                ins.then_inc(prob_T, 1)
                if n + 2 < 16:
                    score(n + 2)
                eng.wait_ge(probT_set, n + 1)
                hp, lo = h // 2, (h % 2) * DH
                if n % 4 == 0 and hp >= 2:
                    eng.wait_ge(a_rest, hp - 1)
                for q in range(4):
                    ins = T.matmul(ps[lo:lo + DH, 2 + hp % 2, t * P:(t + 1) * P], vv[:, q, h * DH:(h + 1) * DH],
                                   probT[:, n % 2, q, :], start=(q == 0), stop=(q == 3))
                ins.then_inc(attended, 1)
            spread_mod(5)
            eng.wait_ge(mod_copied, 12)
            eng.wait_ge(a_rest, 4)

            def after_mix(base, x0):
                def free(n):
                    if n - base >= 4:
                        eng.wait_ge(x_mixed, x0 + n - base - 3)
                return free

            for _ in range(4):
                block_right(lambda k, part, t: (catHi, catLo)[part][:, k, t * P:(t + 1) * P], range(NT), four,
                            after_mix(PROJ["out"], 0))

            def experts(L):
                for t in range(NT):
                    eng.wait_ge(h_set, 4 + 4 * L + t + 1)
                    for a in range(2):
                        for k in range(4):
                            ins = T.transpose(ps[:, 2 * t + a, k * P:(k + 1) * P],
                                              htok[:, t, (4 * a + k) * P:(4 * a + k + 1) * P], ident)
                        ins.then_inc(h_T, 1)
                eng.wait_ge(small_in, 32)
                eng.wait_ge(hT_rounded, 8 + 8 * L + 4)
                for t in range(NT):
                    for k in range(KC):
                        ins = T.matmul(ps[:, BX, t * EXPERTS:(t + 1) * EXPERTS], hTr[:, k, t * P:(t + 1) * P], rw[:, k, :],
                                       start=(k == 0), stop=(k == KC - 1))
                ins.then_inc(route_pe, 1)
                eng.wait_ge(routed, 2 * L + 1)
                one = lambda t: rt[:, 6, t, 0:GROUPS]
                tri = cst[:, C_TRI:C_TRI + P]
                T.matmul(ps[:, BX, 64:68], tri, one(0), start=True, stop=True)
                T.matmul(ps[:, BX, 68:72], tri, one(1), start=True, stop=False)
                T.matmul(ps[:, BX, 68:72], ones[:], one(0), start=False, stop=True)
                T.matmul(ps[:, BX, 72:76], ones[:], one(0), start=True, stop=False)
                T.matmul(ps[:, BX, 72:76], ones[:], one(1), start=False, stop=True).then_inc(route_pe, 1)
                eng.wait_ge(flag_set, L + 1)
                for t in range(NT):
                    ins = T.matmul(ps[:, BT, t * P:(t + 1) * P], ones[:], diag[:, t, :], start=True, stop=True)
                ins.then_inc(route_pe, 1)
                eng.wait_ge(routed, 2 * L + 2)
                for tile in range(TILES):
                    dst = ps[:, BX, tile * EXPERTS:(tile + 1) * EXPERTS]
                    for i in range(2 * NT):
                        t, g_ = i // 2, (gatehi, gatelo)[i % 2]
                        ins = T.matmul(dst, pick[:, t, tile * P:(tile + 1) * P], g_[:, t, :], start=(i == 0), stop=(i == 2 * NT - 1))
                ins.then_inc(route_pe, 1)

                def gather(tile):
                    for k in range(KC):
                        dst = ps[:, k // 4, (k % 4) * P:(k % 4 + 1) * P]
                        for i in range(2 * NT):
                            t, part = i // 2, (hhi, hlo)[i % 2]
                            sel = pick[:, t, bass.ds(tile * P, P)] if not isinstance(tile, int) else pick[:, t, tile * P:(tile + 1) * P]
                            ins = T.matmul(dst, part[:, t, k * P:(k + 1) * P], sel, start=(i == 0), stop=(i == 2 * NT - 1))
                    ins.then_inc(gathered, 1)

                eng.wait_ge(route_act, 6 * L + 6)
                gather(0)

                def scatter(g, i):
                    t, half = i // 2, i % 2
                    if i == 0:
                        eng.wait_ge(y_rest, g + (5 * L + 1))
                        if L == 0:
                            eng.wait_ge(mod_copied, g * 4 + 12)
                    else:
                        eng.wait_ge(x_added, g * 4 + (20 * L + i))
                    T.matmul(ps[:, BX, :], spread[:, t * P:(t + 1) * P], yhi[:, half * HALF:(half + 1) * HALF], start=True, stop=False)
                    T.matmul(ps[:, BX, :], spread[:, t * P:(t + 1) * P], ylo[:, half * HALF:(half + 1) * HALF], start=False, stop=True) \
                     .then_inc(scattered, 1)

                def transpose_hidden(g, e):
                    eng.wait_ge(hid_set, g * PER_GROUP + (16 * L + e + 1))
                    for k in range(FC):
                        ins = T.transpose(ps[:, BT, k * P:(k + 1) * P], hid[:, k * P:(k + 1) * P], ident)
                    ins.then_inc(hid_T, 1)

                def mod_piece(g, s, i):
                    if i == 0:
                        eng.wait_ge(unit_done, g * TURN_UNITS[L] + (MOE_U[L] + MOD_POS[KC * s + KC - 1] + 1))
                        if s == 0:
                            eng.wait_ge(x_added, g * 4 + (20 * L + 4))
                    if not (s == 0 and i == 0):
                        eng.wait_ge(mod_copied, g * 4 + (12 + 2 * s + i))
                    w = MOD_BLOCK // 2
                    T.matmul(ps[:, BX, 0:w], ones[:], acc[:, s, i * w:(i + 1) * w], start=True, stop=True).then_inc(mod_spread, 1)

                order_ = expert_order()
                with eng.Fori(0, GROUPS) as g:
                    for pos, (kind, j) in enumerate(TURN[L]):
                        if kind == "mod":
                            continue
                        e, name = order_[j // 4]
                        q = j % 4
                        n = MOE_W[L] + j
                        if j == 0:
                            eng.wait_ge(xg_rest, g * 2 + (10 * L + 2))
                        for i in range(4):
                            if j == SCATTER[i]:
                                scatter(g, i)
                        for ee in range(PER_GROUP):
                            if j == HID_T[ee]:
                                transpose_hidden(g, ee)
                                if ee == PER_GROUP - 1:
                                    gather(g + 1)
                        if L == 0:
                            for i in range(4):
                                if j == MOD_PE[i]:
                                    mod_piece(g, i // 2, i % 2)
                        eng.wait_ge(unit_done, g * TURN_UNITS[L] + (MOE_U[L] + pos + 1))
                        if name == "w2":
                            if q == 0:
                                eng.wait_ge(hidT_rest, g * PER_GROUP + (16 * L + e + 1))
                            for half in range(2):
                                cut = slice(half * HALF, (half + 1) * HALF)
                                ins = three(ps[:, BY + half, :], hidThi[:, q, :], hidTlo[:, q, :],
                                            moe_slot(whi, n)[:, cut], moe_slot(wlo, n)[:, cut],
                                            e == 0 and q == 0, e == PER_GROUP - 1 and q == 3)
                        else:
                            bank = (BA if name == "w1" else BB)[e % 2]
                            for k in range(2):
                                cut = slice(k * FF, (k + 1) * FF)
                                ins = three(ps[:, bank, :], xghi[:, 2 * q + k, :], xglo[:, 2 * q + k, :],
                                            moe_slot(whi, n)[:, cut], moe_slot(wlo, n)[:, cut],
                                            q == 0 and k == 0, q == 3 and k == 1)
                        ins.then_inc(w_used, 1)
                for i in range(4):
                    scatter(GROUPS, i)
                s = sp[L]
                eng.wait_ge(flag_set, L + 1)
                over = eng.value_load(flag[0:1, 0:1], min_val=0, max_val=1)
                with eng.If(over > 0):
                    eng.wait_ge(s["x"], 2)
                    eng.wait_ge(y_rest, 5 * L + 5)
                    n = 0

                    def take():
                        nonlocal n
                        eng.wait_ge(s[f"in{n % 2}"], 16 * (n // 2 + 1))
                        n += 1
                        return spraw[:, (n - 1) % 2, :]

                    for e in range(PER_GROUP):
                        for bank in (BA[0], BB[0]):
                            for k in range(KC):
                                T.matmul(ps[:, bank, :], xg32[:, k, :], take(), start=(k == 0), stop=(k == KC - 1)).then_inc(s["used"], 1)
                        eng.wait_ge(s["hid"], e + 1)
                        for k in range(FC):
                            ins = T.transpose(ps[:, BT, k * P:(k + 1) * P], hid[:, k * P:(k + 1) * P], ident)
                        ins.then_inc(s["pe"], 1)
                        eng.wait_ge(s["hT"], e + 1)
                        for k in range(FC):
                            for half in range(2):
                                T.matmul(ps[:, BY + half, :], hidT32[:, k, :], take(), start=(e == 0 and k == 0),
                                         stop=(e == PER_GROUP - 1 and k == FC - 1)).then_inc(s["used"], 1)
                    eng.wait_ge(s["ylo"], 1)
                    for i in range(4):
                        t, half = i // 2, i % 2
                        if i:
                            eng.wait_ge(s["add"], i)
                        T.matmul(ps[:, BX, :], spread[:, t * P:(t + 1) * P], yhi[:, half * HALF:(half + 1) * HALF], start=True, stop=False)
                        T.matmul(ps[:, BX, :], spread[:, t * P:(t + 1) * P], ylo[:, half * HALF:(half + 1) * HALF], start=False, stop=True) \
                         .then_inc(s["pe"], 1)
                with eng.Else():
                    eng.nop()
                eng.end_ifs()

            experts(0)

            for t in range(NT):
                eng.wait_ge(h_set, 6 + t + 1)
                for a in range(2):
                    for k in range(4):
                        ins = T.transpose(ps[:, 2 * t + a, k * P:(k + 1) * P], fh[:, t, (4 * a + k) * P:(4 * a + k + 1) * P], ident)
                    ins.then_inc(h_T, 1)
            eng.wait_ge(hT_rest, 12)
            nproj[0] = PROJ["pw1"]
            w_off = SECOND_W - W_FIRST
            nw[0] = W_FIRST
            slot_n = [SECOND_W]

            def wpart2(n0, k, part, c0, width):
                tile = (whi, wlo)[part]
                return dense(tile, n0 + k // 4)[:, k % 4, c0:c0 + width]

            nd = 0

            def conv(ch):
                nonlocal nd
                eng.wait_ge(gate_set, ch + 1)
                if ch >= 2:
                    eng.wait_ge(conv_set, ch - 1)
                for tap in range(PE_TAPS):
                    eng.wait_ge(diag_set, nd + 1)
                    T.matmul(ps[:, 4 + ch % 2, 0:SEQ], dg[:, nd % 4, :], uT[:, ch, tap:tap + SEQ], start=(tap == 0),
                             stop=(tap == PE_TAPS - 1)).then_inc(diag_used, 1)
                    nd += 1

            done_n = SECOND_W
            for j in range(4):
                for part_i in range(2):
                    eng.wait_ge(unit_done, SECOND_U + (done_n - SECOND_W) + 2)
                    for m in range(2):
                        bank = 2 * part_i + m
                        if j:
                            eng.wait_ge(gate_set, 2 * (j - 1) + m + 1)
                        dst = ps[:, bank, 0:SEQ]
                        for k in range(KC):
                            a0, a1 = fThi[:, k, :], fTlo[:, k, :]
                            T.matmul(dst, wpart2(done_n, k, 0, m * P, P), a0, start=(k == 0), stop=False)
                            T.matmul(dst, wpart2(done_n, k, 1, m * P, P), a0, start=False, stop=False)
                            ins = T.matmul(dst, wpart2(done_n, k, 0, m * P, P), a1, start=False, stop=(k == KC - 1))
                            if m == 1 and k == 3:
                                ins.then_inc(w_used, 1)
                        ins.then_inc(w_used if m == 1 else proj, 1)
                    done_n += DENSE
                if j:
                    conv(2 * j - 2)
                    conv(2 * j - 1)
            conv(6)
            conv(7)
            eng.wait_ge(conv_set, KC)
            for k in range(KC):
                ins = T.matmul(ps[:, BT, 0:SEQ], ones[:], cT[:, k, :], start=(k == 0), stop=(k == KC - 1))
            ins.then_inc(ln_sum, 1)
            for k in range(KC):
                if k % 4 == 0:
                    eng.wait_ge(sq_set, k // 4 + 1)
                ins = T.matmul(ps[:, BX, 0:SEQ], ones[:], sq[:, k, :], start=(k == 0), stop=(k == KC - 1))
            ins.then_inc(ln_sum, 1)
            eng.wait_ge(s_rest, KC)
            npj = 0
            for b in range(4):
                eng.wait_ge(unit_done, SECOND_U + (done_n - SECOND_W) + 2)
                for t in range(NT):
                    if npj >= 4:
                        eng.wait_ge(x_mixed, 8 + npj - 3)
                    dst = ps[:, npj % 4, 0:BLOCK]
                    for k in range(KC):
                        a0, a1 = sThi[:, k, t * P:(t + 1) * P], sTlo[:, k, t * P:(t + 1) * P]
                        T.matmul(dst, a0, wpart2(done_n, k, 0, 0, BLOCK), start=(k == 0), stop=False)
                        T.matmul(dst, a0, wpart2(done_n, k, 1, 0, BLOCK), start=False, stop=False)
                        ins = T.matmul(dst, a1, wpart2(done_n, k, 0, 0, BLOCK), start=False, stop=(k == KC - 1))
                        if t == NT - 1 and k == 3:
                            ins.then_inc(w_used, 1)
                    ins.then_inc(w_used if t == NT - 1 else proj, 1)
                    npj += 1
                done_n += DENSE
            experts(1)


W13 = [expert_order().index((e, "w1")) * 4 for e in range(PER_GROUP)]
HID_T = [12, 20, 32, 44]
SCATTER = [4, 8, 12, 16]
MOD_PE = [24, 28, 40, 44]
MOD_POS = [TURN[0].index(("mod", i)) for i in range(MOD_TURN)]
PROJ = {"out": 28, "pw1": 36, "pw2": 36 + 16}


def tile_ends():
    out, tiles, units = [], 0, 0
    for per, blocks in ((2, 2), (4, 2), (2, 2), (2, 2), (2, 2), (2, 2), (2, 4), (2, 8), (2, 4)):
        for _ in range(blocks):
            if units == W_FIRST:
                units = SECOND_W
            units += DENSE
            for i in range(per - 1):
                tiles += 1
                out.append(("proj", tiles))
            out.append(("w_used", units))
    return out


TILE_END = tile_ends()

_INS = ["x", "c", "ctx", "c_ctx", "norm1_g", "norm2_g", "w_mod", "b_mod", "na_w_in", "na_rpb", "sc_conv_w", "ab_w_out",
        "cf_pw1_w", "cf_pw1_b", "cf_dw_w", "cf_dw_b", "cf_ln_g", "cf_ln_b", "cf_pw2_w", "cf_pw2_b", "router_w",
        "router_b", "moe_w1", "moe_w3", "moe_w2", "final_g"]


def shape_constants():
    import numpy as np

    k = np.zeros((P, C_N), np.float32)
    k[:, C_ID:C_ID + P] = np.eye(P)
    k[:, C_TRI:C_TRI + P] = np.triu(np.ones((P, P)), 1)
    k[:, C_ROW:C_ROW + TILES * P] = np.arange(TILES * P)
    k[:, C_SLOT:C_SLOT + TILES] = np.arange(P)[:, None] + P * np.arange(TILES)
    q = np.arange(GRID_W)
    start = np.clip(q - KCOL // 2, 0, GRID_W - KCOL)
    inside = (q[None, :] >= start[:, None]) & (q[None, :] < start[:, None] + KCOL)
    k[:, C_MASK:C_MASK + GRID_W] = np.tile(np.where(inside, 0.0, -1e30)[::-1], (2, 1))
    k[:, C_FLIP:C_FLIP + P] = np.kron(np.eye(2), np.eye(GRID_W)[::-1])
    k[:, C_PRIO:C_PRIO + GROUPS] = GROUPS - np.arange(GROUPS)
    return k


def kernel(**inputs):
    import numpy as np
    import concourse.bacc as bacc
    from concourse.bass_utils import run_bass_kernel_spmd

    nc = bacc.Bacc("TRN2", target_bir_lowering=False, num_devices=1)
    arrays, args = {}, []
    for name in _INS:
        a = np.ascontiguousarray(inputs[name])
        arrays[f"in_{name}"] = a
        args.append(nc.dram_tensor(f"in_{name}", a.shape, mybir.dt.from_np(a.dtype), kind="ExternalInput").ap())
    arrays["in_consts"] = shape_constants()
    args.append(nc.dram_tensor("in_consts", [P, C_N], F32, kind="ExternalInput").ap())
    args.append(nc.dram_tensor("bias_scratch", [HEADS * 7, P], F32, kind="Internal").ap())
    args.append(nc.dram_tensor("out_0", [1, SEQ, D], F32, kind="ExternalOutput").ap())
    program(nc, *args)
    r = run_bass_kernel_spmd(nc, [arrays], core_ids=[0])
    return r.results[0]["out_0"]
```

```python
from contextlib import ExitStack

import concourse.bass as bass
from concourse import mybir

F32 = mybir.dt.float32
F32R = mybir.dt.float32r
I32 = mybir.dt.int32
ALU = mybir.AluOpType
ACT = mybir.ActivationFunctionType
AX = mybir.AxisListType

P = 128
D = 1024
KC = D // P
SEQ = 256
CTX = 256
NT = SEQ // P
HALF = 512
GRID_W = 64
ROWS = SEQ // GRID_W
HEADS = 8
DH = 64
NA = HEADS * DH
KR_MAX = 8
KCOL = 16
SC = D - NA
TAPS = 31
PAD = (TAPS - 1) // 2
EXPERTS = 16
GROUPS = 4
PER_GROUP = EXPERTS // GROUPS
FF = 512
FC = FF // P
TILES = GROUPS + 1
EPS = 1e-6

UNIT = 1024
RAW = 8
SPL = 6
BLOCK = 256
DENSE = 2
W_EXPERT = 12
W_GROUP = PER_GROUP * W_EXPERT
MOD_BLOCK = 768
MOD_TURN = 2 * KC
MOD_AFTER = [2 + (12 * i) // 5 for i in range(MOD_TURN)]

C_ID, C_TRI, C_ROW, C_SLOT, C_MASK, C_PRIO = 0, P, 2 * P, 2 * P + TILES * P, 2 * P + TILES * P + TILES, 0
C_PRIO = C_MASK + GRID_W
C_FLIP = C_PRIO + GROUPS
C_LOW = C_FLIP + P
C_OFF = C_LOW + PER_GROUP ** 2
C_N = C_OFF + PER_GROUP ** 2
R_C, R_CC, R_CONV, R_PW1, R_DWB, R_LNG, R_LNB = 0, 8, 16, 28, 44, 52, 60
R_N = 68
PE_TAPS = 13

BA, BB, BY, BT, BX = (0, 2), (1, 3), 4, 6, 7


def expert_order():
    out = []
    for e in range(PER_GROUP):
        out += [(e, "w1"), (e, "w3")]
        if e:
            out.append((e - 1, "w2"))
    return out + [(PER_GROUP - 1, "w2")]


def first_stream():
    out = []

    def mod(v):
        out.extend(("mod", v, k) for k in range(KC))

    def w(name, c0, width):
        for c in range(c0, c0 + width, BLOCK):
            out.extend(("w", name, c, h) for h in range(DENSE))

    def between(name_cols, mods_, per):
        m = [("mod", v, k) for v in mods_ for k in range(KC)]
        first = len(out)
        for name, c0, width in name_cols:
            w(name, c0, width)
        units = out[first:]
        del out[first:]
        for u in units:
            out.extend(m[:per])
            del m[:per]
            out.append(u)
        assert not m

    mod(0)
    mod(1)
    between([("in", NA, NA), ("in", 2 * NA, NA)], (2, 3), 2)
    between([("in", 0, NA), ("in", 3 * NA + SC, SC), ("in", 3 * NA + 2 * SC, SC), ("in", 3 * NA, SC)], (4, 5), 1)
    w("out", 0, D)
    return out


def second_stream():
    out = []
    for c in range(0, D, BLOCK):
        out.extend(("w", "pw1", c, h) for h in range(DENSE))
        out.extend(("w", "pw1", D + c, h) for h in range(DENSE))
    for c in range(0, D, BLOCK):
        out.extend(("w", "pw2", c, h) for h in range(DENSE))
    return out


FIRST = first_stream()
SECOND = second_stream()
W_FIRST = sum(u[0] == "w" for u in FIRST)
TURN_UNITS = (W_GROUP + MOD_TURN, W_GROUP)
MOE_U = (len(FIRST), len(FIRST) + GROUPS * TURN_UNITS[0] + len(SECOND))
MOE_W = (W_FIRST, W_FIRST + GROUPS * W_GROUP + len(SECOND))
SECOND_U = len(FIRST) + GROUPS * TURN_UNITS[0]
SECOND_W = W_FIRST + GROUPS * W_GROUP
assert TURN_UNITS[0] % RAW == 0 and TURN_UNITS[1] % RAW == 0 and W_GROUP % SPL == 0


def turn_stream(layer):
    out = []
    for j in range(W_GROUP):
        out.append(("w", j))
        if layer == 0:
            out.extend(("mod", i) for i in range(MOD_TURN) if MOD_AFTER[i] == j)
    assert len(out) == TURN_UNITS[layer]
    return out


TURN = (turn_stream(0), turn_stream(1))

PER = {
    "w_rounded": (lambda L: W_GROUP, lambda L: MOE_W[L]),
    "w_used": (lambda L: W_GROUP, lambda L: MOE_W[L]),
    "unit_done": (lambda L: TURN_UNITS[L], lambda L: MOE_U[L]),
    "xg_rounded": (lambda L: 2, lambda L: 10 * L),
    "xg_rest": (lambda L: 2, lambda L: 10 * L),
    "silu_set": (lambda L: PER_GROUP, lambda L: 4 * PER_GROUP * L),
    "hid_set": (lambda L: PER_GROUP, lambda L: 4 * PER_GROUP * L),
    "hid_T": (lambda L: PER_GROUP, lambda L: 4 * PER_GROUP * L),
    "hidT_rounded": (lambda L: PER_GROUP, lambda L: 4 * PER_GROUP * L),
    "hidT_rest": (lambda L: PER_GROUP, lambda L: 4 * PER_GROUP * L),
    "y_scaled": (lambda L: 1, lambda L: 5 * L),
    "y_rounded": (lambda L: 1, lambda L: 5 * L),
    "y_rest": (lambda L: 1, lambda L: 5 * L),
    "scattered": (lambda L: 4, lambda L: 20 * L),
    "x_added": (lambda L: 4, lambda L: 20 * L),
}
SPILL_SEMS = ("w_rounded", "w_used", "unit_done", "silu_set", "hid_set", "hid_T", "hidT_rounded", "hidT_rest",
              "y_scaled", "y_rounded", "y_rest", "scattered", "x_added")


class Turn:

    def __init__(self, L, g, sems, spill=None, spill_raw=None):
        self.L, self.g, self.sems, self.spill, self.spill_raw = L, g, sems, spill, spill_raw

    def wait(self, eng, name, k):
        per, base = (f(self.L) for f in PER[name])
        if self.spill is None:
            eng.wait_ge(self.sems[name], self.g * per + (base + k))
        elif k <= 0:
            eng.wait_ge(self.sems[name], GROUPS * per + base + k)
        else:
            eng.wait_ge(self.spill[name], k)

    def sem(self, name):
        return (self.sems if self.spill is None else self.spill)[name]

    def loaded(self, eng, pos):
        u = MOE_U[self.L] + pos
        if self.spill is None:
            eng.wait_ge(self.sems["raw_in"][u % RAW], self.g * (16 * TURN_UNITS[self.L] // RAW) + 16 * (u // RAW + 1))
        else:
            eng.wait_ge(self.spill_raw[u % RAW], 16 * (pos // RAW + 1))

    def loaded_sem(self, pos):
        u = MOE_U[self.L] + pos
        return (self.sems["raw_in"] if self.spill is None else self.spill_raw)[u % RAW]

    def stream(self):
        return TURN[self.L] if self.spill is None else TURN[1]


def program(nc, x, c, ctx, c_ctx, norm1_g, norm2_g, w_mod, b_mod, na_w_in, na_rpb, sc_conv_w, ab_w_out,
            cf_pw1_w, cf_pw1_b, cf_dw_w, cf_dw_b, cf_ln_g, cf_ln_b, cf_pw2_w, cf_pw2_b, router_w, router_b,
            moe_w1, moe_w3, moe_w2, final_g, consts, bias_scratch, out):
    with ExitStack() as stack:
        def sb(name, shape, dt=F32):
            return stack.enter_context(nc.sbuf_tensor(name, shape, dt))

        def sem(name):
            return stack.enter_context(nc.semaphore(name))

        raw = sb("raw", [P, RAW, UNIT])
        whi = sb("whi", [P, SPL, UNIT], F32R)
        wlo = sb("wlo", [P, SPL, UNIT], F32R)
        xres = sb("xres", [P, NT, D])
        mods_at = nc.sbuf_base
        mods = sb("mods", [P, 6 * D])
        g2keep = sb("g2keep", [P, D])
        acc = sb("acc", [P, 2, UNIT])
        gB = sb("gB", [P, D])
        cst = sb("cst", [P, C_N])
        ones = sb("ones", [P, P])
        zero = sb("zero", [P, 1])
        cols = sb("cols", [P, R_N])
        dwT = sb("dwT", [P, KC, TAPS])
        rw = sb("rw", [P, KC, EXPERTS])
        rb = sb("rb", [P, EXPERTS])
        stat = sb("stat", [P, 3, 4])
        flag = sb("flag", [P, 2], I32)
        room = nc.sbuf_usable_end - nc.sbuf_base - 64
        arena = nc.sbuf_base + 31 & ~31
        sb("arena", [P, room // 4])

        def at(name, shape, kb, dt=F32, base=None):
            n = 4
            for s in shape[1:]:
                n *= s
            where = (arena if base is None else base) + int(kb * 1024)
            assert base is not None or int(kb * 1024) + n <= room, (name, kb, room)
            return nc.alloc_sbuf_tensor_at(name, shape, dt, offset=where)

        hThi = at("hThi", [P, 2, KC, SEQ], 0, F32R)
        hTlo = at("hTlo", [P, 2, KC, SEQ], 16, F32R)
        hx = at("hx", [P, NT, D], 32)
        hc = at("hc", [P, NT, D], 40)
        ctxt = at("ctxt", [P, NT, D], 52)
        cG = at("cG", [P, D], 60)
        ccB = at("ccB", [P, KC, P], 64)
        stage = at("stage", [R_N, P], 0)
        dwst = at("dwst", [TAPS, D], 1)
        brow = at("brow", [1, 2 * D], 5)
        rpbt = at("rpbt", [HEADS * 7, P], 13)
        kT = at("kT", [P, 4, SEQ + CTX], 32)
        vv = at("vv", [P, 4, NA], 40)
        qT = at("qT", [P, 4, SEQ], 48)
        gcT = at("gcT", [P, 4, SEQ], 52)
        ghp = at("ghp", [P, 4, SEQ + 2], 56)
        cvT = at("cvT", [P, 4, SEQ], 60.25)
        catHi = at("catHi", [P, KC, SEQ], 64.5, F32R)
        catLo = at("catLo", [P, KC, SEQ], 0, F32R, base=mods_at)
        prob = at("prob", [P, 2, 512], 8)
        bias = at("bias", [P, 2, NT, SEQ], 12)
        probT = at("probT", [P, 2, 4, P], 24)
        gated = at("gated", [P, 2, SEQ], 28)
        smx = at("smx", [P, 3, 2], 30)
        ytmp = at("ytmp", [P, 2, BLOCK], 30.5)
        hhi = at("hhi", [P, NT, D], 0, F32R)
        hlo = at("hlo", [P, NT, D], 8, F32R)
        htok = at("htok", [P, NT, D], 16)
        xghi = at("xghi", [P, KC, P], 16, F32R)
        xglo = at("xglo", [P, KC, P], 20, F32R)
        silu = at("silu", [P, 2, FF], 24)
        hid = at("hid", [P, FF], 28)
        hidThi = at("hidThi", [P, FC, P], 30, F32R)
        hidTlo = at("hidTlo", [P, FC, P], 32, F32R)
        yg = at("yg", [P, D], 34)
        yhi = at("yhi", [P, D], 38, F32R)
        ylo = at("ylo", [P, D], 42, F32R)
        pick = at("pick", [P, NT, TILES * P], 46, F32R)
        spread = at("spread", [P, SEQ], 51, F32R)
        posB = at("posB", [P, SEQ], 52)
        gslot = at("gslot", [P, TILES, EXPERTS], 53)
        gspill = at("gspill", [P, PER_GROUP], 53.5)
        diag = at("diag", [P, NT, P], 54)
        rt = at("rt", [P, 14, NT, EXPERTS], 55)
        gatehi = at("gatehi", [P, NT, EXPERTS], 57, F32R)
        gatelo = at("gatelo", [P, NT, EXPERTS], 57.25, F32R)
        pairs = at("pairs", [P, 2, NT * GROUPS, PER_GROUP ** 2], 57.5)
        hTr = at("hTr", [P, KC, SEQ], 60)
        fThi = at("fThi", [P, KC, SEQ], 0, F32R)
        fTlo = at("fTlo", [P, KC, SEQ], 8, F32R)
        uT = at("uT", [P, KC, SEQ + 2 * PAD], 16)
        sq = at("sq", [P, KC, SEQ], 16)
        cT = at("cT", [P, KC, SEQ], 25)
        sg = at("sg", [P, 2, SEQ], 33)
        mB = at("mB", [P, SEQ], 35)
        rB = at("rB", [P, SEQ], 36)
        sThi = at("sThi", [P, KC, SEQ], 37, F32R)
        sTlo = at("sTlo", [P, KC, SEQ], 45, F32R)
        fh = at("fh", [P, NT, D], 53)
        sT = at("sT", [P, KC, SEQ], 53)
        pbB = at("pbB", [P, D], 61)
        dg = at("dg", [P, 2 * PE_TAPS, P], 37)
        ytmp2 = at("ytmp2", [P, 2, BLOCK], 8)

        ps = stack.enter_context(nc.psum_tensor("ps", [P, 8, HALF], F32))

        ident = cst[:, C_ID:C_ID + P]

        consts_in = sem("consts_in")
        rows_in = sem("rows_in")
        x_in = sem("x_in")
        small_in = sem("small_in")
        pw2b_in = sem("pw2b_in")
        raw_in = [sem(f"raw_in{i}") for i in range(RAW)]
        w_rounded = sem("w_rounded")
        unit_done = sem("unit_done")
        w_used = sem("w_used")
        gb_in = sem("gb_in")
        g_folded = sem("g_folded")
        acc_clear = sem("acc_clear")
        acc_in = [sem("acc_in0"), sem("acc_in1")]
        mod_spread = sem("mod_spread")
        mod_copied = sem("mod_copied")
        ones_set = sem("ones_set")
        rows_T = sem("rows_T")
        cols_set = sem("cols_set")
        cc_set = sem("cc_set")
        ctx_unit = sem("ctx_unit")
        ctx_mod = sem("ctx_mod")
        squares = sem("squares")
        meansq = sem("meansq")
        root = sem("root")
        h_set = sem("h_set")
        h_T = sem("h_T")
        hT_rounded = sem("hT_rounded")
        hT_rest = sem("hT_rest")
        proj = sem("proj")
        proj_taken = sem("proj_taken")
        proj_vec = sem("proj_vec")
        b_set = sem("b_set")
        b_rounded = sem("b_rounded")
        rpb_set = sem("rpb_set")
        spread_set = sem("spread_set")
        zero_set = sem("zero_set")
        rpb_in = sem("rpb_in")
        rpb_out = sem("rpb_out")
        bias_in = [sem("bias_in0"), sem("bias_in1")]
        bias_masked = sem("bias_masked")
        scores = sem("scores")
        biased = sem("biased")
        exped = sem("exped")
        normed = sem("normed")
        prob_T = sem("prob_T")
        probT_set = sem("probT_set")
        attended = sem("attended")
        a_rounded = sem("a_rounded")
        a_rest = sem("a_rest")
        x_mixed = sem("x_mixed")
        g2_kept = sem("g2_kept")
        vec = sem("vec")
        routed = sem("routed")
        route_pe = sem("route_pe")
        route_act = sem("route_act")
        flag_set = sem("flag_set")
        y_clear = sem("y_clear")
        gathered = sem("gathered")
        layer_out = sem("layer_out")
        xg_rounded = sem("xg_rounded")
        xg_rest = sem("xg_rest")
        silu_set = sem("silu_set")
        hid_set = sem("hid_set")
        hid_T = sem("hid_T")
        hidT_rounded = sem("hidT_rounded")
        hidT_rest = sem("hidT_rest")
        y_scaled = sem("y_scaled")
        y_rounded = sem("y_rounded")
        y_rest = sem("y_rest")
        scattered = sem("scattered")
        x_added = sem("x_added")
        gate_set = sem("gate_set")
        diag_set = sem("diag_set")
        diag_used = sem("diag_used")
        conv_set = sem("conv_set")
        ln_sum = sem("ln_sum")
        centred = sem("centred")
        sq_set = sem("sq_set")
        s_act = sem("s_act")
        s_rounded = sem("s_rounded")
        s_rest = sem("s_rest")
        out_set = sem("out_set")
        out_done = sem("out_done")
        spill = [{n: sem(f"spill{L}_{n}") for n in SPILL_SEMS} for L in range(2)]
        spill_raw = [[sem(f"spill{L}_raw_in{i}") for i in range(RAW)] for L in range(2)]
        sems = {"w_rounded": w_rounded, "w_used": w_used, "unit_done": unit_done, "xg_rounded": xg_rounded,
                "xg_rest": xg_rest, "silu_set": silu_set, "hid_set": hid_set, "hid_T": hid_T,
                "hidT_rounded": hidT_rounded, "hidT_rest": hidT_rest, "y_scaled": y_scaled, "y_rounded": y_rounded,
                "y_rest": y_rest, "scattered": scattered, "x_added": x_added, "raw_in": raw_in}

        def spill_turn(L):
            return Turn(L, GROUPS, sems, spill[L], spill_raw[L])

        w_dram = {
            "in": na_w_in[0].rearrange("(k p) n -> p k n", p=P),
            "out": ab_w_out[0].rearrange("(k p) n -> p k n", p=P),
            "pw1": cf_pw1_w[0].rearrange("(k p) n -> p k n", p=P),
            "pw2": cf_pw2_w[0].rearrange("(k p) n -> p k n", p=P),
        }

        def dense(tile, n, h=None):
            return tile[:, n % (RAW if tile is raw else SPL), :].rearrange("p (k n) -> p k n", k=KC // DENSE)

        def moe_slot(tile, n):
            return tile[:, n % (RAW if tile is raw else SPL), :]

        def tile_done(eng, n):
            which, value = TILE_END[n]
            eng.wait_ge(proj if which == "proj" else w_used, value)

        block = stack.enter_context(nc.Block())

        @block.sync
        def _(eng):
            def free(u):
                if not isinstance(u, int) or u >= RAW:
                    eng.wait_ge(unit_done, u - RAW + 1)

            def load_dense(stream, u0):
                for i, unit in enumerate(stream):
                    u = u0 + i
                    free(u)
                    if unit[0] == "mod":
                        _, v, k = unit
                        eng.dma_start(raw[:, u % RAW, :], w_mod[0, k * P:(k + 1) * P, v * D:(v + 1) * D]) \
                           .then_inc(raw_in[u % RAW], 16)
                    else:
                        _, name, c0, h = unit
                        eng.dma_start(dense(raw, u), w_dram[name][:, 4 * h:4 * h + 4, c0:c0 + BLOCK]) \
                           .then_inc(raw_in[u % RAW], 16)

            order = expert_order()

            def load_turn(tn, group):
                for pos, (kind, j) in enumerate(tn.stream()):
                    slot = (MOE_U[tn.L] + pos) % RAW
                    tn.wait(eng, "unit_done", pos - RAW + 1)
                    if kind == "mod":
                        c0 = 2 * MOD_BLOCK * tn.g + MOD_BLOCK * (j // KC)
                        eng.dma_start(raw[:, slot, 0:MOD_BLOCK],
                                      w_mod[1, (j % KC) * P:(j % KC + 1) * P, bass.ds(c0, MOD_BLOCK)]) \
                           .then_inc(tn.loaded_sem(pos), 16)
                        continue
                    e, name = order[j // 4]
                    q = j % 4
                    table = {"w1": moe_w1, "w3": moe_w3, "w2": moe_w2}[name]
                    src = table[tn.L, bass.ds(group * PER_GROUP + e, 1)]
                    if name == "w2":
                        src = src[0, q * P:(q + 1) * P, :]
                        dst = raw[:, slot, :]
                    else:
                        src = src[0].rearrange("(k p) n -> p k n", p=P)[:, 2 * q:2 * q + 2, :]
                        dst = raw[:, slot, :].rearrange("p (k n) -> p k n", k=2)
                    eng.dma_start(dst, src).then_inc(tn.loaded_sem(pos), 16)

            def load_experts(L):
                with eng.Fori(0, GROUPS) as g:
                    load_turn(Turn(L, g, sems), g)

            def load_spill(L):
                eng.wait_ge(flag_set, L + 1)
                over = eng.value_load(flag[0:1, 0:1], min_val=0, max_val=1)
                group = eng.value_load(flag[0:1, 1:2], min_val=0, max_val=GROUPS - 1)
                with eng.If(over > 0):
                    tn = spill_turn(L)
                    load_turn(tn, group)
                    tn.wait(eng, "unit_done", W_GROUP)
                with eng.Else():
                    eng.nop()
                eng.end_ifs()

            load_dense(FIRST[:RAW], 0)
            eng.dma_start(ctxt[:], ctx[0].rearrange("(t p) d -> p t d", p=P)).then_inc(x_in, 16)
            eng.dma_start(xres[:], x[0].rearrange("(t p) d -> p t d", p=P)).then_inc(x_in, 16)
            load_dense(FIRST[RAW:], RAW)
            load_experts(0)
            load_spill(0)
            load_dense(SECOND, SECOND_U)
            load_experts(1)
            load_spill(1)
            for t in range(NT):
                eng.wait_ge(out_set, t + 1)
                eng.dma_start(out[0, t * P:(t + 1) * P, :], fh[:, t, :]).then_inc(out_done, 16)
            eng.wait_ge(out_done, 16 * NT)

        @block.gpsimd
        def _(eng):
            nc.gpsimd.memset(ones[:], 1.0).then_inc(ones_set, 1)
            nc.gpsimd.memset(zero[:], 0.0).then_inc(zero_set, 1)
            nc.gpsimd.memset(rpbt[:], 0.0).then_inc(rpb_set, 1)

            def clear(b, slot, width, src, spread_before):
                if spread_before is not None:
                    eng.wait_ge(mod_spread, spread_before)
                nc.gpsimd.memset(acc[:, slot, 0:width], 0.0).then_inc(acc_clear, 1)
                eng.wait_ge(acc_clear, b + 1)
                eng.dma_start(acc[0:1, slot, 0:width], src).then_inc(acc_in[slot], 16)

            def load_g(n, src):
                if n:
                    eng.wait_ge(g_folded, n)
                eng.dma_start(gB[:], src.partition_broadcast(P)).then_inc(gb_in, 16)

            for b in range(2):
                clear(b, b, D, b_mod[0:1, b * D:(b + 1) * D], None)
            load_g(0, norm1_g[0])
            eng.wait_ge(rpb_set, 1)
            for h in range(HEADS):
                eng.dma_start(rpbt[h * 7:(h + 1) * 7, 48:48 + 2 * KCOL - 1], na_rpb[0, h, 4:11, :]).then_inc(rpb_in, 16)
            eng.wait_ge(rpb_in, 16 * HEADS)
            eng.dma_start(bias_scratch, rpbt[:]).then_inc(rpb_out, 16)
            for b in range(2, 6):
                clear(b, b % 2, D, b_mod[0:1, b * D:(b + 1) * D], 2 * (b - 1))
                if b == 2:
                    load_g(1, norm2_g[0])
            eng.wait_ge(rpb_out, 16)
            for h in range(HEADS):
                if h == 0:
                    tile_done(eng, 11)
                if h >= 2:
                    eng.wait_ge(scores, 2 * (h - 1))
                for t in range(NT):
                    for half in range(2):
                        r = 2 * t + half
                        src = bass.AP(tensor=bias_scratch.tensor, offset=(h * 7 + 3 - r) * P,
                                      ap=[[1, GRID_W], [P, ROWS], [1, GRID_W]])
                        dst = bias[half * GRID_W:(half + 1) * GRID_W, h % 2, t, :].rearrange("p (r c) -> p r c", r=ROWS)
                        eng.dma_start(dst, src).then_inc(bias_in[h % 2], 16)
                eng.wait_ge(bias_in[h % 2], 64 * (h // 2 + 1))
                full = bias[:, h % 2].rearrange("p t (r c) -> p (t r) c", r=ROWS)
                mask = cst[:, C_MASK:C_MASK + GRID_W].unsqueeze(1).broadcast_to([P, NT * ROWS, GRID_W])
                nc.gpsimd.tensor_tensor(full, full, mask, ALU.add).then_inc(bias_masked, 1)
            load_g(2, norm1_g[1])
            eng.wait_ge(zero_set, 1)
            with eng.Fori(0, GROUPS) as g:
                for s in range(2):
                    b = 6 + s
                    eng.wait_ge(mod_spread, g * 4 + 2 * (b - 1))
                    none = zero[:].broadcast_to([P, MOD_BLOCK])
                    nc.gpsimd.tensor_tensor(acc[:, s, 0:MOD_BLOCK], none, none, ALU.add).then_inc(acc_clear, 1)
                    eng.wait_ge(acc_clear, g * 2 + (b + 1))
                    eng.dma_start(acc[0:1, s, 0:MOD_BLOCK], b_mod[1:2, bass.ds(2 * MOD_BLOCK * g + MOD_BLOCK * s, MOD_BLOCK)]) \
                       .then_inc(acc_in[s], 16)
            eng.wait_ge(h_T, 13)
            eng.dma_start(pbB[:], cf_pw2_b[0].partition_broadcast(P)).then_inc(pw2b_in, 16)
            load_g(3, norm2_g[1])
            load_g(4, final_g)
            for s in acc_in:
                eng.wait_ge(s, 16 * (3 + GROUPS))
            eng.wait_ge(gb_in, 16 * 5)

        @block.scalar
        def _(eng):
            A = nc.scalar

            def round_dense(u, n):
                eng.wait_ge(raw_in[u % RAW], 16 * (u // RAW + 1))
                if n >= SPL:
                    eng.wait_ge(w_used, n - SPL + 1)
                A.copy(whi[:, n % SPL, :], raw[:, u % RAW, :]).then_inc(w_rounded, 1)

            def round_turn(tn, pos, j):
                tn.loaded(eng, pos)
                tn.wait(eng, "w_used", j - SPL + 1)
                A.copy(whi[:, (MOE_W[tn.L] + j) % SPL, :], raw[:, (MOE_U[tn.L] + pos) % RAW, :]).then_inc(tn.sem("w_rounded"), 1)

            def copy_mod(b):
                for i in range(2):
                    eng.wait_ge(mod_spread, 2 * b + i + 1)
                    A.copy(mods[:, b * D + i * HALF:b * D + (i + 1) * HALF], ps[:, 6 + i, :]).then_inc(mod_copied, 1)

            def norm(n, srcs, dsts):
                for i, (s, d) in enumerate(zip(srcs, dsts)):
                    A.activation(d, s, ACT.Square, accum_out=stat[:, 0, i:i + 1]).then_inc(squares, 1)
                eng.wait_ge(meansq, n)
                A.activation(stat[:, 2, 0:len(srcs)], stat[:, 1, 0:len(srcs)], ACT.Sqrt).then_inc(root, 1)

            units = [(u, unit) for u, unit in enumerate(FIRST)]
            dense_units = [u for u, unit in units if unit[0] == "w"]
            pending = iter(list(enumerate(dense_units)))

            def round_upto(k):
                for n, u in pending_list[:]:
                    if n < k:
                        round_dense(u, n)
                        pending_list.remove((n, u))
            pending_list = list(pending)

            eng.dma_start(cst[:], consts).then_inc(consts_in, 16)
            eng.dma_start(stage[R_C:R_C + 8, :], c.rearrange("a (k p) -> (a k) p", p=P)).then_inc(rows_in, 16)
            eng.dma_start(stage[R_CC:R_CC + 8, :], c_ctx.rearrange("(k p) -> k p", p=P)).then_inc(rows_in, 16)
            eng.dma_start(brow[0:1, :], b_mod[0:1, 0:2 * D]).then_inc(rows_in, 16)
            eng.dma_start(stage[R_CONV:R_CONV + 12, :], sc_conv_w[0].rearrange("t (k p) -> (t k) p", p=P)).then_inc(rows_in, 16)
            eng.dma_start(stage[R_PW1:R_PW1 + 16, :], cf_pw1_b[0].rearrange("(k p) -> k p", p=P)).then_inc(rows_in, 16)
            eng.dma_start(stage[R_DWB:R_DWB + 8, :], cf_dw_b[0].rearrange("(k p) -> k p", p=P)).then_inc(rows_in, 16)
            eng.dma_start(stage[R_LNG:R_LNG + 8, :], cf_ln_g[0].rearrange("(k p) -> k p", p=P)).then_inc(rows_in, 16)
            eng.dma_start(stage[R_LNB:R_LNB + 8, :], cf_ln_b[0].rearrange("(k p) -> k p", p=P)).then_inc(rows_in, 16)
            eng.dma_start(dwst[:], cf_dw_w[0]).then_inc(rows_in, 16)
            eng.dma_start(rw[:], router_w.rearrange("(k p) n -> p k n", p=P)).then_inc(small_in, 16)
            eng.dma_start(rb[:], router_b.partition_broadcast(P)).then_inc(small_in, 16)
            eng.wait_ge(rows_T, 1)
            A.activation(cols[:, 0:16], ps[:, 6, 0:16], ACT.Silu).then_inc(cols_set, 1)
            A.copy(cols[:, 16:R_N], ps[:, 6, 16:R_N]).then_inc(cols_set, 1)
            eng.wait_ge(rows_T, 2)
            A.copy(dwT[:].rearrange("p k t -> p (k t)"), ps[:, 7, 0:KC * TAPS]).then_inc(cols_set, 1)
            eng.wait_ge(cols_set, 3)
            eng.wait_ge(ones_set, 1)
            for k in range(KC):
                A.activation(ccB[:, k, :], ones[:], ACT.Copy, scale=cols[:, R_CC + k:R_CC + k + 1]).then_inc(cc_set, 1)
            eng.wait_ge(x_in, 32)
            norm(1, [xres[:, 0], xres[:, 1], ctxt[:, 0], ctxt[:, 1]], [hx[:, 0], hx[:, 1], hc[:, 0], hc[:, 1]])
            copy_mod(0)
            copy_mod(1)
            round_upto(4)
            eng.wait_ge(rpb_out, 16)
            for i in range(4):
                for a in range(2):
                    n = 2 * i + a
                    eng.wait_ge(h_T, n + 1)
                    A.copy(hThi[:, i // 2, 4 * a:4 * a + 4, (i % 2) * P:(i % 2 + 1) * P],
                           ps[:, n, :].rearrange("p (k n) -> p k n", k=4)).then_inc(hT_rounded, 1)
            round_upto(6)
            for n in range(4):
                tile_done(eng, n)
                A.copy(kT[:, n, :], ps[:, n % 4, :]).then_inc(proj_taken, 1)
                if n % 2 == 1:
                    round_upto(6 + n + 1)
            for n in range(8):
                blk, tile = n // 4, n % 4
                tile_done(eng, 4 + n)
                A.copy(vv[:, tile, blk * BLOCK:(blk + 1) * BLOCK], ps[:, n % 4, 0:BLOCK]).then_inc(proj_taken, 1)
                if n == 1:
                    copy_mod(2)
                if n % 4 == 3:
                    round_upto(10 + 2 * (blk + 1))
            for n in range(4):
                tile_done(eng, 12 + n)
                A.mul(qT[:, n, :], ps[:, n % 4, 0:SEQ], float(DH) ** -0.5).then_inc(proj_taken, 1)
                if n == 1:
                    copy_mod(3)
                if n % 2 == 1:
                    round_upto(14 + n + 1)
            for n in range(4):
                tile_done(eng, 16 + n)
                A.copy(gcT[:, n, :], ps[:, n % 4, 0:SEQ]).then_inc(proj_taken, 1)
                if n % 2 == 1:
                    round_upto(18 + n + 1)
            copy_mod(4)
            round_upto(24)
            for n in range(4):
                eng.wait_ge(b_set, n + 1)
                A.copy(catHi[:, 4 + n, :], gated[:, n % 2, :]).then_inc(b_rounded, 1)
            for n in range(16 + 1):
                if n < 16:
                    eng.wait_ge(biased, n + 1)
                    if n >= 2:
                        eng.wait_ge(prob_T, n - 1)
                    A.activation(prob[:, n % 2, :], ps[:, 4 + n % 2, :], ACT.Exp, bias=smx[:, 0, n % 2:n % 2 + 1],
                                 accum_out=smx[:, 1, n % 2:n % 2 + 1]).then_inc(exped, 1)
                if n == 0:
                    copy_mod(5)
                if n < 6:
                    round_upto(24 + n + 1)
                if n >= 1:
                    m = n - 1
                    eng.wait_ge(prob_T, m + 1)
                    if m >= 2:
                        eng.wait_ge(attended, m - 1)
                    A.copy(probT[:, m % 2], ps[:, m % 2, :].rearrange("p (k n) -> p k n", k=4)).then_inc(probT_set, 1)
                    if m % 4 == 3:
                        hp = m // 4
                        eng.wait_ge(attended, m + 1)
                        A.copy(catHi[:, hp, :], ps[:, 2 + hp % 2, 0:SEQ]).then_inc(a_rounded, 1)
            round_upto(len(dense_units))

            def experts(L):
                eng.wait_ge(x_mixed, (L + 1) * 8)
                if L == 0:
                    eng.wait_ge(mod_copied, 12)
                    A.copy(g2keep[:], mods[:, 5 * D:6 * D]).then_inc(g2_kept, 1)
                else:
                    A.copy(g2keep[:], mods[:, 5 * D:6 * D]).then_inc(g2_kept, 1)
                norm(2 + 2 * L, [xres[:, 0], xres[:, 1]], [htok[:, 0], htok[:, 1]])
                for t in range(NT):
                    for a in range(2):
                        n = 8 + 8 * L + 2 * t + a
                        eng.wait_ge(h_T, n + 1)
                        A.copy(hTr[:, 4 * a:4 * a + 4, t * P:(t + 1) * P],
                               ps[:, 2 * t + a, :].rearrange("p (k n) -> p k n", k=4)).then_inc(hT_rounded, 1)
                eng.wait_ge(route_pe, 4 * L + 1)
                A.activation(rt[:, 0].rearrange("p t n -> p (t n)"), ps[:, BX, 0:NT * EXPERTS], ACT.Sigmoid) \
                 .then_inc(route_act, 1)
                for t in range(NT):
                    A.copy(hhi[:, t, :], htok[:, t, :]).then_inc(route_act, 1)
                eng.wait_ge(routed, 3 * L + 2)
                A.copy(gatehi[:], rt[:, 10]).then_inc(route_act, 1)
                eng.wait_ge(route_pe, 4 * L + 3)
                A.copy(posB[:], ps[:, BT, 0:SEQ]).then_inc(route_act, 1)
                eng.wait_ge(route_pe, 4 * L + 4)
                A.copy(gslot[:].rearrange("p t n -> p (t n)"), ps[:, BX, 0:TILES * EXPERTS]).then_inc(route_act, 1)
                eng.wait_ge(gathered, 5 * L + 1)
                for a in range(2):
                    A.copy(xghi[:, 4 * a:4 * a + 4, :], ps[:, a, :].rearrange("p (k n) -> p k n", k=4)).then_inc(xg_rounded, 1)

                def silu_of(tn, e):
                    tn.wait(eng, "w_used", W13[e] + 4)
                    A.activation(silu[:, e % 2, :], ps[:, BA[e % 2], :], ACT.Silu).then_inc(tn.sem("silu_set"), 1)

                def hidT_round(tn, e):
                    tn.wait(eng, "hid_T", e + 1)
                    A.copy(hidThi[:], ps[:, BT, :].rearrange("p (k n) -> p k n", k=4)).then_inc(tn.sem("hidT_rounded"), 1)

                def y_round(tn):
                    tn.wait(eng, "y_scaled", 1)
                    A.copy(yhi[:], yg[:]).then_inc(tn.sem("y_rounded"), 1)

                def mod_piece(g, s, i):
                    eng.wait_ge(mod_spread, g * 4 + (12 + 2 * s + i + 1))
                    w = MOD_BLOCK // 2
                    A.copy(mods[:, bass.ds(2 * MOD_BLOCK * g + (MOD_BLOCK * s + i * w), w)], ps[:, BX, 0:w]).then_inc(mod_copied, 1)

                def turn(tn):
                    looped = tn.spill is None
                    for pos, (kind, j) in enumerate(tn.stream()):
                        if kind == "mod":
                            continue
                        if j == 6 and looped:
                            y_round(tn)
                        for e in range(PER_GROUP):
                            if j == W13[e] + 4 + 5:
                                silu_of(tn, e)
                            if j == HID_T[e] + 6:
                                hidT_round(tn, e)
                        if L == 0 and looped:
                            for i in range(3):
                                if j == MOD_PE[i] + 6:
                                    mod_piece(tn.g, i // 2, i % 2)
                        round_turn(tn, pos, j)
                    hidT_round(tn, PER_GROUP - 1)

                with eng.Fori(0, GROUPS) as g:
                    turn(Turn(L, g, sems))
                    eng.wait_ge(gathered, g + (5 * L + 2))
                    for a in range(2):
                        A.copy(xghi[:, 4 * a:4 * a + 4, :], ps[:, a, :].rearrange("p (k n) -> p k n", k=4)).then_inc(xg_rounded, 1)
                    if L == 0:
                        mod_piece(g, 1, 1)
                y_round(Turn(L, GROUPS, sems))
                eng.wait_ge(flag_set, L + 1)
                over = eng.value_load(flag[0:1, 0:1], min_val=0, max_val=1)
                with eng.If(over > 0):
                    tn = spill_turn(L)
                    turn(tn)
                    y_round(tn)
                    tn.wait(eng, "w_used", W_GROUP)
                with eng.Else():
                    eng.nop()
                eng.end_ifs()

            experts(0)

            eng.wait_ge(layer_out, 1)
            norm(3, [xres[:, 0], xres[:, 1]], [fh[:, 0], fh[:, 1]])
            second = [("w", SECOND_U + i, SECOND_W + i) for i in range(len(SECOND))]

            def round_second(k):
                while second and second[0][2] - SECOND_W < k:
                    _, u, n = second.pop(0)
                    round_dense(u, n)
            round_second(6)
            for t in range(NT):
                for a in range(2):
                    n = 12 + 2 * t + a
                    eng.wait_ge(h_T, n + 1)
                    A.copy(fThi[:, 4 * a:4 * a + 4, t * P:(t + 1) * P],
                           ps[:, 2 * t + a, :].rearrange("p (k n) -> p k n", k=4)).then_inc(hT_rounded, 1)
            def diags(ch):
                if ch >= 2:
                    eng.wait_ge(diag_used, PE_TAPS * (ch - 1))
                for tap in range(PE_TAPS):
                    A.activation(dg[:, (ch % 2) * PE_TAPS + tap, :], ident, ACT.Copy, scale=dwT[:, ch, tap:tap + 1]) \
                     .then_inc(diag_set, 1)

            for j in range(4):
                for m in range(2):
                    ch = 2 * j + m
                    tile_done(eng, PROJ["pw1"] + 4 * j + 2 + m)
                    if ch >= 2:
                        eng.wait_ge(gate_set, ch - 1)
                    A.activation(sg[:, ch % 2, :], ps[:, ch, SEQ:2 * SEQ], ACT.Sigmoid,
                                 bias=cols[:, R_PW1 + 8 + ch:R_PW1 + 9 + ch]).then_inc(proj_taken, 1)
                round_second(4 * (j + 1) + 6)
                for m in range(2):
                    diags(2 * j + m)
            round_second(len(SECOND) - 2)
            eng.wait_ge(centred, 1)
            for a in range(2):
                A.activation(sq[:, 4 * a:4 * a + 4, :].rearrange("p k n -> p (k n)"),
                             cT[:, 4 * a:4 * a + 4, :].rearrange("p k n -> p (k n)"), ACT.Square).then_inc(sq_set, 1)
            eng.wait_ge(centred, 2)
            A.activation(rB[:], mB[:], ACT.Sqrt).then_inc(root, 1)
            for ch in range(KC):
                if ch % 2 == 0:
                    eng.wait_ge(centred, 3 + ch // 2)
                A.activation(sT[:, ch, :], cT[:, ch, :], ACT.Silu, bias=cols[:, R_LNB + ch:R_LNB + ch + 1],
                             scale=cols[:, R_LNG + ch:R_LNG + ch + 1]).then_inc(s_act, 1)
                eng.wait_ge(s_act, ch + 1)
                A.copy(sThi[:, ch, :], sT[:, ch, :]).then_inc(s_rounded, 1)
            round_second(len(SECOND))
            experts(1)
            eng.wait_ge(layer_out, 2)
            norm(5, [xres[:, 0], xres[:, 1]], [fh[:, 0], fh[:, 1]])

        @block.vector
        def _(eng):
            V = nc.vector
            own = [0]

            def link(ins):
                own[0] += 1
                ins.then_inc(vec, 1)
                eng.wait_ge(vec, own[0])

            def rest_dense(u, n):
                eng.wait_ge(w_rounded, n + 1)
                V.tensor_tensor(wlo[:, n % SPL, :], raw[:, u % RAW, :], whi[:, n % SPL, :], ALU.subtract).then_inc(unit_done, 1)

            def sum_mod(u, b, k, ctx_too):
                eng.wait_ge(raw_in[u % RAW], 16 * (u // RAW + 1))
                if k == 0:
                    eng.wait_ge(acc_in[b % 2], 16 * (b // 2 + 1))
                else:
                    eng.wait_ge(unit_done, FIRST.index(("mod", b, k - 1)) + 1)
                if ctx_too:
                    eng.wait_ge(ctx_unit, u + 1)
                V.scalar_tensor_tensor(out=acc[:, b % 2, :], in0=raw[:, u % RAW, :], scalar=cols[:, R_C + k:R_C + k + 1],
                                       in1=acc[:, b % 2, :], op0=ALU.mult, op1=ALU.add).then_inc(unit_done, 1)

            todo = [(u, unit) for u, unit in enumerate(FIRST)]
            nw = [0]

            def upto(k):
                while nw[0] < k:
                    u, unit = todo.pop(0)
                    if unit[0] == "w":
                        rest_dense(u, nw[0])
                        nw[0] += 1
                    else:
                        sum_mod(u, unit[1], unit[2], unit[1] < 2)

            def mean_eps(n, count):
                eng.wait_ge(squares, n)
                V.tensor_scalar(stat[:, 1, 0:count], stat[:, 0, 0:count], 1.0 / D, EPS, ALU.mult, ALU.add).then_inc(meansq, 1)

            def inv_root(n, count):
                eng.wait_ge(root, n)
                link(V.reciprocal(stat[:, 0, 0:count], stat[:, 2, 0:count]))

            def fold_gain(scale, n):
                eng.wait_ge(gb_in, 16 * n)
                V.scalar_tensor_tensor(out=scale, in0=scale, scalar=1.0, in1=gB[:], op0=ALU.add, op1=ALU.mult).then_inc(g_folded, 1)
                eng.wait_ge(g_folded, n)

            def modulated(dst, src, i, gain, shift):
                link(V.scalar_tensor_tensor(out=dst, in0=src, scalar=stat[:, 0, i:i + 1], in1=gain, op0=ALU.mult, op1=ALU.mult))
                V.tensor_tensor(dst, dst, shift, ALU.add).then_inc(h_set, 1)

            eng.wait_ge(cols_set, 2)
            mean_eps(4, 4)
            while todo[0][1][1] in (0, 1):
                u, unit = todo.pop(0)
                sum_mod(u, unit[1], unit[2], True)
            inv_root(1, 4)
            eng.wait_ge(ctx_mod, 2)
            eng.wait_ge(gb_in, 16)
            link(V.scalar_tensor_tensor(out=cG[:].rearrange("p (a n) -> p a n", a=2), in0=ps[:, 2:4, :], scalar=1.0,
                                        in1=gB[:].rearrange("p (a n) -> p a n", a=2), op0=ALU.add, op1=ALU.mult))
            for t in range(NT):
                modulated(hc[:, t, :].rearrange("p (a n) -> p a n", a=2), ctxt[:, t, :].rearrange("p (a n) -> p a n", a=2),
                          2 + t, cG[:].rearrange("p (a n) -> p a n", a=2), ps[:, 0:2, :])
            eng.wait_ge(mod_copied, 4)
            fold_gain(mods[:, D:2 * D], 1)
            for t in range(NT):
                modulated(hx[:, t, :], xres[:, t, :], t, mods[:, D:2 * D], mods[:, 0:D])
            upto(2)
            for i in range(4):
                for a in range(2):
                    n = 2 * i + a
                    eng.wait_ge(hT_rounded, n + 1)
                    hi = hThi[:, i // 2, 4 * a:4 * a + 4, (i % 2) * P:(i % 2 + 1) * P]
                    lo = hTlo[:, i // 2, 4 * a:4 * a + 4, (i % 2) * P:(i % 2 + 1) * P]
                    V.tensor_tensor(lo, ps[:, n, :].rearrange("p (k n) -> p k n", k=4), hi, ALU.subtract).then_inc(hT_rest, 1)

            upto(16)
            link(V.memset(ghp[:, :, 0:1], 0.0))
            link(V.memset(ghp[:, :, SEQ + 1:SEQ + 2], 0.0))
            for n in range(4):
                if n % 2 == 0:
                    upto(20 + n)
                tile_done(eng, 20 + n)
                eng.wait_ge(proj_taken, 16 + n + 1)
                V.tensor_tensor(ghp[:, n, 1:SEQ + 1], ps[:, n % 4, 0:SEQ], gcT[:, n, :], ALU.mult).then_inc(proj_vec, 1)
            for n in range(4):
                if n == 0:
                    upto(24)
                eng.wait_ge(proj_vec, n + 1)
                for tap in range(3):
                    w = cols[:, R_CONV + 4 * tap + n:R_CONV + 4 * tap + n + 1]
                    src = ghp[:, n, tap:tap + SEQ]
                    if tap == 0:
                        link(V.tensor_scalar(cvT[:, n, :], src, w, None, ALU.mult))
                    else:
                        link(V.scalar_tensor_tensor(out=cvT[:, n, :], in0=src, scalar=w, in1=cvT[:, n, :], op0=ALU.mult, op1=ALU.add))
            for n in range(4):
                tile_done(eng, 24 + n)
                if n >= 2:
                    eng.wait_ge(b_rounded, n - 1)
                V.tensor_tensor(gated[:, n % 2, :], ps[:, n % 4, 0:SEQ], cvT[:, n, :], ALU.mult).then_inc(b_set, 1)
                eng.wait_ge(b_rounded, n + 1)
                V.tensor_tensor(catLo[:, 4 + n, :], gated[:, n % 2, :], catHi[:, 4 + n, :], ALU.subtract).then_inc(proj_vec, 1)
            for n in range(16 + 1):
                if n < 16:
                    h, t = n // 2, n % 2
                    eng.wait_ge(scores, n + 1)
                    V.tensor_reduce(smx[:, 0, n % 2:n % 2 + 1], ps[:, 4 + n % 2, :], AX.X, ALU.max, negate=True).then_inc(biased, 1)
                if n >= 1:
                    m = n - 1
                    eng.wait_ge(exped, m + 1)
                    link(V.reciprocal(smx[:, 2, m % 2:m % 2 + 1], smx[:, 1, m % 2:m % 2 + 1]))
                    V.tensor_scalar(prob[:, m % 2, :], prob[:, m % 2, :], smx[:, 2, m % 2:m % 2 + 1], None, ALU.mult).then_inc(normed, 1)
                    if m % 4 == 3 and m >= 4:
                        hp = m // 4 - 1
                        eng.wait_ge(a_rounded, hp + 1)
                        V.tensor_tensor(catLo[:, hp, :], ps[:, 2 + hp % 2, 0:SEQ], catHi[:, hp, :], ALU.subtract).then_inc(a_rest, 1)
                if n < 6:
                    upto(24 + n + 1)
            eng.wait_ge(a_rounded, 4)
            V.tensor_tensor(catLo[:, 3, :], ps[:, 3, 0:SEQ], catHi[:, 3, :], ALU.subtract).then_inc(a_rest, 1)

            def mix(n, base, gate, tmp, extra=None):
                blk, t = n // 2, n % 2
                cols_ = slice(blk * BLOCK, (blk + 1) * BLOCK)
                tile_done(eng, base + n)
                src = ps[:, n % 4, 0:BLOCK]
                if extra is not None:
                    link(V.tensor_tensor(tmp[:, n % 2, :], src, extra[:, cols_], ALU.add))
                    src = tmp[:, n % 2, :]
                link(V.tensor_tensor(tmp[:, n % 2, :], src, gate[:, cols_], ALU.mult))
                V.tensor_tensor(xres[:, t, cols_], xres[:, t, cols_], tmp[:, n % 2, :], ALU.add).then_inc(x_mixed, 1)

            g1 = mods[:, 2 * D:3 * D]
            for n in range(8):
                if n == 2:
                    upto(32)
                mix(n, PROJ["out"], g1, ytmp)
            assert not todo, todo

            def experts(L):
                mean_eps([6, 10][L], 2)
                inv_root([2, 5][L], 2)
                eng.wait_ge(x_mixed, 8 * (L + 1))
                fold_gain(mods[:, 4 * D:5 * D], [2, 4][L])
                for t in range(NT):
                    modulated(htok[:, t, :], xres[:, t, :], t, mods[:, 4 * D:5 * D], mods[:, 3 * D:4 * D])
                (SCO, SEL, PAIR, GRP, EQ, W4, ONE, RANK, T1, GSEL, GATE, POS, RR, T2) = range(14)

                def r(i, n=EXPERTS):
                    return rt[:, i, :, 0:n]

                def grp(i):
                    return rt[:, i].rearrange("p t (g e) -> p t g e", e=PER_GROUP)

                def by_pair(tile):
                    return tile.rearrange("p n (i j) -> p n i j", i=PER_GROUP)

                eng.wait_ge(route_act, 6 * L + 1)
                eng.wait_ge(small_in, 32)
                link(V.tensor_tensor(r(SEL), r(SCO), rb[:].unsqueeze(1).broadcast_to([P, NT, EXPERTS]), ALU.add))
                sel = rt[:, SEL].rearrange("p t (g e) -> p (t g) e", e=PER_GROUP)
                full = [P, NT * GROUPS, PER_GROUP, PER_GROUP]
                s_i = sel.unsqueeze(3).broadcast_to(full)
                s_j = sel.unsqueeze(2).broadcast_to(full)
                q0, q1 = pairs[:, 0], pairs[:, 1]
                wide = [P, NT * GROUPS, PER_GROUP ** 2]
                off = cst[:, C_OFF:C_OFF + PER_GROUP ** 2].unsqueeze(1).broadcast_to(wide)
                low = cst[:, C_LOW:C_LOW + PER_GROUP ** 2].unsqueeze(1).broadcast_to(wide)
                groups = rt[:, GRP, :, 0:GROUPS]
                link(V.tensor_tensor(by_pair(q0), s_i, s_j, ALU.add))
                V.tensor_tensor(by_pair(q1), s_j, s_i, ALU.is_ge).then_inc(vec, 1)
                own[0] += 1
                link(V.tensor_tensor(q0, q0, off, ALU.add))
                V.tensor_reduce(rt[:, RANK].rearrange("p t n -> p (t n)")[:, 0:NT * GROUPS], q0, AX.X, ALU.max).then_inc(vec, 1)
                own[0] += 1
                link(V.tensor_tensor(q1, q1, low, ALU.mult))
                link(V.tensor_tensor(by_pair(q0), s_j, s_i, ALU.is_gt))
                gsc = rt[:, RANK].rearrange("p t n -> p (t n)")[:, 0:NT * GROUPS].rearrange("p (t g) -> p t g", t=NT)
                link(V.tensor_reduce(r(EQ, 1), gsc, AX.X, ALU.max))
                link(V.tensor_tensor(r(W4, GROUPS), gsc, r(EQ, 1).broadcast_to([P, NT, GROUPS]), ALU.is_equal))
                prio = cst[:, C_PRIO:C_PRIO + GROUPS].unsqueeze(1).broadcast_to([P, NT, GROUPS])
                V.tensor_tensor(q0, q0, q1, ALU.max).then_inc(vec, 1)
                own[0] += 1
                link(V.tensor_tensor(r(W4, GROUPS), r(W4, GROUPS), prio, ALU.mult))
                link(V.tensor_reduce(r(EQ, 1), r(W4, GROUPS), AX.X, ALU.max))
                link(V.tensor_tensor(r(ONE, GROUPS), r(W4, GROUPS), r(EQ, 1).broadcast_to([P, NT, GROUPS]), ALU.is_equal))
                V.tensor_reduce(rt[:, T1].rearrange("p t (g e) -> p (t g) e", e=PER_GROUP), by_pair(q0), AX.X, ALU.add) \
                 .then_inc(routed, 1)
                eng.wait_ge(routed, 3 * L + 1)
                link(V.tensor_scalar(r(GSEL), r(T1), 1.5, None, ALU.is_lt))
                one_b = rt[:, ONE, :, 0:GROUPS].unsqueeze(3).broadcast_to([P, NT, GROUPS, PER_GROUP])
                link(V.tensor_tensor(grp(GSEL), grp(GSEL), one_b, ALU.mult))
                link(V.tensor_tensor(r(T1), r(GSEL), r(SCO), ALU.mult))
                link(V.tensor_reduce(r(T2, 1), r(T1), AX.X, ALU.add))
                link(V.reciprocal(r(EQ, 1), r(T2, 1)))
                V.tensor_tensor(r(GATE), r(T1), r(EQ, 1).broadcast_to([P, NT, EXPERTS]), ALU.mult).then_inc(routed, 1)
                for t in range(NT):
                    eng.wait_ge(route_act, 6 * L + t + 2)
                    V.tensor_tensor(hlo[:, t, :], htok[:, t, :], hhi[:, t, :], ALU.subtract).then_inc(vec, 1)
                    own[0] += 1
                eng.wait_ge(routed, 3 * L + 2)
                eng.wait_ge(route_pe, 4 * L + 2)
                cnt = ps[:, BX, 64:64 + 3 * GROUPS]
                link(V.tensor_tensor(r(T1, GROUPS), cnt[:, 0:2 * GROUPS].rearrange("p (t g) -> p t g", t=NT), r(ONE, GROUPS), ALU.mult))
                link(V.tensor_reduce(r(POS, 1), r(T1, GROUPS), AX.X, ALU.add))
                link(V.tensor_tensor(r(T1, GROUPS), r(ONE, GROUPS), prio, ALU.mult))
                link(V.tensor_reduce(r(T2, 1), r(T1, GROUPS), AX.X, ALU.add))
                link(V.tensor_scalar(r(T2, 1), r(T2, 1), -float(P), float(P * GROUPS), ALU.mult, ALU.add))
                link(V.tensor_scalar(r(W4, 1), r(POS, 1), P - 0.5, None, ALU.is_gt))
                link(V.tensor_scalar(r(T1, 1), r(T2, 1), -1.0, float(P * GROUPS - P), ALU.mult, ALU.add))
                link(V.tensor_tensor(r(T1, 1), r(T1, 1), r(W4, 1), ALU.mult))
                link(V.tensor_tensor(r(T2, 1), r(T2, 1), r(T1, 1), ALU.add))
                link(V.tensor_tensor(r(POS, 1), r(POS, 1), r(T2, 1), ALU.add))
                for t in range(NT):
                    link(V.tensor_scalar(diag[:, t, :], ident, rt[:, POS, t, 0:1], None, ALU.mult))
                link(V.tensor_scalar(rt[:, RR, 0, 0:GROUPS], cnt[:, 2 * GROUPS:3 * GROUPS], P + 0.5, None, ALU.is_gt))
                link(V.tensor_reduce(rt[:, RR, 1, 0:1], rt[:, RR, 0, 0:GROUPS], AX.X, ALU.add))
                link(V.tensor_tensor(rt[:, RR, 0, 4:8], rt[:, RR, 0, 0:GROUPS], cst[:, C_PRIO:C_PRIO + GROUPS], ALU.mult))
                link(V.tensor_reduce(rt[:, RR, 1, 1:2], rt[:, RR, 0, 4:8], AX.X, ALU.add))
                link(V.tensor_scalar(rt[:, RR, 1, 2:3], rt[:, RR, 1, 0:1], float(GROUPS), None, ALU.mult))
                link(V.tensor_tensor(rt[:, RR, 1, 1:2], rt[:, RR, 1, 2:3], rt[:, RR, 1, 1:2], ALU.subtract))
                V.tensor_copy(flag[:], rt[:, RR, 1, 0:2]).then_inc(flag_set, 1)
                eng.wait_ge(route_act, 6 * L + 4)
                for t in range(NT):
                    link(V.tensor_scalar(pick[:, t, :], cst[:, C_ROW:C_ROW + TILES * P], rt[:, POS, t, 0:1], None, ALU.is_equal))
                V.tensor_tensor(gatelo[:], rt[:, GATE], gatehi[:], ALU.subtract).then_inc(routed, 1)
                V.memset(spread[:].bitcast(F32), 0.0).then_inc(y_clear, 1)
                V.memset(ps[:, BY:BY + 2, :], 0.0).then_inc(y_clear, 1)
                eng.wait_ge(route_act, 6 * L + 6)
                link(V.tensor_reduce(gspill[:], gslot[:, GROUPS, :].rearrange("p (g e) -> p e g", e=PER_GROUP), AX.X, ALU.add))
                eng.wait_ge(y_clear, 2 * L + 2)
                for a in range(2):
                    eng.wait_ge(xg_rounded, 10 * L + a + 1)
                    V.tensor_tensor(xglo[:, 4 * a:4 * a + 4, :], ps[:, a, :].rearrange("p (k n) -> p k n", k=4),
                                    xghi[:, 4 * a:4 * a + 4, :], ALU.subtract).then_inc(xg_rest, 1)

                def rest_turn(tn, pos, j):
                    n = MOE_W[L] + j
                    tn.wait(eng, "w_rounded", j + 1)
                    V.tensor_tensor(wlo[:, n % SPL, :], raw[:, (MOE_U[L] + pos) % RAW, :], whi[:, n % SPL, :],
                                    ALU.subtract).then_inc(tn.sem("unit_done"), 1)

                def mod_turn(tn, pos, i):
                    s, k = i // KC, i % KC
                    tn.loaded(eng, pos)
                    if k == 0:
                        eng.wait_ge(acc_in[s], tn.g * 16 + 16 * 4)
                    else:
                        tn.wait(eng, "unit_done", MOD_POS[i - 1] + 1)
                    V.scalar_tensor_tensor(out=acc[:, s, 0:MOD_BLOCK], in0=raw[:, (MOE_U[L] + pos) % RAW, 0:MOD_BLOCK],
                                           scalar=cols[:, R_C + k:R_C + k + 1], in1=acc[:, s, 0:MOD_BLOCK],
                                           op0=ALU.mult, op1=ALU.add).then_inc(unit_done, 1)

                def y_scale(tn):
                    tn.wait(eng, "w_used", 0 if tn.spill is None else W_GROUP)
                    V.tensor_tensor(yg[:].rearrange("p (a n) -> p a n", a=2), ps[:, BY:BY + 2, :],
                                    g2keep[:].rearrange("p (a n) -> p a n", a=2), ALU.mult).then_inc(tn.sem("y_scaled"), 1)

                def y_remainder(tn):
                    tn.wait(eng, "y_rounded", 1)
                    V.tensor_tensor(ylo[:], yg[:], yhi[:], ALU.subtract).then_inc(tn.sem("y_rest"), 1)

                def x_add(tn, i):
                    t, half = i // 2, i % 2
                    tn.wait(eng, "scattered", i + 1)
                    dst = xres[:, t, half * HALF:(half + 1) * HALF]
                    V.tensor_tensor(dst, dst, ps[:, XBANK[i], :], ALU.add).then_inc(tn.sem("x_added"), 1)

                def set_spread(column):
                    return V.tensor_scalar(spread[:], posB[:], column, None, ALU.is_equal)

                def hid_mul(tn, e):
                    tn.wait(eng, "silu_set", e + 1)
                    tn.wait(eng, "w_used", W13[e] + 8)
                    if tn.spill is None:
                        gate = gslot[:].rearrange("p t n -> p (t n)")[:, bass.ds(tn.g * (EXPERTS + PER_GROUP) + e, 1)]
                    else:
                        gate = gspill[:, e:e + 1]
                    V.scalar_tensor_tensor(out=hid[:], in0=silu[:, e % 2, :], scalar=gate, in1=ps[:, BB[e % 2], :],
                                           op0=ALU.mult, op1=ALU.mult).then_inc(tn.sem("hid_set"), 1)

                def hidT_remainder(tn, e):
                    tn.wait(eng, "hidT_rounded", e + 1)
                    V.tensor_tensor(hidTlo[:], ps[:, BT, :].rearrange("p (k n) -> p k n", k=4), hidThi[:], ALU.subtract) \
                     .then_inc(tn.sem("hidT_rest"), 1)

                def turn(tn):
                    looped = tn.spill is None
                    for pos, (kind, j) in enumerate(tn.stream()):
                        if kind == "mod":
                            mod_turn(tn, pos, j)
                            continue
                        if looped:
                            if j == 5:
                                y_scale(tn)
                            if j == 7:
                                y_remainder(tn)
                        for e in range(PER_GROUP):
                            if j == W13[e] + 8 + 5:
                                hid_mul(tn, e)
                            if j == HID_T[e] + 6:
                                hidT_remainder(tn, e)
                        if looped:
                            for i in range(4):
                                if j == SCATTER[i] + 6:
                                    x_add(tn, i)
                            if j == SCATTER[3] + 6:
                                set_spread(cst[:, bass.ds(tn.g + C_SLOT, 1)]).then_inc(vec, 1)
                        rest_turn(tn, pos, j)
                    hidT_remainder(tn, PER_GROUP - 1)

                eng.wait_ge(g2_kept, L + 1)
                with eng.Fori(0, GROUPS) as g:
                    turn(Turn(L, g, sems))
                    for a in range(2):
                        eng.wait_ge(xg_rounded, g * 2 + (10 * L + 3 + a))
                        V.tensor_tensor(xglo[:, 4 * a:4 * a + 4, :], ps[:, a, :].rearrange("p (k n) -> p k n", k=4),
                                        xghi[:, 4 * a:4 * a + 4, :], ALU.subtract).then_inc(xg_rest, 1)
                own[0] += GROUPS
                last = Turn(L, GROUPS, sems)
                y_scale(last)
                y_remainder(last)
                for i in range(4):
                    x_add(last, i)
                eng.wait_ge(flag_set, L + 1)
                over = eng.value_load(flag[0:1, 0:1], min_val=0, max_val=1)
                with eng.If(over > 0):
                    tn = spill_turn(L)
                    set_spread(cst[:, C_SLOT + GROUPS:C_SLOT + GROUPS + 1]).then_inc(spread_set, 1)
                    turn(tn)
                    y_scale(tn)
                    y_remainder(tn)
                    for i in range(4):
                        x_add(tn, i)
                    tn.wait(eng, "x_added", 4)
                with eng.Else():
                    eng.nop()
                eng.end_ifs()
                eng.wait_ge(x_added, 20 * (L + 1))
                V.memset(stat[:, 1, :], 0.0).then_inc(layer_out, 1)

            experts(0)

            mean_eps(8, 2)
            inv_root(3, 2)
            eng.wait_ge(mod_copied, 12 + 4 * GROUPS)
            fold_gain(mods[:, D:2 * D], 3)
            for t in range(NT):
                modulated(fh[:, t, :], xres[:, t, :], t, mods[:, D:2 * D], mods[:, 0:D])
            second = [(SECOND_U + i, SECOND_W + i) for i in range(len(SECOND))]

            def rest_second(k):
                while second and second[0][1] - SECOND_W < k:
                    u, n = second.pop(0)
                    rest_dense(u, n)
            rest_second(6)
            for t in range(NT):
                for a in range(2):
                    n = 12 + 2 * t + a
                    eng.wait_ge(hT_rounded, n + 1)
                    hi = fThi[:, 4 * a:4 * a + 4, t * P:(t + 1) * P]
                    lo = fTlo[:, 4 * a:4 * a + 4, t * P:(t + 1) * P]
                    V.tensor_tensor(lo, ps[:, 2 * t + a, :].rearrange("p (k n) -> p k n", k=4), hi, ALU.subtract).then_inc(hT_rest, 1)
            link(V.memset(uT[:, :, 0:PAD], 0.0))
            link(V.memset(uT[:, :, PAD + SEQ:], 0.0))

            def conv(c0, until):
                first = own[0]
                for i, tap in enumerate(range(PE_TAPS, TAPS)):
                    for m in range(2):
                        ch = c0 + m
                        src, w = uT[:, ch, tap:tap + SEQ], dwT[:, ch, tap:tap + 1]
                        if i:
                            eng.wait_ge(vec, first + 2 * i + m - 1)
                            ins = V.scalar_tensor_tensor(out=cT[:, ch, :], in0=src, scalar=w, in1=cT[:, ch, :],
                                                         op0=ALU.mult, op1=ALU.add)
                        else:
                            eng.wait_ge(gate_set, ch + 1)
                            ins = V.tensor_scalar(cT[:, ch, :], src, w, cols[:, R_DWB + ch:R_DWB + ch + 1], ALU.mult, ALU.add)
                        ins.then_inc(vec, 1)
                        own[0] += 1
                    if i % 2 == 0 and second and second[0][1] - SECOND_W < until:
                        rest_second(second[0][1] - SECOND_W + 1)
                rest_second(until)
                for m in range(2):
                    ch = c0 + m
                    eng.wait_ge(vec, own[0] - 1 + m)
                    eng.wait_ge(diag_used, PE_TAPS * (ch + 1))
                    V.tensor_tensor(cT[:, ch, :], cT[:, ch, :], ps[:, ch, 0:SEQ], ALU.add).then_inc(conv_set, 1)

            for j in range(4):
                for m in range(2):
                    ch = 2 * j + m
                    eng.wait_ge(proj_taken, 20 + ch + 1)
                    V.scalar_tensor_tensor(out=uT[:, ch, PAD:PAD + SEQ], in0=ps[:, ch, 0:SEQ],
                                           scalar=cols[:, R_PW1 + ch:R_PW1 + ch + 1], in1=sg[:, ch % 2, :],
                                           op0=ALU.add, op1=ALU.mult).then_inc(gate_set, 1)
                conv(2 * j, min(4 * (j + 1) + 6, len(SECOND) - 2))
            rest_second(len(SECOND) - 2)
            flat = lambda tile, a: tile[:, 4 * a:4 * a + 4, :]
            eng.wait_ge(ln_sum, 1)
            link(V.tensor_scalar(mB[:], ps[:, BT, 0:SEQ], 1.0 / D, None, ALU.mult))
            V.tensor_tensor(cT[:], cT[:], mB[:].unsqueeze(1).broadcast_to([P, KC, SEQ]), ALU.subtract).then_inc(centred, 1)
            eng.wait_ge(centred, 1)
            eng.wait_ge(ln_sum, 2)
            V.tensor_scalar(mB[:], ps[:, BX, 0:SEQ], 1.0 / D, EPS, ALU.mult, ALU.add).then_inc(centred, 1)
            eng.wait_ge(root, 4)
            link(V.reciprocal(mB[:], rB[:]))
            for q in range(4):
                V.tensor_tensor(cT[:, 2 * q:2 * q + 2, :], cT[:, 2 * q:2 * q + 2, :],
                                mB[:].unsqueeze(1).broadcast_to([P, 2, SEQ]), ALU.mult).then_inc(centred, 1)
            for ch in range(KC):
                eng.wait_ge(s_rounded, ch + 1)
                V.tensor_tensor(sTlo[:, ch, :], sT[:, ch, :], sThi[:, ch, :], ALU.subtract).then_inc(s_rest, 1)
            eng.wait_ge(pw2b_in, 16)
            for n in range(8):
                if n == 2:
                    rest_second(len(SECOND))
                mix(n, PROJ["pw2"], mods[:, 2 * D:3 * D], ytmp2, pbB)
            experts(1)
            mean_eps(12, 2)
            inv_root(6, 2)
            eng.wait_ge(gb_in, 16 * 5)
            for t in range(NT):
                V.scalar_tensor_tensor(out=fh[:, t, :], in0=xres[:, t, :], scalar=stat[:, 0, t:t + 1], in1=gB[:],
                                       op0=ALU.mult, op1=ALU.mult).then_inc(out_set, 1)

        @block.tensor
        def _(eng):
            T = nc.tensor

            def three(dst, lhi, llo, rhi, rlo, first, last):
                T.matmul(dst, lhi, rhi, start=first, stop=False)
                T.matmul(dst, llo, rhi, start=False, stop=False)
                return T.matmul(dst, lhi, rlo, start=False, stop=last)

            def spread_mod(b):
                if b == 0:
                    eng.wait_ge(cols_set, 3)
                else:
                    eng.wait_ge(mod_copied, 2 * b)
                last_u = max(u for u, unit in enumerate(FIRST) if unit[0] == "mod" and unit[1] == b)
                eng.wait_ge(unit_done, last_u + 1)
                for i in range(2):
                    T.matmul(ps[:, 6 + i, :], ones[:], acc[:, b % 2, i * HALF:(i + 1) * HALF], start=True, stop=True).then_inc(mod_spread, 1)

            eng.wait_ge(consts_in, 16)
            eng.wait_ge(rows_in, 16 * 9)
            T.transpose(ps[:, 6, 0:R_N], stage[:], cst[0:R_N, C_ID:C_ID + R_N]).then_inc(rows_T, 1)
            for k in range(KC):
                ins = T.transpose(ps[:, 7, k * TAPS:(k + 1) * TAPS], dwst[:, k * P:(k + 1) * P], cst[0:TAPS, C_ID:C_ID + TAPS])
            ins.then_inc(rows_T, 1)
            eng.wait_ge(cc_set, KC)
            for b in range(2):
                for k in range(KC):
                    u = KC * b + k
                    eng.wait_ge(raw_in[u % RAW], 16 * (u // RAW + 1))
                    for i in range(2):
                        cols_ = slice(b * D + i * HALF, b * D + (i + 1) * HALF)
                        ins = T.matmul(ps[:, 2 * b + i, :], ccB[:, k, :], raw[:, u % RAW, i * HALF:(i + 1) * HALF],
                                       start=(k == 0), stop=False)
                    ins.then_inc(ctx_unit, 1)
                for i in range(2):
                    ins = T.matmul(ps[:, 2 * b + i, :], ones[0:1, :], brow[0:1, b * D + i * HALF:b * D + (i + 1) * HALF],
                                   start=False, stop=True)
                ins.then_inc(ctx_mod, 1)
                spread_mod(b)
            order = [(hx, 0), (hx, 1), (hc, 0), (hc, 1)]
            eng.wait_ge(h_set, 4)
            eng.wait_ge(mod_copied, 4)
            for i, (src, t) in enumerate(order):
                for a in range(2):
                    for k in range(4):
                        ins = T.transpose(ps[:, 2 * i + a, k * P:(k + 1) * P], src[:, t, (4 * a + k) * P:(4 * a + k + 1) * P], ident)
                    ins.then_inc(h_T, 1)
            nw = [0]
            nproj = [0]
            w_unit = [u for u, unit in enumerate(FIRST) if unit[0] == "w"] + [SECOND_U + i for i in range(len(SECOND))]
            base_w = [0]

            def have(n):
                u = w_unit[n]
                eng.wait_ge(unit_done, u + 1)

            def project(kind, n0, u_list, dst, left, right, done_unit):
                for k in range(KC):
                    ins = three(dst, left(k, 0), left(k, 1), right(k, 0), right(k, 1), k == 0, k == KC - 1)
                    if done_unit and k == KC // 2 - 1:
                        ins.then_inc(w_used, 1)
                return ins

            def wpart(n0, k, part, c0, width):
                tile = (whi, wlo)[part]
                return dense(tile, n0 + k // 4)[:, k % 4, c0:c0 + width]

            def release(n_before, kind="act"):
                pass

            def weights_left(n0, width_tok, acts, bank, m, done):
                dst = ps[:, bank, 0:width_tok]
                for k in range(KC):
                    T.matmul(dst, wpart(n0, k, 0, m * P, P), acts(k, 0), start=(k == 0), stop=False)
                    T.matmul(dst, wpart(n0, k, 0, m * P, P), acts(k, 1), start=False, stop=False)
                    ins = T.matmul(dst, wpart(n0, k, 1, m * P, P), acts(k, 0), start=False, stop=(k == KC - 1))
                    if done and k == 3:
                        ins.then_inc(w_used, 1)
                return ins

            def finish(ins, last):
                ins.then_inc(w_used if last else proj, 1)
                nproj[0] += 1

            def xc(k, part):
                return (hThi, hTlo)[part][:, :, k, :]

            def xonly(k, part):
                return (hThi, hTlo)[part][:, 0, k, :]

            def block_left(acts, width_tok, banks, free):
                n0 = nw[0]
                have(n0 + 1)
                for m in range(2):
                    free(nproj[0])
                    dst = ps[:, banks[nproj[0] % len(banks)], 0:width_tok]
                    if width_tok > HALF // 2:
                        dst = dst.rearrange("p (a n) -> p a n", a=2)
                    for k in range(KC):
                        T.matmul(dst, wpart(n0, k, 0, m * P, P), acts(k, 0), start=(k == 0), stop=False)
                        i2 = T.matmul(dst, wpart(n0, k, 1, m * P, P), acts(k, 0), start=False, stop=False)
                        i3 = T.matmul(dst, wpart(n0, k, 0, m * P, P), acts(k, 1), start=False, stop=(k == KC - 1))
                        if m == 1 and k == 3:
                            i3.then_inc(w_used, 1)
                    finish(i3, m == 1)
                nw[0] += DENSE

            def block_right(acts, tiles, banks, free):
                n0 = nw[0]
                have(n0 + 1)
                for i, t in enumerate(tiles):
                    free(nproj[0])
                    dst = ps[:, banks[nproj[0] % len(banks)], 0:BLOCK]
                    for k in range(KC):
                        T.matmul(dst, acts(k, 0, t), wpart(n0, k, 0, 0, BLOCK), start=(k == 0), stop=False)
                        T.matmul(dst, acts(k, 0, t), wpart(n0, k, 1, 0, BLOCK), start=False, stop=False)
                        i3 = T.matmul(dst, acts(k, 1, t), wpart(n0, k, 0, 0, BLOCK), start=False, stop=(k == KC - 1))
                        if i == len(tiles) - 1 and k == 3:
                            i3.then_inc(w_used, 1)
                    finish(i3, i == len(tiles) - 1)
                nw[0] += DENSE

            four = [0, 1, 2, 3]
            eng.wait_ge(hT_rest, 8)

            def after_copy(n):
                if n >= 4:
                    eng.wait_ge(proj_taken, n - 3)

            for _ in range(2):
                block_left(xc, SEQ + CTX, four, after_copy)
            spread_mod(2)
            for _ in range(2):
                block_right(lambda k, part, t: (hThi, hTlo)[part][:, t // 2, k, (t % 2) * P:(t % 2 + 1) * P],
                            range(4), four, after_copy)
            spread_mod(3)
            for _ in range(2):
                block_left(xonly, SEQ, four, after_copy)
            for _ in range(2):
                block_left(xonly, SEQ, four, after_copy)
            spread_mod(4)
            for _ in range(2):
                block_left(xonly, SEQ, four, after_copy)

            def after_hb(n):
                eng.wait_ge(proj_vec, n - 24 + 1)

            for _ in range(2):
                block_left(xonly, SEQ, four, after_hb)
            assert nproj[0] == PROJ["out"]

            def score(n):
                h, t = n // 2, n % 2
                lo = (h % 2) * DH
                if n >= 2:
                    eng.wait_ge(exped, n - 1)
                T.matmul(ps[:, 4 + n % 2, :], qT[lo:lo + DH, h // 2, t * P:(t + 1) * P], kT[lo:lo + DH, h // 2, :],
                         start=True, stop=False)
                eng.wait_ge(bias_masked, h + 1)
                T.matmul(ps[:, 4 + n % 2, 0:SEQ], cst[:, C_FLIP:C_FLIP + P], bias[:, h % 2, t, :],
                         start=False, stop=True).then_inc(scores, 1)

            eng.wait_ge(proj_taken, 16)
            score(0)
            score(1)
            spread_mod(5)
            eng.wait_ge(proj_vec, 8)
            for n in range(16):
                h, t = n // 2, n % 2
                eng.wait_ge(normed, n + 1)
                if n >= 2:
                    eng.wait_ge(probT_set, n - 1)
                for q in range(4):
                    ins = T.transpose(ps[:, n % 2, q * P:(q + 1) * P], prob[:, n % 2, q * P:(q + 1) * P], ident)
                ins.then_inc(prob_T, 1)
                if n + 2 < 16:
                    score(n + 2)
                eng.wait_ge(probT_set, n + 1)
                hp, lo = h // 2, (h % 2) * DH
                if n % 4 == 0 and hp >= 2:
                    eng.wait_ge(a_rest, hp - 1)
                for q in range(4):
                    ins = T.matmul(ps[lo:lo + DH, 2 + hp % 2, t * P:(t + 1) * P], vv[:, q, h * DH:(h + 1) * DH],
                                   probT[:, n % 2, q, :], start=(q == 0), stop=(q == 3))
                ins.then_inc(attended, 1)
            eng.wait_ge(a_rest, 4)

            def after_mix(base, x0):
                def free(n):
                    if n - base >= 4:
                        eng.wait_ge(x_mixed, x0 + n - base - 3)
                return free

            for _ in range(4):
                block_right(lambda k, part, t: (catHi, catLo)[part][:, k, t * P:(t + 1) * P], range(NT), four,
                            after_mix(PROJ["out"], 0))

            def experts(L):
                for t in range(NT):
                    eng.wait_ge(h_set, 4 + 4 * L + t + 1)
                    for a in range(2):
                        for k in range(4):
                            ins = T.transpose(ps[:, 2 * t + a, k * P:(k + 1) * P],
                                              htok[:, t, (4 * a + k) * P:(4 * a + k + 1) * P], ident)
                        ins.then_inc(h_T, 1)
                eng.wait_ge(small_in, 32)
                eng.wait_ge(mod_copied, 12)
                eng.wait_ge(hT_rounded, 8 + 8 * L + 4)
                for t in range(NT):
                    for k in range(KC):
                        ins = T.matmul(ps[:, BX, t * EXPERTS:(t + 1) * EXPERTS], hTr[:, k, t * P:(t + 1) * P], rw[:, k, :],
                                       start=(k == 0), stop=(k == KC - 1))
                ins.then_inc(route_pe, 1)
                eng.wait_ge(routed, 3 * L + 1)
                one = lambda t: rt[:, 6, t, 0:GROUPS]
                tri = cst[:, C_TRI:C_TRI + P]
                T.matmul(ps[:, BX, 64:68], tri, one(0), start=True, stop=True)
                T.matmul(ps[:, BX, 68:72], tri, one(1), start=True, stop=False)
                T.matmul(ps[:, BX, 68:72], ones[:], one(0), start=False, stop=True)
                T.matmul(ps[:, BX, 72:76], ones[:], one(0), start=True, stop=False)
                T.matmul(ps[:, BX, 72:76], ones[:], one(1), start=False, stop=True).then_inc(route_pe, 1)
                eng.wait_ge(flag_set, L + 1)
                for t in range(NT):
                    ins = T.matmul(ps[:, BT, t * P:(t + 1) * P], ones[:], diag[:, t, :], start=True, stop=True)
                ins.then_inc(route_pe, 1)
                eng.wait_ge(routed, 3 * L + 3)
                for tile in range(TILES):
                    dst = ps[:, BX, tile * EXPERTS:(tile + 1) * EXPERTS]
                    for i in range(2 * NT):
                        t, g_ = i // 2, (gatehi, gatelo)[i % 2]
                        ins = T.matmul(dst, pick[:, t, tile * P:(tile + 1) * P], g_[:, t, :], start=(i == 0), stop=(i == 2 * NT - 1))
                ins.then_inc(route_pe, 1)

                def gather(tile):
                    for k in range(KC):
                        dst = ps[:, k // 4, (k % 4) * P:(k % 4 + 1) * P]
                        for i in range(2 * NT):
                            t, part = i // 2, (hhi, hlo)[i % 2]
                            sel = pick[:, t, bass.ds(tile * P, P)] if not isinstance(tile, int) else pick[:, t, tile * P:(tile + 1) * P]
                            ins = T.matmul(dst, part[:, t, k * P:(k + 1) * P], sel, start=(i == 0), stop=(i == 2 * NT - 1))
                    ins.then_inc(gathered, 1)

                eng.wait_ge(route_act, 6 * L + 6)
                gather(0)

                def scatter(tn, i):
                    t, half = i // 2, i % 2
                    if i == 0:
                        tn.wait(eng, "y_rest", 1)
                        if L == 0 and tn.spill is None:
                            eng.wait_ge(mod_copied, tn.g * 4 + 12)
                    elif XBANK[i] == XBANK[i - 1]:
                        tn.wait(eng, "x_added", i)
                    dst = ps[:, XBANK[i], :]
                    T.matmul(dst, spread[:, t * P:(t + 1) * P], yhi[:, half * HALF:(half + 1) * HALF], start=True, stop=False)
                    T.matmul(dst, spread[:, t * P:(t + 1) * P], ylo[:, half * HALF:(half + 1) * HALF], start=False, stop=True) \
                     .then_inc(tn.sem("scattered"), 1)

                def transpose_hidden(tn, e):
                    tn.wait(eng, "hid_set", e + 1)
                    for k in range(FC):
                        ins = T.transpose(ps[:, BT, k * P:(k + 1) * P], hid[:, k * P:(k + 1) * P], ident)
                    ins.then_inc(tn.sem("hid_T"), 1)

                def mod_piece(tn, s, i):
                    g = tn.g
                    if i == 0:
                        tn.wait(eng, "unit_done", MOD_POS[KC * s + KC - 1] + 1)
                        if s == 0:
                            tn.wait(eng, "x_added", 4)
                    if not (s == 0 and i == 0):
                        eng.wait_ge(mod_copied, g * 4 + (12 + 2 * s + i))
                    w = MOD_BLOCK // 2
                    T.matmul(ps[:, BX, 0:w], ones[:], acc[:, s, i * w:(i + 1) * w], start=True, stop=True).then_inc(mod_spread, 1)

                order_ = expert_order()

                def turn(tn):
                    looped = tn.spill is None
                    for pos, (kind, j) in enumerate(tn.stream()):
                        if kind == "mod":
                            continue
                        e, name = order_[j // 4]
                        q = j % 4
                        n = MOE_W[L] + j
                        if looped:
                            for i in range(4):
                                if j == SCATTER[i]:
                                    scatter(tn, i)
                        for ee in range(PER_GROUP):
                            if j == HID_T[ee]:
                                transpose_hidden(tn, ee)
                                if looped and ee == PER_GROUP - 1:
                                    gather(tn.g + 1)
                        if L == 0 and looped:
                            for i in range(4):
                                if j == MOD_PE[i]:
                                    mod_piece(tn, i // 2, i % 2)
                        tn.wait(eng, "unit_done", pos + 1)
                        if name == "w2":
                            if q == 0:
                                tn.wait(eng, "hidT_rest", e + 1)
                            for half in range(2):
                                cut = slice(half * HALF, (half + 1) * HALF)
                                ins = three(ps[:, BY + half, :], hidThi[:, q, :], hidTlo[:, q, :],
                                            moe_slot(whi, n)[:, cut], moe_slot(wlo, n)[:, cut],
                                            e == 0 and q == 0, e == PER_GROUP - 1 and q == 3)
                        else:
                            bank = (BA if name == "w1" else BB)[e % 2]
                            for k in range(2):
                                cut = slice(k * FF, (k + 1) * FF)
                                ins = three(ps[:, bank, :], xghi[:, 2 * q + k, :], xglo[:, 2 * q + k, :],
                                            moe_slot(whi, n)[:, cut], moe_slot(wlo, n)[:, cut],
                                            q == 0 and k == 0, q == 3 and k == 1)
                        ins.then_inc(tn.sem("w_used"), 1)

                with eng.Fori(0, GROUPS) as g:
                    eng.wait_ge(xg_rest, g * 2 + (10 * L + 2))
                    turn(Turn(L, g, sems))
                last = Turn(L, GROUPS, sems)
                for i in range(4):
                    scatter(last, i)
                eng.wait_ge(flag_set, L + 1)
                over = eng.value_load(flag[0:1, 0:1], min_val=0, max_val=1)
                with eng.If(over > 0):
                    eng.wait_ge(xg_rest, 10 * (L + 1))
                    tn = spill_turn(L)
                    turn(tn)
                    eng.wait_ge(spread_set, 1)
                    for i in range(4):
                        scatter(tn, i)
                with eng.Else():
                    eng.nop()
                eng.end_ifs()

            experts(0)

            for t in range(NT):
                eng.wait_ge(h_set, 6 + t + 1)
                for a in range(2):
                    for k in range(4):
                        ins = T.transpose(ps[:, 2 * t + a, k * P:(k + 1) * P], fh[:, t, (4 * a + k) * P:(4 * a + k + 1) * P], ident)
                    ins.then_inc(h_T, 1)
            eng.wait_ge(hT_rest, 12)
            nproj[0] = PROJ["pw1"]
            w_off = SECOND_W - W_FIRST
            nw[0] = W_FIRST
            slot_n = [SECOND_W]

            def wpart2(n0, k, part, c0, width):
                tile = (whi, wlo)[part]
                return dense(tile, n0 + k // 4)[:, k % 4, c0:c0 + width]

            def conv(ch):
                eng.wait_ge(gate_set, ch + 1)
                for tap in range(PE_TAPS):
                    eng.wait_ge(diag_set, PE_TAPS * ch + tap + 1)
                    T.matmul(ps[:, ch, 0:SEQ], dg[:, (ch % 2) * PE_TAPS + tap, :], uT[:, ch, tap:tap + SEQ], start=(tap == 0),
                             stop=(tap == PE_TAPS - 1)).then_inc(diag_used, 1)

            done_n = SECOND_W
            for j in range(4):
                for part_i in range(2):
                    eng.wait_ge(unit_done, SECOND_U + (done_n - SECOND_W) + 2)
                    for m in range(2):
                        dst = ps[:, 2 * j + m, part_i * SEQ:(part_i + 1) * SEQ]
                        for k in range(KC):
                            a0, a1 = fThi[:, k, :], fTlo[:, k, :]
                            T.matmul(dst, wpart2(done_n, k, 0, m * P, P), a0, start=(k == 0), stop=False)
                            T.matmul(dst, wpart2(done_n, k, 1, m * P, P), a0, start=False, stop=False)
                            ins = T.matmul(dst, wpart2(done_n, k, 0, m * P, P), a1, start=False, stop=(k == KC - 1))
                            if m == 1 and k == 3:
                                ins.then_inc(w_used, 1)
                        ins.then_inc(w_used if m == 1 else proj, 1)
                    done_n += DENSE
                if j:
                    conv(2 * j - 2)
                    conv(2 * j - 1)
            conv(6)
            conv(7)
            eng.wait_ge(conv_set, KC)
            for k in range(KC):
                ins = T.matmul(ps[:, BT, 0:SEQ], ones[:], cT[:, k, :], start=(k == 0), stop=(k == KC - 1))
            ins.then_inc(ln_sum, 1)
            for k in range(KC):
                if k % 4 == 0:
                    eng.wait_ge(sq_set, k // 4 + 1)
                ins = T.matmul(ps[:, BX, 0:SEQ], ones[:], sq[:, k, :], start=(k == 0), stop=(k == KC - 1))
            ins.then_inc(ln_sum, 1)
            eng.wait_ge(s_rest, KC)
            npj = 0
            for b in range(4):
                eng.wait_ge(unit_done, SECOND_U + (done_n - SECOND_W) + 2)
                for t in range(NT):
                    if npj >= 4:
                        eng.wait_ge(x_mixed, 8 + npj - 3)
                    dst = ps[:, npj % 4, 0:BLOCK]
                    for k in range(KC):
                        a0, a1 = sThi[:, k, t * P:(t + 1) * P], sTlo[:, k, t * P:(t + 1) * P]
                        T.matmul(dst, a0, wpart2(done_n, k, 0, 0, BLOCK), start=(k == 0), stop=False)
                        T.matmul(dst, a0, wpart2(done_n, k, 1, 0, BLOCK), start=False, stop=False)
                        ins = T.matmul(dst, a1, wpart2(done_n, k, 0, 0, BLOCK), start=False, stop=(k == KC - 1))
                        if t == NT - 1 and k == 3:
                            ins.then_inc(w_used, 1)
                    ins.then_inc(w_used if t == NT - 1 else proj, 1)
                    npj += 1
                done_n += DENSE
            experts(1)


W13 = [expert_order().index((e, "w1")) * 4 for e in range(PER_GROUP)]
HID_T = [12, 20, 32, 44]
SCATTER = [4, 8, 12, 16]
XBANK = [BX] * 4
MOD_PE = [24, 28, 40, 44]
MOD_POS = [TURN[0].index(("mod", i)) for i in range(MOD_TURN)]
PROJ = {"out": 28, "pw1": 36, "pw2": 36 + 16}


def tile_ends():
    out, tiles, units = [], 0, 0
    for per, blocks in ((2, 2), (4, 2), (2, 2), (2, 2), (2, 2), (2, 2), (2, 4), (2, 8), (2, 4)):
        for _ in range(blocks):
            if units == W_FIRST:
                units = SECOND_W
            units += DENSE
            for i in range(per - 1):
                tiles += 1
                out.append(("proj", tiles))
            out.append(("w_used", units))
    return out


TILE_END = tile_ends()

_INS = ["x", "c", "ctx", "c_ctx", "norm1_g", "norm2_g", "w_mod", "b_mod", "na_w_in", "na_rpb", "sc_conv_w", "ab_w_out",
        "cf_pw1_w", "cf_pw1_b", "cf_dw_w", "cf_dw_b", "cf_ln_g", "cf_ln_b", "cf_pw2_w", "cf_pw2_b", "router_w",
        "router_b", "moe_w1", "moe_w3", "moe_w2", "final_g"]


def shape_constants():
    import numpy as np

    k = np.zeros((P, C_N), np.float32)
    k[:, C_ID:C_ID + P] = np.eye(P)
    k[:, C_TRI:C_TRI + P] = np.triu(np.ones((P, P)), 1)
    k[:, C_ROW:C_ROW + TILES * P] = np.arange(TILES * P)
    k[:, C_SLOT:C_SLOT + TILES] = np.arange(P)[:, None] + P * np.arange(TILES)
    q = np.arange(GRID_W)
    start = np.clip(q - KCOL // 2, 0, GRID_W - KCOL)
    inside = (q[None, :] >= start[:, None]) & (q[None, :] < start[:, None] + KCOL)
    k[:, C_MASK:C_MASK + GRID_W] = np.tile(np.where(inside, 0.0, -1e30)[::-1], (2, 1))
    k[:, C_FLIP:C_FLIP + P] = np.kron(np.eye(2), np.eye(GRID_W)[::-1])
    k[:, C_PRIO:C_PRIO + GROUPS] = GROUPS - np.arange(GROUPS)
    i, j = np.divmod(np.arange(PER_GROUP ** 2), PER_GROUP)
    k[:, C_LOW:C_LOW + PER_GROUP ** 2] = j < i
    k[:, C_OFF:C_OFF + PER_GROUP ** 2] = np.where(i == j, -1e30, 0.0)
    return k


def kernel(**inputs):
    import numpy as np
    import concourse.bacc as bacc
    from concourse.bass_utils import run_bass_kernel_spmd

    nc = bacc.Bacc("TRN2", target_bir_lowering=False, num_devices=1)
    arrays, args = {}, []
    for name in _INS:
        a = np.ascontiguousarray(inputs[name])
        arrays[f"in_{name}"] = a
        args.append(nc.dram_tensor(f"in_{name}", a.shape, mybir.dt.from_np(a.dtype), kind="ExternalInput").ap())
    arrays["in_consts"] = shape_constants()
    args.append(nc.dram_tensor("in_consts", [P, C_N], F32, kind="ExternalInput").ap())
    args.append(nc.dram_tensor("bias_scratch", [HEADS * 7, P], F32, kind="Internal").ap())
    args.append(nc.dram_tensor("out_0", [1, SEQ, D], F32, kind="ExternalOutput").ap())
    program(nc, *args)
    r = run_bass_kernel_spmd(nc, [arrays], core_ids=[0])
    return r.results[0]["out_0"]
```

```python
from contextlib import ExitStack

import concourse.bass as bass
from concourse import mybir

F32 = mybir.dt.float32
F32R = mybir.dt.float32r
I32 = mybir.dt.int32
ALU = mybir.AluOpType
ACT = mybir.ActivationFunctionType
AX = mybir.AxisListType

P = 128
D = 1024
KC = D // P
SEQ = 256
CTX = 256
NT = SEQ // P
HALF = 512
GRID_W = 64
ROWS = SEQ // GRID_W
HEADS = 8
DH = 64
NA = HEADS * DH
KR_MAX = 8
KCOL = 16
SC = D - NA
TAPS = 31
PAD = (TAPS - 1) // 2
EXPERTS = 16
GROUPS = 4
PER_GROUP = EXPERTS // GROUPS
FF = 512
FC = FF // P
TILES = GROUPS + 1
EPS = 1e-6

UNIT = 1024
RAW = 8
SPL = 6
BLOCK = 256
DENSE = 2
W_EXPERT = 12
W_GROUP = PER_GROUP * W_EXPERT
MOD_BLOCK = 768
MODS = 12

C_ID, C_TRI, C_ROW, C_SLOT, C_MASK, C_PRIO = 0, P, 2 * P, 2 * P + TILES * P, 2 * P + TILES * P + TILES, 0
C_PRIO = C_MASK + GRID_W
C_FLIP = C_PRIO + GROUPS
C_LOW = C_FLIP + P
C_OFF = C_LOW + PER_GROUP ** 2
C_N = C_OFF + PER_GROUP ** 2
R_C, R_CC, R_G, R_B, R_CONV, R_PW1, R_DWB, R_LNG, R_LNB = 0, 8, 16, 24, 40, 52, 68, 76, 84
R_N = 92
R_EARLY = R_CONV
PE_TAPS = 13

BA, BB, BC, BY, BT, BX = (0, 2), (1, 3), 3, 4, 6, 7


def expert_order():
    out = []
    for e in range(PER_GROUP):
        out += [(e, "w1"), (e, "w3")]
        if e:
            out.append((e - 1, "w2"))
    return out + [(PER_GROUP - 1, "w2")]


def first_stream():
    out = []

    def mod(v):
        out.extend(("mod", v, k) for k in range(KC))

    def w(name, c0, width):
        for c in range(c0, c0 + width, BLOCK):
            out.extend(("w", name, c, h) for h in range(DENSE))

    def between(name_cols, mods_, per, ahead=True):
        m = [("mod", v, k) for v in mods_ for k in range(KC)]
        first = len(out)
        for name, c0, width in name_cols:
            w(name, c0, width)
        units = out[first:]
        del out[first:]
        for u in units:
            if not ahead:
                out.append(u)
                if u is units[0]:
                    continue
            out.extend(m[:per])
            del m[:per]
            if ahead:
                out.append(u)
        out.extend(m)

    mod(0)
    mod(1)
    between([("in", NA, NA), ("in", 2 * NA, NA)], (2, 3), 2, ahead=False)
    between([("in", 0, NA), ("in", 3 * NA + SC, SC), ("in", 3 * NA + 2 * SC, SC), ("in", 3 * NA, SC)], (4, 5), 1)
    between([("out", 0, D)], (6, 7, 8), 3)
    late = out[-2 * 3 - 2:]
    del out[-2 * 3 - 2:]
    out.extend(u for u in late if u[0] == "mod")
    out.extend(u for u in late if u[0] == "w")
    mod(9)
    last, pe = [("mod", 10, k) for k in range(KC)], [("mod", 11, k) for k in range(KC)]
    out.extend(pe[:6] + last[:2] + pe[6:] + last[2:])
    return out


def by_tensor(unit):
    return unit[0] == "mod" and unit[1] in (0, 1, 11)


def second_stream():
    out = []
    for c in range(0, D, BLOCK):
        out.extend(("w", "pw1", c, h) for h in range(DENSE))
        out.extend(("w", "pw1", D + c, h) for h in range(DENSE))
    for c in range(0, D, BLOCK):
        out.extend(("w", "pw2", c, h) for h in range(DENSE))
    return out


FIRST = first_stream()
SECOND = second_stream()
PE_UNITS = sum(by_tensor(u) for u in FIRST)


def done_count(u):
    return sum(not by_tensor(x) for x in FIRST[:u + 1]) + max(0, u + 1 - len(FIRST))


def tensor_count(u):
    return sum(by_tensor(x) for x in FIRST[:u + 1])


W_FIRST = sum(u[0] == "w" for u in FIRST)
TURN_UNITS = (W_GROUP, W_GROUP)
MOE_U = (len(FIRST), len(FIRST) + GROUPS * TURN_UNITS[0] + len(SECOND))
MOE_W = (W_FIRST, W_FIRST + GROUPS * W_GROUP + len(SECOND))
SECOND_U = len(FIRST) + GROUPS * TURN_UNITS[0]
SECOND_W = W_FIRST + GROUPS * W_GROUP
assert TURN_UNITS[0] % RAW == 0 and TURN_UNITS[1] % RAW == 0 and W_GROUP % SPL == 0


def turn_stream(layer):
    out = []
    for j in range(W_GROUP):
        out.append(("w", j))
    assert len(out) == TURN_UNITS[layer]
    return out


TURN = (turn_stream(0), turn_stream(1))

PER = {
    "w_rounded": (lambda L: W_GROUP, lambda L: MOE_W[L]),
    "w_used": (lambda L: W_GROUP, lambda L: MOE_W[L]),
    "unit_done": (lambda L: TURN_UNITS[L], lambda L: MOE_U[L] - PE_UNITS),
    "xg_rounded": (lambda L: 2, lambda L: 10 * L),
    "xg_rest": (lambda L: 2, lambda L: 10 * L),
    "silu_set": (lambda L: PER_GROUP, lambda L: 4 * PER_GROUP * L),
    "hid_set": (lambda L: PER_GROUP, lambda L: 4 * PER_GROUP * L),
    "hid_T": (lambda L: PER_GROUP, lambda L: 4 * PER_GROUP * L),
    "hidT_rounded": (lambda L: PER_GROUP, lambda L: 4 * PER_GROUP * L),
    "hidT_rest": (lambda L: PER_GROUP, lambda L: 4 * PER_GROUP * L),
    "y_scaled": (lambda L: 1, lambda L: 5 * L),
    "y_rounded": (lambda L: 1, lambda L: 5 * L),
    "y_rest": (lambda L: 1, lambda L: 5 * L),
    "scattered": (lambda L: 4, lambda L: 20 * L),
    "x_added": (lambda L: 4, lambda L: 20 * L),
}
SPILL_SEMS = ("w_rounded", "w_used", "unit_done", "silu_set", "hid_set", "hid_T", "hidT_rounded", "hidT_rest",
              "y_scaled", "y_rounded", "y_rest", "scattered", "x_added")


class Turn:

    def __init__(self, L, g, sems, spill=None, spill_raw=None):
        self.L, self.g, self.sems, self.spill, self.spill_raw = L, g, sems, spill, spill_raw

    def wait(self, eng, name, k):
        per, base = (f(self.L) for f in PER[name])
        if self.spill is None:
            eng.wait_ge(self.sems[name], self.g * per + (base + k))
        elif k <= 0:
            eng.wait_ge(self.sems[name], GROUPS * per + base + k)
        else:
            eng.wait_ge(self.spill[name], k)

    def sem(self, name):
        return (self.sems if self.spill is None else self.spill)[name]

    def loaded(self, eng, pos):
        u = MOE_U[self.L] + pos
        if self.spill is None:
            eng.wait_ge(self.sems["raw_in"][u % RAW], self.g * (16 * TURN_UNITS[self.L] // RAW) + 16 * (u // RAW + 1))
        else:
            eng.wait_ge(self.spill_raw[u % RAW], 16 * (pos // RAW + 1))

    def loaded_sem(self, pos):
        u = MOE_U[self.L] + pos
        return (self.sems["raw_in"] if self.spill is None else self.spill_raw)[u % RAW]

    def stream(self):
        return TURN[self.L] if self.spill is None else TURN[1]


def program(nc, x, c, ctx, c_ctx, norm1_g, norm2_g, w_mod, b_mod, na_w_in, na_rpb, sc_conv_w, ab_w_out,
            cf_pw1_w, cf_pw1_b, cf_dw_w, cf_dw_b, cf_ln_g, cf_ln_b, cf_pw2_w, cf_pw2_b, router_w, router_b,
            moe_w1, moe_w3, moe_w2, final_g, consts, bias_scratch, out):
    with ExitStack() as stack:
        def sb(name, shape, dt=F32):
            return stack.enter_context(nc.sbuf_tensor(name, shape, dt))

        def sem(name):
            return stack.enter_context(nc.semaphore(name))

        raw = sb("raw", [P, RAW, UNIT])
        whi = sb("whi", [P, SPL, UNIT], F32R)
        wlo = sb("wlo", [P, SPL, UNIT], F32R)
        xres = sb("xres", [P, NT, D])
        mods_at = nc.sbuf_base
        mods = sb("mods", [P, 6 * D])
        g2keep = sb("g2keep", [P, D])
        acc = sb("acc", [P, 2, UNIT])
        gB = sb("gB", [P, D])
        cst = sb("cst", [P, C_N])
        ones = sb("ones", [P, P])
        zero = sb("zero", [P, 1])
        cols = sb("cols", [P, R_N])
        dwT = sb("dwT", [P, KC, TAPS])
        rw = sb("rw", [P, KC, EXPERTS])
        rb = sb("rb", [P, EXPERTS])
        stat = sb("stat", [P, 3, 4])
        flag = sb("flag", [P, 2], I32)
        mcols = sb("mcols", [P, (MODS - 6) * KC])
        pair = sb("pair", [P, KC, 2])
        room = nc.sbuf_usable_end - nc.sbuf_base - 64
        arena = nc.sbuf_base + 31 & ~31
        sb("arena", [P, room // 4])

        def at(name, shape, kb, dt=F32, base=None):
            n = 4
            for s in shape[1:]:
                n *= s
            where = (arena if base is None else base) + int(kb * 1024)
            assert base is not None or int(kb * 1024) + n <= room, (name, kb, room)
            return nc.alloc_sbuf_tensor_at(name, shape, dt, offset=where)

        hThi = at("hThi", [P, 2, KC, SEQ], 0, F32R)
        hTlo = at("hTlo", [P, 2, KC, SEQ], 16, F32R)
        hx = at("hx", [P, NT, D], 32)
        hc = at("hc", [P, NT, D], 40)
        ctxt = at("ctxt", [P, NT, D], 52)
        early = at("early", [R_EARLY, P], 0)
        stage = at("stage", [R_N - R_EARLY, P], 0.5)
        early_rows = at("early_rows", [2, 2 * D], 20)
        smod = at("smod", [P, 2 * KC, 2], 68.5)
        xT = (at("xT", [P, KC, SEQ], 60), at("ctxT", [P, KC, SEQ], 0, base=mods_at))
        dwst = at("dwst", [TAPS, D], 1)
        rpbt = at("rpbt", [HEADS * 7, P], 13)
        kT = at("kT", [P, 4, SEQ + CTX], 32)
        vv = at("vv", [P, 4, NA], 40)
        qT = at("qT", [P, 4, SEQ], 48)
        gcT = at("gcT", [P, 4, SEQ], 52)
        ghp = at("ghp", [P, 4, SEQ + 2], 56)
        cvT = at("cvT", [P, 4, SEQ], 60.25)
        catHi = at("catHi", [P, KC, SEQ], 64.5, F32R)
        catLo = at("catLo", [P, KC, SEQ], 0, F32R, base=mods_at)
        prob = at("prob", [P, 2, 512], 8)
        bias = at("bias", [P, 2, NT, SEQ], 12)
        probT = at("probT", [P, 2, 4, P], 24)
        gated = at("gated", [P, 2, SEQ], 28)
        smx = at("smx", [P, 3, 2], 30)
        ytmp = at("ytmp", [P, 2, BLOCK], 30.5)
        htok = at("htok", [P, NT, D], 0)
        xghi = at("xghi", [P, KC, P], 16, F32R)
        xglo = at("xglo", [P, KC, P], 20, F32R)
        silu = at("silu", [P, 2, FF], 24)
        hid = at("hid", [P, FF], 28)
        hidThi = at("hidThi", [P, FC, P], 30, F32R)
        hidTlo = at("hidTlo", [P, FC, P], 32, F32R)
        yg = at("yg", [P, D], 34)
        yhi = at("yhi", [P, D], 38, F32R)
        ylo = at("ylo", [P, D], 42, F32R)
        pick = at("pick", [P, NT, TILES * P], 46)
        spread = at("spread", [P, SEQ], 51, F32R)
        posB = at("posB", [P, SEQ], 52)
        gslot = at("gslot", [P, TILES, EXPERTS], 53)
        gspill = at("gspill", [P, PER_GROUP], 53.5)
        diag = at("diag", [P, NT, P], 54)
        rt = at("rt", [P, 14, NT, EXPERTS], 55)
        scoT = at("scoT", [EXPERTS, SEQ], 58.5)
        brow = at("brow", [1, D], 48)
        last_row = at("last_row", [1, D], 68.5)
        pairs = at("pairs", [P, 2, NT * GROUPS, PER_GROUP ** 2], 57.5)
        hTr = at("hTr", [P, KC, SEQ], 60)
        fThi = at("fThi", [P, KC, SEQ], 0, F32R)
        fTlo = at("fTlo", [P, KC, SEQ], 8, F32R)
        uT = at("uT", [P, KC, SEQ + 2 * PAD], 16)
        sq = at("sq", [P, KC, SEQ], 16)
        cT = at("cT", [P, KC, SEQ], 25)
        sg = at("sg", [P, 2, SEQ], 33)
        mB = at("mB", [P, SEQ], 35)
        rB = at("rB", [P, SEQ], 36)
        sThi = at("sThi", [P, KC, SEQ], 37, F32R)
        sTlo = at("sTlo", [P, KC, SEQ], 45, F32R)
        fh = at("fh", [P, NT, D], 53)
        sT = at("sT", [P, KC, SEQ], 53)
        pbB = at("pbB", [P, D], 61)
        dg = at("dg", [P, 2 * PE_TAPS, P], 37)
        ytmp2 = at("ytmp2", [P, 2, BLOCK], 8)

        ps = stack.enter_context(nc.psum_tensor("ps", [P, 8, HALF], F32))

        ident = cst[:, C_ID:C_ID + P]

        consts_in = sem("consts_in")
        early_in = sem("early_in")
        rows_in = sem("rows_in")
        x_in = sem("x_in")
        small_in = sem("small_in")
        pw2b_in = sem("pw2b_in")
        raw_in = [sem(f"raw_in{i}") for i in range(RAW)]
        w_rounded = sem("w_rounded")
        unit_done = sem("unit_done")
        tensor_unit = sem("tensor_unit")
        brow_in = sem("brow_in")
        w_used = sem("w_used")
        gb_in = sem("gb_in")
        g_folded = sem("g_folded")
        acc_clear = sem("acc_clear")
        acc_in = [sem("acc_in0"), sem("acc_in1")]
        mod_spread = sem("mod_spread")
        mod_copied = sem("mod_copied")
        mod_diag_set = sem("mod_diag_set")
        ones_set = sem("ones_set")
        rows_T = sem("rows_T")
        cols_set = sem("cols_set")
        pair_set = sem("pair_set")
        x_normed = sem("x_normed")
        xT_set = sem("xT_set")
        rows_copied = sem("rows_copied")
        early_cols = sem("early_cols")
        early_h = sem("early_h")
        early_rounded = sem("early_rounded")
        early_rest = sem("early_rest")
        squares = sem("squares")
        meansq = sem("meansq")
        root = sem("root")
        h_set = sem("h_set")
        h_T = sem("h_T")
        hT_rounded = sem("hT_rounded")
        hT_rest = sem("hT_rest")
        proj = sem("proj")
        proj_taken = sem("proj_taken")
        proj_vec = sem("proj_vec")
        b_set = sem("b_set")
        b_rounded = sem("b_rounded")
        rpb_set = sem("rpb_set")
        spread_set = sem("spread_set")
        zero_set = sem("zero_set")
        rpb_in = sem("rpb_in")
        rpb_out = sem("rpb_out")
        bias_in = [sem("bias_in0"), sem("bias_in1")]
        bias_masked = sem("bias_masked")
        scores = sem("scores")
        biased = sem("biased")
        exped = sem("exped")
        recips = sem("recips")
        normed = sem("normed")
        prob_T = sem("prob_T")
        probT_set = sem("probT_set")
        attended = sem("attended")
        a_rounded = sem("a_rounded")
        a_rest = sem("a_rest")
        x_mixed = sem("x_mixed")
        g2_kept = sem("g2_kept")
        vec = sem("vec")
        routed = sem("routed")
        pick_set = sem("pick_set")
        route_pe = sem("route_pe")
        route_act = sem("route_act")
        flag_set = sem("flag_set")
        y_clear = sem("y_clear")
        gathered = sem("gathered")
        layer_out = sem("layer_out")
        xg_rounded = sem("xg_rounded")
        xg_rest = sem("xg_rest")
        silu_set = sem("silu_set")
        hid_set = sem("hid_set")
        hid_T = sem("hid_T")
        hidT_rounded = sem("hidT_rounded")
        hidT_rest = sem("hidT_rest")
        y_scaled = sem("y_scaled")
        y_rounded = sem("y_rounded")
        y_rest = sem("y_rest")
        scattered = sem("scattered")
        x_added = sem("x_added")
        gate_set = sem("gate_set")
        diag_set = sem("diag_set")
        diag_used = sem("diag_used")
        conv_set = sem("conv_set")
        ln_sum = sem("ln_sum")
        centred = sem("centred")
        sq_set = sem("sq_set")
        s_act = sem("s_act")
        s_rounded = sem("s_rounded")
        s_rest = sem("s_rest")
        out_set = sem("out_set")
        out_done = sem("out_done")
        spill = [{n: sem(f"spill{L}_{n}") for n in SPILL_SEMS} for L in range(2)]
        spill_raw = [[sem(f"spill{L}_raw_in{i}") for i in range(RAW)] for L in range(2)]
        sems = {"w_rounded": w_rounded, "w_used": w_used, "unit_done": unit_done, "xg_rounded": xg_rounded,
                "xg_rest": xg_rest, "silu_set": silu_set, "hid_set": hid_set, "hid_T": hid_T,
                "hidT_rounded": hidT_rounded, "hidT_rest": hidT_rest, "y_scaled": y_scaled, "y_rounded": y_rounded,
                "y_rest": y_rest, "scattered": scattered, "x_added": x_added, "raw_in": raw_in}

        def spill_turn(L):
            return Turn(L, GROUPS, sems, spill[L], spill_raw[L])

        w_dram = {
            "in": na_w_in[0].rearrange("(k p) n -> p k n", p=P),
            "out": ab_w_out[0].rearrange("(k p) n -> p k n", p=P),
            "pw1": cf_pw1_w[0].rearrange("(k p) n -> p k n", p=P),
            "pw2": cf_pw2_w[0].rearrange("(k p) n -> p k n", p=P),
        }

        def dense(tile, n, h=None):
            return tile[:, n % (RAW if tile is raw else SPL), :].rearrange("p (k n) -> p k n", k=KC // DENSE)

        def moe_slot(tile, n):
            return tile[:, n % (RAW if tile is raw else SPL), :]

        def tile_done(eng, n):
            which, value = TILE_END[n]
            eng.wait_ge(proj if which == "proj" else w_used, value)

        block = stack.enter_context(nc.Block())

        @block.sync
        def _(eng):
            def free(u):
                if u >= RAW:
                    last = u - RAW
                    if last < len(FIRST) and by_tensor(FIRST[last]):
                        eng.wait_ge(tensor_unit, tensor_count(last))
                    else:
                        eng.wait_ge(unit_done, done_count(last))

            def load_dense(stream, u0):
                for i, unit in enumerate(stream):
                    u = u0 + i
                    free(u)
                    if unit[0] == "mod":
                        _, v, k = unit
                        layer, v = divmod(v, 6)
                        eng.dma_start(raw[:, u % RAW, :], w_mod[layer, k * P:(k + 1) * P, v * D:(v + 1) * D]) \
                           .then_inc(raw_in[u % RAW], 16)
                    else:
                        _, name, c0, h = unit
                        eng.dma_start(dense(raw, u), w_dram[name][:, 4 * h:4 * h + 4, c0:c0 + BLOCK]) \
                           .then_inc(raw_in[u % RAW], 16)

            order = expert_order()

            def load_turn(tn, group):
                for pos, (kind, j) in enumerate(tn.stream()):
                    slot = (MOE_U[tn.L] + pos) % RAW
                    tn.wait(eng, "unit_done", pos - RAW + 1)
                    e, name = order[j // 4]
                    q = j % 4
                    table = {"w1": moe_w1, "w3": moe_w3, "w2": moe_w2}[name]
                    src = table[tn.L, bass.ds(group * PER_GROUP + e, 1)]
                    if name == "w2":
                        src = src[0, q * P:(q + 1) * P, :]
                        dst = raw[:, slot, :]
                    else:
                        src = src[0].rearrange("(k p) n -> p k n", p=P)[:, 2 * q:2 * q + 2, :]
                        dst = raw[:, slot, :].rearrange("p (k n) -> p k n", k=2)
                    eng.dma_start(dst, src).then_inc(tn.loaded_sem(pos), 16)

            def load_experts(L):
                with eng.Fori(0, GROUPS) as g:
                    load_turn(Turn(L, g, sems), g)

            def load_spill(L):
                eng.wait_ge(flag_set, L + 1)
                over = eng.value_load(flag[0:1, 0:1], min_val=0, max_val=1)
                group = eng.value_load(flag[0:1, 1:2], min_val=0, max_val=GROUPS - 1)
                with eng.If(over > 0):
                    tn = spill_turn(L)
                    load_turn(tn, group)
                    tn.wait(eng, "unit_done", W_GROUP)
                with eng.Else():
                    eng.nop()
                eng.end_ifs()

            load_dense(FIRST[:4], 0)
            eng.dma_start(ctxt[:], ctx[0].rearrange("(t p) d -> p t d", p=P)).then_inc(x_in, 16)
            eng.dma_start(xres[:], x[0].rearrange("(t p) d -> p t d", p=P)).then_inc(x_in, 16)
            load_dense(FIRST[4:], 4)
            eng.wait_ge(tensor_unit, PE_UNITS)
            load_experts(0)
            load_spill(0)
            load_dense(SECOND, SECOND_U)
            load_experts(1)
            load_spill(1)
            for t in range(NT):
                eng.wait_ge(out_set, t + 1)
                eng.dma_start(out[0, t * P:(t + 1) * P, :], fh[:, t, :]).then_inc(out_done, 16)
            eng.wait_ge(out_done, 16 * NT)

        @block.gpsimd
        def _(eng):
            nc.gpsimd.memset(ones[:], 1.0).then_inc(ones_set, 1)
            nc.gpsimd.memset(zero[:], 0.0).then_inc(zero_set, 1)
            nc.gpsimd.memset(rpbt[:], 0.0).then_inc(rpb_set, 1)

            def clear(b, slot, width, src, spread_before):
                if spread_before is not None:
                    eng.wait_ge(mod_spread, spread_before)
                nc.gpsimd.memset(acc[:, slot, 0:width], 0.0).then_inc(acc_clear, 1)
                eng.wait_ge(acc_clear, b - 1)
                eng.dma_start(acc[0:1, slot, 0:width], src).then_inc(acc_in[slot], 16)

            def load_g(n, src):
                if n:
                    eng.wait_ge(g_folded, n)
                eng.dma_start(gB[:], src.partition_broadcast(P)).then_inc(gb_in, 16)

            for b in range(2, 4):
                clear(b, b % 2, D, b_mod[0:1, b * D:(b + 1) * D], None)
            load_g(0, norm2_g[0])
            eng.wait_ge(rpb_set, 1)
            for h in range(HEADS):
                eng.dma_start(rpbt[h * 7:(h + 1) * 7, 48:48 + 2 * KCOL - 1], na_rpb[0, h, 4:11, :]).then_inc(rpb_in, 16)
            eng.wait_ge(rpb_in, 16 * HEADS)
            eng.dma_start(bias_scratch, rpbt[:]).then_inc(rpb_out, 16)
            def clear_later(b):
                layer, v = divmod(b, 6)
                clear(b, b % 2, D, b_mod[layer:layer + 1, v * D:(v + 1) * D], spread_count(b - 2))

            for b in range(4, 7):
                clear_later(b)
            def load_bias(h):
                for t in range(NT):
                    for half in range(2):
                        src = bass.AP(tensor=bias_scratch.tensor, offset=(h * 7 + 3 - 2 * t - (1 - half)) * P,
                                      ap=[[1, GRID_W], [P, ROWS], [1, GRID_W]])
                        dst = bias[half * GRID_W:(half + 1) * GRID_W, h % 2, t, :].rearrange("p (r c) -> p r c", r=ROWS)
                        eng.dma_start(dst, src).then_inc(bias_in[h % 2], 16)

            eng.wait_ge(rpb_out, 16)
            tile_done(eng, 11)
            load_bias(0)
            load_bias(1)
            for h in range(HEADS):
                eng.wait_ge(bias_in[h % 2], 64 * (h // 2 + 1))
                full = bias[:, h % 2].rearrange("p t (r c) -> p (t r) c", r=ROWS)
                mask = cst[:, C_MASK:C_MASK + GRID_W].unsqueeze(1).broadcast_to([P, NT * ROWS, GRID_W])
                nc.gpsimd.tensor_tensor(full, full, mask, ALU.add).then_inc(bias_masked, 1)
                if 1 <= h < HEADS - 1:
                    eng.wait_ge(scores, 2 * h)
                    load_bias(h + 1)
                if h == 1:
                    clear_later(7)
                if h == 4:
                    clear_later(8)
            clear_later(9)
            clear_later(10)
            load_g(1, norm1_g[1])
            eng.wait_ge(h_T, 13)
            eng.dma_start(pbB[:], cf_pw2_b[0].partition_broadcast(P)).then_inc(pw2b_in, 16)
            load_g(2, norm2_g[1])
            load_g(3, final_g)
            for s in acc_in:
                eng.wait_ge(s, 16 * ACC_USES[acc_in.index(s)])
            eng.wait_ge(gb_in, 16 * 4)

        @block.scalar
        def _(eng):
            A = nc.scalar

            def round_dense(u, n):
                eng.wait_ge(raw_in[u % RAW], 16 * (u // RAW + 1))
                if n >= SPL:
                    eng.wait_ge(w_used, n - SPL + 1)
                A.copy(whi[:, n % SPL, :], raw[:, u % RAW, :]).then_inc(w_rounded, 1)

            def round_turn(tn, pos, j):
                tn.loaded(eng, pos)
                tn.wait(eng, "w_used", j - SPL + 1)
                A.copy(whi[:, (MOE_W[tn.L] + j) % SPL, :], raw[:, (MOE_U[tn.L] + pos) % RAW, :]).then_inc(tn.sem("w_rounded"), 1)

            def copy_mod(b):
                for i in range(2):
                    eng.wait_ge(mod_spread, spread_count(b) - 1 + i)
                    A.copy(mods[:, b * D + i * HALF:b * D + (i + 1) * HALF], ps[:, 6 + i, :]).then_inc(mod_copied, 1)

            def copy_cols(b):
                eng.wait_ge(mod_spread, spread_count(b))
                A.copy(mcols[:, (b - 6) * KC:(b - 5) * KC], ps[:, 6 + b % 2, 0:KC]).then_inc(mod_copied, 1)

            def norm(n, srcs, dsts):
                for i, (s, d) in enumerate(zip(srcs, dsts)):
                    A.activation(d, s, ACT.Square, accum_out=stat[:, 0, i:i + 1]).then_inc(squares, 1)
                eng.wait_ge(meansq, n)
                A.activation(stat[:, 2, 0:len(srcs)], stat[:, 1, 0:len(srcs)], ACT.Sqrt).then_inc(root, 1)

            units = [(u, unit) for u, unit in enumerate(FIRST)]
            dense_units = [u for u, unit in units if unit[0] == "w"]
            pending = iter(list(enumerate(dense_units)))

            def round_upto(k):
                for n, u in pending_list[:]:
                    if n < k:
                        round_dense(u, n)
                        pending_list.remove((n, u))
            pending_list = list(pending)

            eng.dma_start(early[R_C:R_C + 8, :], c.rearrange("a (k p) -> (a k) p", p=P)).then_inc(early_in, 16)
            eng.dma_start(early[R_CC:R_CC + 8, :], c_ctx.rearrange("(k p) -> k p", p=P)).then_inc(early_in, 16)
            eng.dma_start(cst[:], consts).then_inc(consts_in, 16)
            eng.dma_start(early[R_G:R_G + 8, :], norm1_g[0].rearrange("(k p) -> k p", p=P)).then_inc(early_in, 16)
            eng.dma_start(early[R_B:R_B + 16, :], b_mod[0, 0:2 * D].rearrange("(k p) -> k p", p=P)).then_inc(early_in, 16)
            eng.wait_ge(rows_T, 1)
            A.activation(pair[:].rearrange("p k s -> p s k"), ps[:, 4, 0:2 * KC].rearrange("p (s k) -> p s k", s=2), ACT.Silu) \
             .then_inc(pair_set, 1)
            A.activation(cols[:, 0:16], ps[:, 4, 0:16], ACT.Silu).then_inc(cols_set, 1)
            A.copy(cols[:, 16:R_EARLY], ps[:, 4, 16:R_EARLY]).then_inc(cols_set, 1)
            first_row = lambda r: r - R_EARLY
            for r, n, src in ((R_CONV, 12, sc_conv_w[0].rearrange("t (k p) -> (t k) p", p=P)),
                              (R_PW1, 16, cf_pw1_b[0].rearrange("(k p) -> k p", p=P)),
                              (R_DWB, 8, cf_dw_b[0].rearrange("(k p) -> k p", p=P)),
                              (R_LNG, 8, cf_ln_g[0].rearrange("(k p) -> k p", p=P)),
                              (R_LNB, 8, cf_ln_b[0].rearrange("(k p) -> k p", p=P))):
                eng.dma_start(stage[first_row(r):first_row(r) + n, :], src).then_inc(rows_in, 16)
            eng.dma_start(dwst[:], cf_dw_w[0]).then_inc(rows_in, 16)
            eng.dma_start(rw[:], router_w.rearrange("(k p) n -> p k n", p=P)).then_inc(small_in, 16)
            eng.dma_start(rb[:], router_b.partition_broadcast(P)).then_inc(small_in, 16)
            eng.wait_ge(x_in, 32)
            norm(1, [xres[:, 0], xres[:, 1], ctxt[:, 0], ctxt[:, 1]], [hx[:, 0], hx[:, 1], hc[:, 0], hc[:, 1]])
            eng.wait_ge(tensor_unit, KC)
            A.copy(early_rows[:, 0:D].rearrange("p (a n) -> p a n", a=2), ps[0:2, 0:2, :]).then_inc(rows_copied, 1)
            for n in range(8):
                i, t, a = n // 4, n // 2 % 2, n % 2
                eng.wait_ge(h_T, n + 1)
                A.copy(xT[i][:, 4 * a:4 * a + 4, t * P:(t + 1) * P], ps[:, 4 + n % 4, :].rearrange("p (k n) -> p k n", k=4)) \
                 .then_inc(xT_set, 1)
            eng.wait_ge(tensor_unit, 2 * KC)
            A.copy(early_rows[:, D:2 * D].rearrange("p (a n) -> p a n", a=2), ps[0:2, 2:4, :]).then_inc(rows_copied, 1)
            round_upto(2)
            eng.wait_ge(rpb_out, 16)
            eng.wait_ge(rows_T, 3)
            A.copy(cols[:, R_EARLY:R_N], ps[:, 4, 0:R_N - R_EARLY]).then_inc(cols_set, 1)
            A.copy(dwT[:].rearrange("p k t -> p (k t)"), ps[:, 5, 0:KC * TAPS]).then_inc(cols_set, 1)
            for k in range(KC):
                for i in range(2):
                    eng.wait_ge(early_h, 2 * k + i + 1)
                    A.copy(hThi[:, i, k, :], xT[i][:, k, :]).then_inc(early_rounded, 1)
            eng.wait_ge(cols_set, 4)
            round_upto(6)
            for n in range(4):
                tile_done(eng, n)
                A.copy(kT[:, n, :], ps[:, n % 4, :]).then_inc(proj_taken, 1)
                if n % 2 == 1:
                    round_upto(6 + n + 1)
            for n in range(8):
                blk, tile = n // 4, n % 4
                tile_done(eng, 4 + n)
                A.copy(vv[:, tile, blk * BLOCK:(blk + 1) * BLOCK], ps[:, n % 4, 0:BLOCK]).then_inc(proj_taken, 1)
                if n == 1:
                    copy_mod(2)
                if n % 4 == 3:
                    round_upto(10 + 2 * (blk + 1))
            for n in range(4):
                tile_done(eng, 12 + n)
                A.mul(qT[:, n, :], ps[:, n % 4, 0:SEQ], float(DH) ** -0.5).then_inc(proj_taken, 1)
                if n == 1:
                    copy_mod(3)
                if n % 2 == 1:
                    round_upto(14 + n + 1)
            for n in range(4):
                tile_done(eng, 16 + n)
                A.copy(gcT[:, n, :], ps[:, n % 4, 0:SEQ]).then_inc(proj_taken, 1)
                if n % 2 == 1:
                    round_upto(18 + n + 1)
            copy_mod(4)
            round_upto(24)
            for n in range(4):
                eng.wait_ge(b_set, n + 1)
                A.copy(catHi[:, 4 + n, :], gated[:, n % 2, :]).then_inc(b_rounded, 1)
            for n in range(16 + 2):
                if n < 16:
                    eng.wait_ge(biased, n + 1)
                    if n >= 2:
                        eng.wait_ge(prob_T, n - 1)
                    A.activation(prob[:, n % 2, :], ps[:, 4 + n % 2, :], ACT.Exp, bias=smx[:, 0, n % 2:n % 2 + 1],
                                 accum_out=smx[:, 1, n % 2:n % 2 + 1]).then_inc(exped, 1)
                if n == 0:
                    copy_mod(5)
                if n < 16:
                    eng.wait_ge(recips, n + 1)
                    A.activation(prob[:, n % 2, :], prob[:, n % 2, :], ACT.Copy, scale=smx[:, 2, n % 2:n % 2 + 1]).then_inc(normed, 1)
                if 1 <= n <= 16:
                    m = n - 1
                    if n % 2 == 1 and n < 12:
                        round_upto(24 + n // 2 + 1)
                    if n == 8:
                        copy_cols(6)
                    if n == 14:
                        copy_cols(7)
                    eng.wait_ge(prob_T, m + 1)
                    if m >= 2:
                        eng.wait_ge(attended, m - 1)
                    A.copy(probT[:, m % 2], ps[:, m % 2, :].rearrange("p (k n) -> p k n", k=4)).then_inc(probT_set, 1)
                if n >= 2 and (n - 2) % 4 == 3:
                    hp = (n - 2) // 4
                    eng.wait_ge(attended, n - 1)
                    A.copy(catHi[:, hp, :], ps[:, 2 + hp % 2, 0:SEQ]).then_inc(a_rounded, 1)
            eng.dma_start(brow[:], b_mod[1:2, 5 * D:6 * D]).then_inc(brow_in, 16)
            round_upto(len(dense_units))
            copy_cols(8)
            copy_cols(9)

            def experts(L):
                eng.wait_ge(x_mixed, (L + 1) * 8)
                norm(2 + 2 * L, [xres[:, 0], xres[:, 1]], [htok[:, 0], htok[:, 1]])
                if L == 0:
                    eng.wait_ge(mod_copied, spread_count(5))
                A.copy(g2keep[:], mods[:, 5 * D:6 * D]).then_inc(g2_kept, 1)
                for t in range(NT):
                    for a in range(2):
                        n = 8 + 8 * L + 2 * t + a
                        eng.wait_ge(h_T, n + 1)
                        A.copy(hTr[:, 4 * a:4 * a + 4, t * P:(t + 1) * P],
                               ps[:, 2 * t + a, :].rearrange("p (k n) -> p k n", k=4)).then_inc(hT_rounded, 1)
                eng.wait_ge(route_pe, 5 * L + 1)
                A.activation(scoT[:], ps[0:EXPERTS, BX, P:P + SEQ], ACT.Sigmoid).then_inc(route_act, 1)
                if L == 0:
                    eng.wait_ge(tensor_unit, PE_UNITS)
                    A.copy(last_row[:].rearrange("p (a n) -> p a n", a=2), ps[0:1, BY:BY + 2, :]).then_inc(rows_copied, 1)
                    copy_cols(10)
                eng.wait_ge(route_pe, 5 * L + 4)
                A.copy(posB[:], ps[:, BT, 0:SEQ]).then_inc(route_act, 1)
                eng.wait_ge(route_pe, 5 * L + 5)
                A.copy(gslot[:].rearrange("p t n -> p (t n)"), ps[:, BX, 0:TILES * EXPERTS]).then_inc(route_act, 1)
                if L == 0:
                    copy_cols(11)

                def silu_of(tn, e):
                    tn.wait(eng, "w_used", W13[e] + 4)
                    A.activation(silu[:, e % 2, :], ps[:, BA[e % 2], :], ACT.Silu).then_inc(tn.sem("silu_set"), 1)

                def hidT_round(tn, e):
                    tn.wait(eng, "hid_T", e + 1)
                    A.copy(hidThi[:], ps[:, BT, :].rearrange("p (k n) -> p k n", k=4)).then_inc(tn.sem("hidT_rounded"), 1)

                def y_round(tn):
                    tn.wait(eng, "y_scaled", 1)
                    A.copy(yhi[:], yg[:]).then_inc(tn.sem("y_rounded"), 1)

                def mod_piece(g, s, i):
                    eng.wait_ge(mod_spread, g * 4 + (SPREADS + 2 * s + i + 1))
                    w = MOD_BLOCK // 2
                    A.copy(mods[:, bass.ds(2 * MOD_BLOCK * g + (MOD_BLOCK * s + i * w), w)], ps[:, BX, 0:w]).then_inc(mod_copied, 1)

                def xg_round(g):
                    eng.wait_ge(gathered, g + (5 * L + 1))
                    for a in range(2):
                        A.copy(xghi[:, 4 * a:4 * a + 4, :], ps[:, a, :].rearrange("p (k n) -> p k n", k=4)).then_inc(xg_rounded, 1)

                def turn(tn):
                    looped = tn.spill is None
                    for pos, (kind, j) in enumerate(tn.stream()):
                        if j == XG_AT and looped:
                            xg_round(tn.g)
                        if j == 8 and looped:
                            y_round(tn)
                        for e in range(PER_GROUP):
                            if j == W13[e] + 4 + 5:
                                silu_of(tn, e)
                            if j == HID_T[e] + 6:
                                hidT_round(tn, e)
                        if L == 0 and looped:
                            for i in range(2):
                                if j == MOD_PE[i] + 6:
                                    mod_piece(tn.g, i // 2, i % 2)
                        round_turn(tn, pos, j)
                    hidT_round(tn, PER_GROUP - 1)

                with eng.Fori(0, GROUPS) as g:
                    turn(Turn(L, g, sems))
                    if L == 0:
                        mod_piece(g, 1, 0)
                        mod_piece(g, 1, 1)
                xg_round(GROUPS)
                y_round(Turn(L, GROUPS, sems))
                eng.wait_ge(flag_set, L + 1)
                over = eng.value_load(flag[0:1, 0:1], min_val=0, max_val=1)
                with eng.If(over > 0):
                    tn = spill_turn(L)
                    turn(tn)
                    y_round(tn)
                    tn.wait(eng, "w_used", W_GROUP)
                with eng.Else():
                    eng.nop()
                eng.end_ifs()

            experts(0)

            second = [("w", SECOND_U + i, SECOND_W + i) for i in range(len(SECOND))]

            def round_second(k):
                while second and second[0][2] - SECOND_W < k:
                    _, u, n = second.pop(0)
                    round_dense(u, n)
            round_second(6)
            eng.wait_ge(layer_out, 1)
            norm(3, [xres[:, 0], xres[:, 1]], [fh[:, 0], fh[:, 1]])
            for t in range(NT):
                for a in range(2):
                    n = 12 + 2 * t + a
                    eng.wait_ge(h_T, n + 1)
                    A.copy(fThi[:, 4 * a:4 * a + 4, t * P:(t + 1) * P],
                           ps[:, 2 * t + a, :].rearrange("p (k n) -> p k n", k=4)).then_inc(hT_rounded, 1)
            def diags(ch):
                if ch >= 2:
                    eng.wait_ge(diag_used, PE_TAPS * (ch - 1))
                for tap in range(PE_TAPS):
                    A.activation(dg[:, (ch % 2) * PE_TAPS + tap, :], ident, ACT.Copy, scale=dwT[:, ch, tap:tap + 1]) \
                     .then_inc(diag_set, 1)

            for j in range(4):
                for m in range(2):
                    ch = 2 * j + m
                    tile_done(eng, PROJ["pw1"] + 4 * j + 2 + m)
                    if ch >= 2:
                        eng.wait_ge(gate_set, ch - 1)
                    A.activation(sg[:, ch % 2, :], ps[:, ch, SEQ:2 * SEQ], ACT.Sigmoid,
                                 bias=cols[:, R_PW1 + 8 + ch:R_PW1 + 9 + ch]).then_inc(proj_taken, 1)
                round_second(4 * (j + 1) + 6)
                for m in range(2):
                    diags(2 * j + m)
            round_second(len(SECOND) - 2)
            for q in range(4):
                eng.wait_ge(centred, q + 1)
                A.activation(sq[:, 2 * q:2 * q + 2, :], cT[:, 2 * q:2 * q + 2, :], ACT.Square).then_inc(sq_set, 1)
            eng.wait_ge(centred, 5)
            A.activation(rB[:], mB[:], ACT.Sqrt).then_inc(root, 1)
            for q in range(4):
                eng.wait_ge(centred, 6 + q)
                for ch in (2 * q, 2 * q + 1):
                    A.activation(sT[:, ch, :], cT[:, ch, :], ACT.Silu, bias=cols[:, R_LNB + ch:R_LNB + ch + 1],
                                 scale=cols[:, R_LNG + ch:R_LNG + ch + 1]).then_inc(s_act, 1)
                eng.wait_ge(s_act, 2 * q + 2)
                A.copy(sThi[:, 2 * q:2 * q + 2, :], sT[:, 2 * q:2 * q + 2, :]).then_inc(s_rounded, 1)
            round_second(len(SECOND))
            experts(1)
            eng.wait_ge(layer_out, 2)
            norm(5, [xres[:, 0], xres[:, 1]], [fh[:, 0], fh[:, 1]])

        @block.vector
        def _(eng):
            V = nc.vector
            own = [0]

            def link(ins):
                own[0] += 1
                ins.then_inc(vec, 1)
                eng.wait_ge(vec, own[0])

            def rest_dense(u, n):
                eng.wait_ge(w_rounded, n + 1)
                V.tensor_tensor(wlo[:, n % SPL, :], raw[:, u % RAW, :], whi[:, n % SPL, :], ALU.subtract).then_inc(unit_done, 1)

            def sum_mod(u, b, k):
                eng.wait_ge(raw_in[u % RAW], 16 * (u // RAW + 1))
                if k == 0:
                    eng.wait_ge(acc_in[b % 2], 16 * (b // 2))
                else:
                    eng.wait_ge(unit_done, done_count(FIRST.index(("mod", b, k - 1))))
                V.scalar_tensor_tensor(out=acc[:, b % 2, :], in0=raw[:, u % RAW, :], scalar=cols[:, R_C + k:R_C + k + 1],
                                       in1=acc[:, b % 2, :], op0=ALU.mult, op1=ALU.add).then_inc(unit_done, 1)

            todo = [(u, unit) for u, unit in enumerate(FIRST) if not by_tensor(unit)]
            nw = [0]

            def upto(k):
                while nw[0] < k:
                    u, unit = todo.pop(0)
                    if unit[0] == "w":
                        rest_dense(u, nw[0])
                        nw[0] += 1
                    else:
                        sum_mod(u, unit[1], unit[2])

            def units(count):
                for _ in range(count):
                    if todo:
                        u, unit = todo.pop(0)
                        if unit[0] == "w":
                            rest_dense(u, nw[0])
                            nw[0] += 1
                        else:
                            sum_mod(u, unit[1], unit[2])

            def mean_eps(n, count):
                eng.wait_ge(squares, n)
                V.tensor_scalar(stat[:, 1, 0:count], stat[:, 0, 0:count], 1.0 / D, EPS, ALU.mult, ALU.add).then_inc(meansq, 1)

            def inv_root(n, count):
                eng.wait_ge(root, n)
                link(V.reciprocal(stat[:, 0, 0:count], stat[:, 2, 0:count]))

            def fold_gain(scale, n):
                eng.wait_ge(gb_in, 16 * n)
                V.scalar_tensor_tensor(out=scale, in0=scale, scalar=1.0, in1=gB[:], op0=ALU.add, op1=ALU.mult).then_inc(g_folded, 1)
                eng.wait_ge(g_folded, n)

            def modulated(dst, src, i, gain, shift):
                link(V.scalar_tensor_tensor(out=dst, in0=src, scalar=stat[:, 0, i:i + 1], in1=gain, op0=ALU.mult, op1=ALU.mult))
                V.tensor_tensor(dst, dst, shift, ALU.add).then_inc(h_set, 1)

            mean_eps(4, 4)
            inv_root(1, 4)
            for i, (src, dst, t) in enumerate(((xres, hx, 0), (xres, hx, 1), (ctxt, hc, 0), (ctxt, hc, 1))):
                V.tensor_scalar(dst[:, t, :], src[:, t, :], stat[:, 0, i:i + 1], None, ALU.mult).then_inc(x_normed, 1)
            upto(2)
            eng.wait_ge(cols_set, 2)
            eng.wait_ge(early_cols, 2)
            two = [P, 2 * KC, 2]
            link(V.tensor_tensor(smod[:], ps[:, 0, 0:4 * KC].rearrange("p (k s) -> p k s", s=2),
                                 cols[:, R_B:R_B + 2 * KC].unsqueeze(2).broadcast_to(two), ALU.add))
            link(V.scalar_tensor_tensor(out=smod[:, KC:2 * KC, :], in0=smod[:, KC:2 * KC, :], scalar=1.0,
                                        in1=cols[:, R_G:R_G + KC].unsqueeze(2).broadcast_to([P, KC, 2]), op0=ALU.add, op1=ALU.mult))
            eng.wait_ge(xT_set, 8)

            def early_remainder(k):
                for i in range(2):
                    eng.wait_ge(early_rounded, 2 * k + i + 1)
                    V.tensor_tensor(hTlo[:, i, k, :], xT[i][:, k, :], hThi[:, i, k, :], ALU.subtract).then_inc(early_rest, 1)

            for k in range(KC):
                for i in range(2):
                    V.tensor_scalar(xT[i][:, k, :], xT[i][:, k, :], smod[:, KC + k, i:i + 1], smod[:, k, i:i + 1],
                                    ALU.mult, ALU.add).then_inc(early_h, 1)
                if k:
                    early_remainder(k - 1)
            early_remainder(KC - 1)

            upto(16)
            eng.wait_ge(cols_set, 4)
            link(V.memset(ghp[:, :, 0:1], 0.0))
            link(V.memset(ghp[:, :, SEQ + 1:SEQ + 2], 0.0))
            for n in range(4):
                if n % 2 == 0:
                    upto(20 + n)
                tile_done(eng, 20 + n)
                eng.wait_ge(proj_taken, 16 + n + 1)
                V.tensor_tensor(ghp[:, n, 1:SEQ + 1], ps[:, n % 4, 0:SEQ], gcT[:, n, :], ALU.mult).then_inc(proj_vec, 1)
            for n in range(4):
                if n == 0:
                    upto(24)
                eng.wait_ge(proj_vec, n + 1)
                for tap in range(3):
                    w = cols[:, R_CONV + 4 * tap + n:R_CONV + 4 * tap + n + 1]
                    src = ghp[:, n, tap:tap + SEQ]
                    if tap == 0:
                        link(V.tensor_scalar(cvT[:, n, :], src, w, None, ALU.mult))
                    else:
                        link(V.scalar_tensor_tensor(out=cvT[:, n, :], in0=src, scalar=w, in1=cvT[:, n, :], op0=ALU.mult, op1=ALU.add))
            for n in range(4):
                tile_done(eng, 24 + n)
                if n >= 2:
                    eng.wait_ge(b_rounded, n - 1)
                V.tensor_tensor(gated[:, n % 2, :], ps[:, n % 4, 0:SEQ], cvT[:, n, :], ALU.mult).then_inc(b_set, 1)
                eng.wait_ge(b_rounded, n + 1)
                V.tensor_tensor(catLo[:, 4 + n, :], gated[:, n % 2, :], catHi[:, 4 + n, :], ALU.subtract).then_inc(proj_vec, 1)
            for n in range(16):
                eng.wait_ge(scores, n + 1)
                if n >= 2:
                    eng.wait_ge(normed, n - 1)
                V.tensor_reduce(smx[:, 0, n % 2:n % 2 + 1], ps[:, 4 + n % 2, :], AX.X, ALU.max, negate=True).then_inc(biased, 1)
                units(1)
                eng.wait_ge(exped, n + 1)
                V.reciprocal(smx[:, 2, n % 2:n % 2 + 1], smx[:, 1, n % 2:n % 2 + 1]).then_inc(recips, 1)
                if n < 14:
                    units(1)
                if n % 4 == 2 and n > 2:
                    hp = n // 4 - 1
                    eng.wait_ge(a_rounded, hp + 1)
                    V.tensor_tensor(catLo[:, hp, :], ps[:, 2 + hp % 2, 0:SEQ], catHi[:, hp, :], ALU.subtract).then_inc(a_rest, 1)
            eng.wait_ge(a_rounded, 4)
            V.tensor_tensor(catLo[:, 3, :], ps[:, 3, 0:SEQ], catHi[:, 3, :], ALU.subtract).then_inc(a_rest, 1)

            def mix(n, base, gate, tmp, extra=None):
                blk, t = n // 2, n % 2
                cols_ = slice(blk * BLOCK, (blk + 1) * BLOCK)
                tile_done(eng, base + n)
                src = ps[:, n % 4, 0:BLOCK]
                if extra is not None:
                    link(V.tensor_tensor(tmp[:, n % 2, :], src, extra[:, cols_], ALU.add))
                    src = tmp[:, n % 2, :]
                link(V.tensor_tensor(tmp[:, n % 2, :], src, gate[:, cols_], ALU.mult))
                V.tensor_tensor(xres[:, t, cols_], xres[:, t, cols_], tmp[:, n % 2, :], ALU.add).then_inc(x_mixed, 1)

            g1 = mods[:, 2 * D:3 * D]
            for n in range(8):
                if n == 2:
                    upto(32)
                mix(n, PROJ["out"], g1, ytmp)
                if 2 <= n < 6:
                    units(2)

            def experts(L):
                fold_gain(mods[:, 4 * D:5 * D], [1, 3][L])
                if L == 0:
                    units(2)
                mean_eps([6, 10][L], 2)
                inv_root([2, 5][L], 2)
                eng.wait_ge(x_mixed, 8 * (L + 1))
                for t in range(NT):
                    modulated(htok[:, t, :], xres[:, t, :], t, mods[:, 4 * D:5 * D], mods[:, 3 * D:4 * D])
                if L == 0:
                    units(6)
                (SCO, SEL, PAIR, GRP, EQ, W4, ONE, RANK, T1, GSEL, GATE, POS, RR, T2) = range(14)

                def r(i, n=EXPERTS):
                    return rt[:, i, :, 0:n]

                def grp(i):
                    return rt[:, i].rearrange("p t (g e) -> p t g e", e=PER_GROUP)

                def by_pair(tile):
                    return tile.rearrange("p n (i j) -> p n i j", i=PER_GROUP)

                sco = ps[:, BX, 0:NT * EXPERTS].rearrange("p (t n) -> p t n", t=NT)
                eng.wait_ge(route_pe, 5 * L + 2)
                eng.wait_ge(small_in, 32)
                link(V.tensor_tensor(r(SEL), sco, rb[:].unsqueeze(1).broadcast_to([P, NT, EXPERTS]), ALU.add))
                sel = rt[:, SEL].rearrange("p t (g e) -> p (t g) e", e=PER_GROUP)
                full = [P, NT * GROUPS, PER_GROUP, PER_GROUP]
                s_i = sel.unsqueeze(3).broadcast_to(full)
                s_j = sel.unsqueeze(2).broadcast_to(full)
                q0, q1 = pairs[:, 0], pairs[:, 1]
                wide = [P, NT * GROUPS, PER_GROUP ** 2]
                off = cst[:, C_OFF:C_OFF + PER_GROUP ** 2].unsqueeze(1).broadcast_to(wide)
                low = cst[:, C_LOW:C_LOW + PER_GROUP ** 2].unsqueeze(1).broadcast_to(wide)
                groups = rt[:, GRP, :, 0:GROUPS]
                link(V.tensor_tensor(by_pair(q0), s_i, s_j, ALU.add))
                V.tensor_tensor(by_pair(q1), s_j, s_i, ALU.is_ge).then_inc(vec, 1)
                own[0] += 1
                link(V.tensor_tensor(q0, q0, off, ALU.add))
                V.tensor_reduce(rt[:, RANK].rearrange("p t n -> p (t n)")[:, 0:NT * GROUPS], q0, AX.X, ALU.max).then_inc(vec, 1)
                own[0] += 1
                link(V.tensor_tensor(q1, q1, low, ALU.mult))
                link(V.tensor_tensor(by_pair(q0), s_j, s_i, ALU.is_gt))
                gsc = rt[:, RANK].rearrange("p t n -> p (t n)")[:, 0:NT * GROUPS].rearrange("p (t g) -> p t g", t=NT)
                link(V.tensor_reduce(r(EQ, 1), gsc, AX.X, ALU.max))
                link(V.tensor_tensor(r(W4, GROUPS), gsc, r(EQ, 1).broadcast_to([P, NT, GROUPS]), ALU.is_equal))
                prio = cst[:, C_PRIO:C_PRIO + GROUPS].unsqueeze(1).broadcast_to([P, NT, GROUPS])
                V.tensor_tensor(q0, q0, q1, ALU.max).then_inc(vec, 1)
                own[0] += 1
                link(V.tensor_tensor(r(W4, GROUPS), r(W4, GROUPS), prio, ALU.mult))
                link(V.tensor_reduce(r(EQ, 1), r(W4, GROUPS), AX.X, ALU.max))
                link(V.tensor_tensor(r(ONE, GROUPS), r(W4, GROUPS), r(EQ, 1).broadcast_to([P, NT, GROUPS]), ALU.is_equal))
                V.tensor_reduce(rt[:, T1].rearrange("p t (g e) -> p (t g) e", e=PER_GROUP), by_pair(q0), AX.X, ALU.add) \
                 .then_inc(routed, 1)
                eng.wait_ge(routed, 2 * L + 1)
                link(V.tensor_scalar(r(GSEL), r(T1), 1.5, None, ALU.is_lt))
                one_b = rt[:, ONE, :, 0:GROUPS].unsqueeze(3).broadcast_to([P, NT, GROUPS, PER_GROUP])
                link(V.tensor_tensor(grp(GSEL), grp(GSEL), one_b, ALU.mult))
                link(V.tensor_tensor(r(T1), r(GSEL), sco, ALU.mult))
                link(V.tensor_reduce(r(T2, 1), r(T1), AX.X, ALU.add))
                link(V.reciprocal(r(EQ, 1), r(T2, 1)))
                V.tensor_tensor(r(GATE), r(T1), r(EQ, 1).broadcast_to([P, NT, EXPERTS]), ALU.mult).then_inc(routed, 1)
                eng.wait_ge(routed, 2 * L + 2)
                eng.wait_ge(route_pe, 5 * L + 3)
                cnt = ps[:, BC, 64:64 + 3 * GROUPS]
                link(V.tensor_tensor(r(T1, GROUPS), cnt[:, 0:2 * GROUPS].rearrange("p (t g) -> p t g", t=NT), r(ONE, GROUPS), ALU.mult))
                link(V.tensor_reduce(r(POS, 1), r(T1, GROUPS), AX.X, ALU.add))
                link(V.tensor_tensor(r(T1, GROUPS), r(ONE, GROUPS), prio, ALU.mult))
                link(V.tensor_reduce(r(T2, 1), r(T1, GROUPS), AX.X, ALU.add))
                link(V.tensor_scalar(r(T2, 1), r(T2, 1), -float(P), float(P * GROUPS), ALU.mult, ALU.add))
                link(V.tensor_scalar(r(W4, 1), r(POS, 1), P - 0.5, None, ALU.is_gt))
                link(V.tensor_scalar(r(T1, 1), r(T2, 1), -1.0, float(P * GROUPS - P), ALU.mult, ALU.add))
                link(V.tensor_tensor(r(T1, 1), r(T1, 1), r(W4, 1), ALU.mult))
                link(V.tensor_tensor(r(T2, 1), r(T2, 1), r(T1, 1), ALU.add))
                link(V.tensor_tensor(r(POS, 1), r(POS, 1), r(T2, 1), ALU.add))
                for t in range(NT):
                    V.tensor_scalar(pick[:, t, :], cst[:, C_ROW:C_ROW + TILES * P], rt[:, POS, t, 0:1], None, ALU.is_equal) \
                     .then_inc(pick_set, 1)
                for t in range(NT):
                    link(V.tensor_scalar(diag[:, t, :], ident, rt[:, POS, t, 0:1], None, ALU.mult))
                link(V.tensor_scalar(rt[:, RR, 0, 0:GROUPS], cnt[:, 2 * GROUPS:3 * GROUPS], P + 0.5, None, ALU.is_gt))
                link(V.tensor_reduce(rt[:, RR, 1, 0:1], rt[:, RR, 0, 0:GROUPS], AX.X, ALU.add))
                link(V.tensor_tensor(rt[:, RR, 0, 4:8], rt[:, RR, 0, 0:GROUPS], cst[:, C_PRIO:C_PRIO + GROUPS], ALU.mult))
                link(V.tensor_reduce(rt[:, RR, 1, 1:2], rt[:, RR, 0, 4:8], AX.X, ALU.add))
                link(V.tensor_scalar(rt[:, RR, 1, 2:3], rt[:, RR, 1, 0:1], float(GROUPS), None, ALU.mult))
                link(V.tensor_tensor(rt[:, RR, 1, 1:2], rt[:, RR, 1, 2:3], rt[:, RR, 1, 1:2], ALU.subtract))
                V.tensor_copy(flag[:], rt[:, RR, 1, 0:2]).then_inc(flag_set, 1)
                V.memset(spread[:].bitcast(F32), 0.0).then_inc(y_clear, 1)
                if L == 0:
                    eng.wait_ge(rows_copied, 3)
                V.memset(ps[:, BY:BY + 2, :], 0.0).then_inc(y_clear, 1)
                if L == 0:
                    units(len(todo))
                eng.wait_ge(y_clear, 2 * L + 2)

                eng.wait_ge(route_act, 3 * L + 3)
                link(V.tensor_reduce(gspill[:], gslot[:, GROUPS, :].rearrange("p (g e) -> p e g", e=PER_GROUP), AX.X, ALU.add))

                def rest_turn(tn, pos, j):
                    n = MOE_W[L] + j
                    tn.wait(eng, "w_rounded", j + 1)
                    V.tensor_tensor(wlo[:, n % SPL, :], raw[:, (MOE_U[L] + pos) % RAW, :], whi[:, n % SPL, :],
                                    ALU.subtract).then_inc(tn.sem("unit_done"), 1)

                def mod_diag(g, s):
                    if s == 0:
                        eng.wait_ge(mod_copied, SPREADS)
                    eng.wait_ge(mod_spread, g * 4 + (SPREADS - 4 + 2 * (s + 1)))
                    n = MOD_BLOCK // P
                    V.tensor_tensor(acc[:, s, 0:MOD_BLOCK].rearrange("p (k n) -> p k n", k=n),
                                    ident.unsqueeze(1).broadcast_to([P, n, P]),
                                    mcols[:, bass.ds(g * 2 * n + s * n, n)].unsqueeze(2).broadcast_to([P, n, P]),
                                    ALU.mult).then_inc(mod_diag_set, 1)

                def xg_remainder(g):
                    for a in range(2):
                        eng.wait_ge(xg_rounded, g * 2 + (10 * L + 1 + a))
                        V.tensor_tensor(xglo[:, 4 * a:4 * a + 4, :], ps[:, a, :].rearrange("p (k n) -> p k n", k=4),
                                        xghi[:, 4 * a:4 * a + 4, :], ALU.subtract).then_inc(xg_rest, 1)

                def y_scale(tn):
                    tn.wait(eng, "w_used", 0 if tn.spill is None else W_GROUP)
                    V.tensor_tensor(yg[:].rearrange("p (a n) -> p a n", a=2), ps[:, BY:BY + 2, :],
                                    g2keep[:].rearrange("p (a n) -> p a n", a=2), ALU.mult).then_inc(tn.sem("y_scaled"), 1)

                def y_remainder(tn):
                    tn.wait(eng, "y_rounded", 1)
                    V.tensor_tensor(ylo[:], yg[:], yhi[:], ALU.subtract).then_inc(tn.sem("y_rest"), 1)

                def x_add(tn, i):
                    t, half = i // 2, i % 2
                    tn.wait(eng, "scattered", i + 1)
                    dst = xres[:, t, half * HALF:(half + 1) * HALF]
                    V.tensor_tensor(dst, dst, ps[:, XBANK[i], :], ALU.add).then_inc(tn.sem("x_added"), 1)

                def set_spread(column):
                    return V.tensor_scalar(spread[:], posB[:], column, None, ALU.is_equal)

                def hid_mul(tn, e):
                    tn.wait(eng, "silu_set", e + 1)
                    tn.wait(eng, "w_used", W13[e] + 8)
                    if tn.spill is None:
                        gate = gslot[:].rearrange("p t n -> p (t n)")[:, bass.ds(tn.g * (EXPERTS + PER_GROUP) + e, 1)]
                    else:
                        gate = gspill[:, e:e + 1]
                    V.scalar_tensor_tensor(out=hid[:], in0=silu[:, e % 2, :], scalar=gate, in1=ps[:, BB[e % 2], :],
                                           op0=ALU.mult, op1=ALU.mult).then_inc(tn.sem("hid_set"), 1)

                def hidT_remainder(tn, e):
                    tn.wait(eng, "hidT_rounded", e + 1)
                    V.tensor_tensor(hidTlo[:], ps[:, BT, :].rearrange("p (k n) -> p k n", k=4), hidThi[:], ALU.subtract) \
                     .then_inc(tn.sem("hidT_rest"), 1)

                def turn(tn):
                    looped = tn.spill is None
                    for pos, (kind, j) in enumerate(tn.stream()):
                        if looped and L == 0 and j in MOD_DVE:
                            mod_diag(tn.g, MOD_DVE.index(j))
                        if looped:
                            if j == XG_AT:
                                xg_remainder(tn.g)
                            if j == 5:
                                y_scale(tn)
                            if j == 9:
                                y_remainder(tn)
                        for e in range(PER_GROUP):
                            if j == W13[e] + 8 + 5:
                                hid_mul(tn, e)
                            if j == HID_T[e] + 6:
                                hidT_remainder(tn, e)
                        if looped:
                            for i in range(4):
                                if j == SCATTER[i] + 6:
                                    x_add(tn, i)
                            if j == SCATTER[3] + 6:
                                set_spread(cst[:, bass.ds(tn.g + C_SLOT, 1)]).then_inc(vec, 1)
                        rest_turn(tn, pos, j)
                    hidT_remainder(tn, PER_GROUP - 1)

                eng.wait_ge(g2_kept, L + 1)
                with eng.Fori(0, GROUPS) as g:
                    turn(Turn(L, g, sems))
                own[0] += GROUPS
                xg_remainder(GROUPS)
                last = Turn(L, GROUPS, sems)
                y_scale(last)
                y_remainder(last)
                for i in range(4):
                    x_add(last, i)
                eng.wait_ge(flag_set, L + 1)
                over = eng.value_load(flag[0:1, 0:1], min_val=0, max_val=1)
                with eng.If(over > 0):
                    tn = spill_turn(L)
                    set_spread(cst[:, C_SLOT + GROUPS:C_SLOT + GROUPS + 1]).then_inc(spread_set, 1)
                    turn(tn)
                    y_scale(tn)
                    y_remainder(tn)
                    for i in range(4):
                        x_add(tn, i)
                    tn.wait(eng, "x_added", 4)
                with eng.Else():
                    eng.nop()
                eng.end_ifs()
                eng.wait_ge(x_added, 20 * (L + 1))
                V.memset(stat[:, 1, :], 0.0).then_inc(layer_out, 1)

            experts(0)

            eng.wait_ge(mod_copied, SPREADS + 4 * GROUPS)
            fold_gain(mods[:, D:2 * D], 2)
            second = [(SECOND_U + i, SECOND_W + i) for i in range(len(SECOND))]

            def rest_second(k):
                while second and second[0][1] - SECOND_W < k:
                    u, n = second.pop(0)
                    rest_dense(u, n)
            rest_second(3)
            mean_eps(8, 2)
            inv_root(3, 2)
            for t in range(NT):
                modulated(fh[:, t, :], xres[:, t, :], t, mods[:, D:2 * D], mods[:, 0:D])
            rest_second(4)
            for t in range(NT):
                for a in range(2):
                    n = 12 + 2 * t + a
                    eng.wait_ge(hT_rounded, n - 8 + 1)
                    hi = fThi[:, 4 * a:4 * a + 4, t * P:(t + 1) * P]
                    lo = fTlo[:, 4 * a:4 * a + 4, t * P:(t + 1) * P]
                    V.tensor_tensor(lo, ps[:, 2 * t + a, :].rearrange("p (k n) -> p k n", k=4), hi, ALU.subtract).then_inc(hT_rest, 1)
            rest_second(6)
            link(V.memset(uT[:, :, 0:PAD], 0.0))
            link(V.memset(uT[:, :, PAD + SEQ:], 0.0))

            def conv(c0, until):
                first = own[0]
                for i, tap in enumerate(range(PE_TAPS, TAPS)):
                    for m in range(2):
                        ch = c0 + m
                        src, w = uT[:, ch, tap:tap + SEQ], dwT[:, ch, tap:tap + 1]
                        if i:
                            eng.wait_ge(vec, first + 2 * i + m - 1)
                            ins = V.scalar_tensor_tensor(out=cT[:, ch, :], in0=src, scalar=w, in1=cT[:, ch, :],
                                                         op0=ALU.mult, op1=ALU.add)
                        else:
                            eng.wait_ge(gate_set, ch + 1)
                            ins = V.tensor_scalar(cT[:, ch, :], src, w, cols[:, R_DWB + ch:R_DWB + ch + 1], ALU.mult, ALU.add)
                        ins.then_inc(vec, 1)
                        own[0] += 1
                    if i % 2 == 0 and second and second[0][1] - SECOND_W < until:
                        rest_second(second[0][1] - SECOND_W + 1)
                rest_second(until)
                for m in range(2):
                    ch = c0 + m
                    eng.wait_ge(vec, own[0] - 1 + m)
                    eng.wait_ge(diag_used, PE_TAPS * (ch + 1))
                    V.tensor_tensor(cT[:, ch, :], cT[:, ch, :], ps[:, ch, 0:SEQ], ALU.add).then_inc(conv_set, 1)

            for j in range(4):
                for m in range(2):
                    ch = 2 * j + m
                    eng.wait_ge(proj_taken, 20 + ch + 1)
                    V.scalar_tensor_tensor(out=uT[:, ch, PAD:PAD + SEQ], in0=ps[:, ch, 0:SEQ],
                                           scalar=cols[:, R_PW1 + ch:R_PW1 + ch + 1], in1=sg[:, ch % 2, :],
                                           op0=ALU.add, op1=ALU.mult).then_inc(gate_set, 1)
                conv(2 * j, min(4 * (j + 1) + 6, len(SECOND) - 2))
            rest_second(len(SECOND) - 2)
            wide = [P, 2, SEQ]
            eng.wait_ge(ln_sum, 1)
            link(V.tensor_scalar(mB[:], ps[:, 0, SEQ:2 * SEQ], 1.0 / D, None, ALU.mult))
            for q in range(4):
                V.tensor_tensor(cT[:, 2 * q:2 * q + 2, :], cT[:, 2 * q:2 * q + 2, :],
                                mB[:].unsqueeze(1).broadcast_to(wide), ALU.subtract).then_inc(centred, 1)
            eng.wait_ge(centred, 4)
            eng.wait_ge(ln_sum, 2)
            V.tensor_scalar(mB[:], ps[:, 1, 0:SEQ], 1.0 / D, EPS, ALU.mult, ALU.add).then_inc(centred, 1)
            eng.wait_ge(root, 4)
            link(V.reciprocal(mB[:], rB[:]))
            for q in range(4):
                V.tensor_tensor(cT[:, 2 * q:2 * q + 2, :], cT[:, 2 * q:2 * q + 2, :],
                                mB[:].unsqueeze(1).broadcast_to(wide), ALU.mult).then_inc(centred, 1)
            for q in range(4):
                eng.wait_ge(s_rounded, q + 1)
                V.tensor_tensor(sTlo[:, 2 * q:2 * q + 2, :], sT[:, 2 * q:2 * q + 2, :], sThi[:, 2 * q:2 * q + 2, :],
                                ALU.subtract).then_inc(s_rest, 1)
            eng.wait_ge(pw2b_in, 16)
            for n in range(8):
                if n == 2:
                    rest_second(len(SECOND))
                mix(n, PROJ["pw2"], mods[:, 2 * D:3 * D], ytmp2, pbB)
            experts(1)
            mean_eps(12, 2)
            inv_root(6, 2)
            eng.wait_ge(gb_in, 16 * 4)
            for t in range(NT):
                V.scalar_tensor_tensor(out=fh[:, t, :], in0=xres[:, t, :], scalar=stat[:, 0, t:t + 1], in1=gB[:],
                                       op0=ALU.mult, op1=ALU.mult).then_inc(out_set, 1)

        @block.tensor
        def _(eng):
            T = nc.tensor

            def three(dst, lhi, llo, rhi, rlo, first, last):
                T.matmul(dst, lhi, rhi, start=first, stop=False)
                T.matmul(dst, llo, rhi, start=False, stop=False)
                return T.matmul(dst, lhi, rlo, start=False, stop=last)

            def spread_mod(b):
                if b == 2:
                    eng.wait_ge(cols_set, 4)
                else:
                    eng.wait_ge(mod_copied, spread_count(b - 1))
                last_u = max(u for u, unit in enumerate(FIRST) if unit[0] == "mod" and unit[1] == b)
                eng.wait_ge(unit_done, done_count(last_u))
                for i in range(2):
                    T.matmul(ps[:, 6 + i, :], ones[:], acc[:, b % 2, i * HALF:(i + 1) * HALF], start=True, stop=True).then_inc(mod_spread, 1)

            def spread_cols(b):
                eng.wait_ge(mod_copied, spread_count(max(b - 2, 5)))
                last_u = max(u for u, unit in enumerate(FIRST) if unit[0] == "mod" and unit[1] == b)
                eng.wait_ge(unit_done, done_count(last_u))
                for k in range(KC):
                    ins = T.matmul(ps[:, 6 + b % 2, k:k + 1], acc[:, b % 2, k * P:(k + 1) * P], ones[:, 0:1],
                                   start=True, stop=True)
                ins.then_inc(mod_spread, 1)

            eng.wait_ge(consts_in, 16)
            eng.wait_ge(early_in, 16 * 4)
            T.transpose(ps[:, 4, 0:R_EARLY], early[:], cst[0:R_EARLY, C_ID:C_ID + R_EARLY]).then_inc(rows_T, 1)
            eng.wait_ge(pair_set, 1)
            sources = [(hx, 0), (hx, 1), (hc, 0), (hc, 1)]
            for u in range(2 * KC):
                b, k = u // KC, u % KC
                eng.wait_ge(raw_in[u % RAW], 16 * (u // RAW + 1))
                for i in range(2):
                    ins = T.matmul(ps[0:2, 2 * b + i, :], pair[:, k, :], raw[:, u % RAW, i * HALF:(i + 1) * HALF],
                                   start=(k == 0), stop=(k == KC - 1))
                ins.then_inc(tensor_unit, 1)
                n = u - KC
                if n >= 0:
                    (src, t), a = sources[n // 2], n % 2
                    if n == 0:
                        eng.wait_ge(cols_set, 2)
                    if n >= 4:
                        eng.wait_ge(xT_set, n - 3)
                    if a == 0:
                        eng.wait_ge(x_normed, n // 2 + 1)
                    for k in range(4):
                        ins = T.transpose(ps[:, 4 + n % 4, k * P:(k + 1) * P], src[:, t, (4 * a + k) * P:(4 * a + k + 1) * P], ident)
                    ins.then_inc(h_T, 1)
            for b in range(2):
                eng.wait_ge(rows_copied, b + 1)
                for k in range(KC):
                    n = KC * b + k
                    ins = T.transpose(ps[:, 0, 2 * n:2 * n + 2], early_rows[:, n * P:(n + 1) * P], cst[0:2, C_ID:C_ID + 2])
                ins.then_inc(early_cols, 1)
            eng.wait_ge(rows_in, 16 * 6)
            eng.wait_ge(xT_set, 8)
            T.transpose(ps[:, 4, 0:R_N - R_EARLY], stage[:], cst[0:R_N - R_EARLY, C_ID:C_ID + R_N - R_EARLY]).then_inc(rows_T, 1)
            for k in range(KC):
                ins = T.transpose(ps[:, 5, k * TAPS:(k + 1) * TAPS], dwst[:, k * P:(k + 1) * P], cst[0:TAPS, C_ID:C_ID + TAPS])
            ins.then_inc(rows_T, 1)
            nw = [0]
            nproj = [0]
            w_unit = [u for u, unit in enumerate(FIRST) if unit[0] == "w"] + [SECOND_U + i for i in range(len(SECOND))]
            base_w = [0]

            def have(n):
                u = w_unit[n]
                eng.wait_ge(unit_done, done_count(u))

            def project(kind, n0, u_list, dst, left, right, done_unit):
                for k in range(KC):
                    ins = three(dst, left(k, 0), left(k, 1), right(k, 0), right(k, 1), k == 0, k == KC - 1)
                    if done_unit and k == KC // 2 - 1:
                        ins.then_inc(w_used, 1)
                return ins

            def wpart(n0, k, part, c0, width):
                tile = (whi, wlo)[part]
                return dense(tile, n0 + k // 4)[:, k % 4, c0:c0 + width]

            def release(n_before, kind="act"):
                pass

            def weights_left(n0, width_tok, acts, bank, m, done):
                dst = ps[:, bank, 0:width_tok]
                for k in range(KC):
                    T.matmul(dst, wpart(n0, k, 0, m * P, P), acts(k, 0), start=(k == 0), stop=False)
                    T.matmul(dst, wpart(n0, k, 0, m * P, P), acts(k, 1), start=False, stop=False)
                    ins = T.matmul(dst, wpart(n0, k, 1, m * P, P), acts(k, 0), start=False, stop=(k == KC - 1))
                    if done and k == 3:
                        ins.then_inc(w_used, 1)
                return ins

            def finish(ins, last):
                ins.then_inc(w_used if last else proj, 1)
                nproj[0] += 1

            def xc(k, part):
                return (hThi, hTlo)[part][:, :, k, :]

            def xonly(k, part):
                return (hThi, hTlo)[part][:, 0, k, :]

            def block_left(acts, width_tok, banks, free):
                n0 = nw[0]
                have(n0 + 1)
                for m in range(2):
                    free(nproj[0])
                    dst = ps[:, banks[nproj[0] % len(banks)], 0:width_tok]
                    if width_tok > HALF // 2:
                        dst = dst.rearrange("p (a n) -> p a n", a=2)
                    for k in range(KC):
                        if nproj[0] == 0:
                            eng.wait_ge(early_rest, 2 * (k + 1))
                        T.matmul(dst, wpart(n0, k, 0, m * P, P), acts(k, 0), start=(k == 0), stop=False)
                        i2 = T.matmul(dst, wpart(n0, k, 1, m * P, P), acts(k, 0), start=False, stop=False)
                        i3 = T.matmul(dst, wpart(n0, k, 0, m * P, P), acts(k, 1), start=False, stop=(k == KC - 1))
                        if m == 1 and k == 3:
                            i3.then_inc(w_used, 1)
                    finish(i3, m == 1)
                nw[0] += DENSE

            def block_right(acts, tiles, banks, free):
                n0 = nw[0]
                have(n0 + 1)
                for i, t in enumerate(tiles):
                    free(nproj[0])
                    dst = ps[:, banks[nproj[0] % len(banks)], 0:BLOCK]
                    for k in range(KC):
                        T.matmul(dst, acts(k, 0, t), wpart(n0, k, 0, 0, BLOCK), start=(k == 0), stop=False)
                        T.matmul(dst, acts(k, 0, t), wpart(n0, k, 1, 0, BLOCK), start=False, stop=False)
                        i3 = T.matmul(dst, acts(k, 1, t), wpart(n0, k, 0, 0, BLOCK), start=False, stop=(k == KC - 1))
                        if i == len(tiles) - 1 and k == 3:
                            i3.then_inc(w_used, 1)
                    finish(i3, i == len(tiles) - 1)
                nw[0] += DENSE

            four = [0, 1, 2, 3]
            def after_copy(n):
                if n >= 4:
                    eng.wait_ge(proj_taken, n - 3)

            for _ in range(2):
                block_left(xc, SEQ + CTX, four, after_copy)
            spread_mod(2)
            for _ in range(2):
                block_right(lambda k, part, t: (hThi, hTlo)[part][:, t // 2, k, (t % 2) * P:(t % 2 + 1) * P],
                            range(4), four, after_copy)
            spread_mod(3)
            for _ in range(2):
                block_left(xonly, SEQ, four, after_copy)
            for _ in range(2):
                block_left(xonly, SEQ, four, after_copy)
            spread_mod(4)
            for _ in range(2):
                block_left(xonly, SEQ, four, after_copy)

            def after_hb(n):
                eng.wait_ge(proj_vec, n - 24 + 1)

            for _ in range(2):
                block_left(xonly, SEQ, four, after_hb)
            assert nproj[0] == PROJ["out"]

            def score(n):
                h, t = n // 2, n % 2
                lo = (h % 2) * DH
                if n >= 2:
                    eng.wait_ge(exped, n - 1)
                T.matmul(ps[:, 4 + n % 2, :], qT[lo:lo + DH, h // 2, t * P:(t + 1) * P], kT[lo:lo + DH, h // 2, :],
                         start=True, stop=False)
                eng.wait_ge(bias_masked, h + 1)
                T.matmul(ps[:, 4 + n % 2, 0:SEQ], cst[:, C_FLIP:C_FLIP + P], bias[:, h % 2, t, :],
                         start=False, stop=True).then_inc(scores, 1)

            eng.wait_ge(proj_taken, 16)
            score(0)
            score(1)
            spread_mod(5)
            eng.wait_ge(proj_vec, 8)
            for n in range(16 + 1):
                if n + 2 < 16:
                    score(n + 2)
                if n < 16:
                    eng.wait_ge(normed, n + 1)
                    if n >= 2:
                        eng.wait_ge(probT_set, n - 1)
                    for q in range(4):
                        ins = T.transpose(ps[:, n % 2, q * P:(q + 1) * P], prob[:, n % 2, q * P:(q + 1) * P], ident)
                    ins.then_inc(prob_T, 1)
                if n == 6:
                    spread_cols(6)
                if n == 12:
                    spread_cols(7)
                if n:
                    m = n - 1
                    h, t = m // 2, m % 2
                    eng.wait_ge(probT_set, m + 1)
                    hp, lo = h // 2, (h % 2) * DH
                    if m % 4 == 0 and hp >= 2:
                        eng.wait_ge(a_rest, hp - 1)
                    for q in range(4):
                        ins = T.matmul(ps[lo:lo + DH, 2 + hp % 2, t * P:(t + 1) * P], vv[:, q, h * DH:(h + 1) * DH],
                                       probT[:, m % 2, q, :], start=(q == 0), stop=(q == 3))
                    ins.then_inc(attended, 1)
            eng.wait_ge(a_rest, 4)

            def after_mix(base, x0):
                def free(n):
                    if n - base >= 4:
                        eng.wait_ge(x_mixed, x0 + n - base - 3)
                return free

            for i in range(4):
                block_right(lambda k, part, t: (catHi, catLo)[part][:, k, t * P:(t + 1) * P], range(NT), four,
                            after_mix(PROJ["out"], 0))
                if i == 0:
                    spread_cols(8)
            spread_cols(9)
            last_units = [u for u, unit in enumerate(FIRST) if unit[0] == "mod" and unit[1] == MODS - 1]

            def last_block(count):
                for _ in range(count):
                    u = last_units.pop(0)
                    k = FIRST[u][2]
                    if k == 0:
                        eng.wait_ge(brow_in, 16)
                        for i in range(2):
                            T.matmul(ps[0:1, BY + i, :], ones[0:1, 0:1], brow[0:1, i * HALF:(i + 1) * HALF], start=True, stop=False)
                    eng.wait_ge(raw_in[u % RAW], 16 * (u // RAW + 1))
                    for i in range(2):
                        ins = T.matmul(ps[0:1, BY + i, :], pair[:, k, 0:1], raw[:, u % RAW, i * HALF:(i + 1) * HALF],
                                       start=False, stop=(k == KC - 1))
                    ins.then_inc(tensor_unit, 1)

            last_block(6)

            def experts(L):
                for t in range(NT):
                    eng.wait_ge(h_set, 4 * L + t + 1)
                    for a in range(2):
                        for k in range(4):
                            ins = T.transpose(ps[:, 2 * t + a, k * P:(k + 1) * P],
                                              htok[:, t, (4 * a + k) * P:(4 * a + k + 1) * P], ident)
                        ins.then_inc(h_T, 1)
                eng.wait_ge(small_in, 32)
                eng.wait_ge(mod_copied, spread_count(9))
                eng.wait_ge(hT_rounded, 8 * L + 4)
                for k in range(KC):
                    ins = T.matmul(ps[0:EXPERTS, BX, P:P + SEQ], rw[:, k, :], hTr[:, k, :], start=(k == 0), stop=(k == KC - 1))
                ins.then_inc(route_pe, 1)
                eng.wait_ge(route_act, 3 * L + 1)
                for t in range(NT):
                    ins = T.transpose(ps[:, BX, t * EXPERTS:(t + 1) * EXPERTS], scoT[:, t * P:(t + 1) * P],
                                      cst[0:EXPERTS, C_ID:C_ID + EXPERTS])
                ins.then_inc(route_pe, 1)
                if L == 0:
                    last_block(2)
                eng.wait_ge(routed, 2 * L + 1)
                one = lambda t: rt[:, 6, t, 0:GROUPS]
                tri = cst[:, C_TRI:C_TRI + P]
                T.matmul(ps[:, BC, 64:68], tri, one(0), start=True, stop=True)
                T.matmul(ps[:, BC, 68:72], tri, one(1), start=True, stop=False)
                T.matmul(ps[:, BC, 68:72], ones[:], one(0), start=False, stop=True)
                T.matmul(ps[:, BC, 72:76], ones[:], one(0), start=True, stop=False)
                T.matmul(ps[:, BC, 72:76], ones[:], one(1), start=False, stop=True).then_inc(route_pe, 1)
                def gather(tile):
                    for k in range(KC):
                        dst = ps[:, k // 4, (k % 4) * P:(k % 4 + 1) * P]
                        for t in range(NT):
                            sel = pick[:, t, bass.ds(tile * P, P)] if not isinstance(tile, int) else pick[:, t, tile * P:(tile + 1) * P]
                            ins = T.matmul(dst, htok[:, t, k * P:(k + 1) * P], sel, start=(t == 0), stop=(t == NT - 1))
                    ins.then_inc(gathered, 1)

                if L == 0:
                    spread_cols(10)
                eng.wait_ge(pick_set, 2 * L + 2)
                gather(0)
                eng.wait_ge(flag_set, L + 1)
                eng.wait_ge(mod_copied, spread_count(10))
                for t in range(NT):
                    ins = T.matmul(ps[:, BT, t * P:(t + 1) * P], ones[:], diag[:, t, :], start=True, stop=True)
                ins.then_inc(route_pe, 1)
                eng.wait_ge(routed, 2 * L + 2)
                for tile in range(TILES):
                    dst = ps[:, BX, tile * EXPERTS:(tile + 1) * EXPERTS]
                    for t in range(NT):
                        ins = T.matmul(dst, pick[:, t, tile * P:(tile + 1) * P], rt[:, 10, t, :], start=(t == 0), stop=(t == NT - 1))
                ins.then_inc(route_pe, 1)
                if L == 0:
                    eng.wait_ge(route_act, 3)
                    eng.wait_ge(rows_copied, 3)
                    for k in range(KC):
                        ins = T.transpose(ps[:, BX, k:k + 1], last_row[0:1, k * P:(k + 1) * P], cst[0:1, C_ID:C_ID + 1])
                    ins.then_inc(mod_spread, 1)

                def scatter(tn, i):
                    t, half = i // 2, i % 2
                    if i == 0:
                        tn.wait(eng, "y_rest", 1)
                        if L == 0 and tn.spill is None:
                            eng.wait_ge(mod_copied, tn.g * 4 + SPREADS)
                    elif XBANK[i] == XBANK[i - 1]:
                        tn.wait(eng, "x_added", i)
                    dst = ps[:, XBANK[i], :]
                    T.matmul(dst, spread[:, t * P:(t + 1) * P], yhi[:, half * HALF:(half + 1) * HALF], start=True, stop=False)
                    T.matmul(dst, spread[:, t * P:(t + 1) * P], ylo[:, half * HALF:(half + 1) * HALF], start=False, stop=True) \
                     .then_inc(tn.sem("scattered"), 1)

                def transpose_hidden(tn, e):
                    tn.wait(eng, "hid_set", e + 1)
                    for k in range(FC):
                        ins = T.transpose(ps[:, BT, k * P:(k + 1) * P], hid[:, k * P:(k + 1) * P], ident)
                    ins.then_inc(tn.sem("hid_T"), 1)

                def mod_piece(tn, s, i):
                    g = tn.g
                    if i == 0:
                        eng.wait_ge(mod_diag_set, g * 2 + (s + 1))
                        if s == 0:
                            tn.wait(eng, "x_added", 4)
                    if not (s == 0 and i == 0):
                        eng.wait_ge(mod_copied, g * 4 + (SPREADS + 2 * s + i))
                    w = MOD_BLOCK // 2
                    T.matmul(ps[:, BX, 0:w], ones[:], acc[:, s, i * w:(i + 1) * w], start=True, stop=True).then_inc(mod_spread, 1)

                order_ = expert_order()

                def turn(tn):
                    looped = tn.spill is None
                    for pos, (kind, j) in enumerate(tn.stream()):
                        e, name = order_[j // 4]
                        q = j % 4
                        n = MOE_W[L] + j
                        if looped:
                            for i in range(4):
                                if j == SCATTER[i]:
                                    scatter(tn, i)
                        for ee in range(PER_GROUP):
                            if j == HID_T[ee]:
                                transpose_hidden(tn, ee)
                                if looped and ee == PER_GROUP - 1:
                                    gather(tn.g + 1)
                        if L == 0 and looped:
                            for i in range(4):
                                if j == MOD_PE[i]:
                                    mod_piece(tn, i // 2, i % 2)
                        tn.wait(eng, "unit_done", pos + 1)
                        if name == "w2":
                            if q == 0:
                                tn.wait(eng, "hidT_rest", e + 1)
                            for half in range(2):
                                cut = slice(half * HALF, (half + 1) * HALF)
                                ins = three(ps[:, BY + half, :], hidThi[:, q, :], hidTlo[:, q, :],
                                            moe_slot(whi, n)[:, cut], moe_slot(wlo, n)[:, cut],
                                            e == 0 and q == 0, e == PER_GROUP - 1 and q == 3)
                        else:
                            bank = (BA if name == "w1" else BB)[e % 2]
                            for k in range(2):
                                cut = slice(k * FF, (k + 1) * FF)
                                ins = three(ps[:, bank, :], xghi[:, 2 * q + k, :], xglo[:, 2 * q + k, :],
                                            moe_slot(whi, n)[:, cut], moe_slot(wlo, n)[:, cut],
                                            q == 0 and k == 0, q == 3 and k == 1)
                        ins.then_inc(tn.sem("w_used"), 1)

                with eng.Fori(0, GROUPS) as g:
                    eng.wait_ge(xg_rest, g * 2 + (10 * L + 2))
                    turn(Turn(L, g, sems))
                last = Turn(L, GROUPS, sems)
                for i in range(4):
                    scatter(last, i)
                eng.wait_ge(flag_set, L + 1)
                over = eng.value_load(flag[0:1, 0:1], min_val=0, max_val=1)
                with eng.If(over > 0):
                    eng.wait_ge(xg_rest, 10 * (L + 1))
                    tn = spill_turn(L)
                    turn(tn)
                    eng.wait_ge(spread_set, 1)
                    for i in range(4):
                        scatter(tn, i)
                with eng.Else():
                    eng.nop()
                eng.end_ifs()

            experts(0)

            for t in range(NT):
                eng.wait_ge(h_set, 2 + t + 1)
                for a in range(2):
                    for k in range(4):
                        ins = T.transpose(ps[:, 2 * t + a, k * P:(k + 1) * P], fh[:, t, (4 * a + k) * P:(4 * a + k + 1) * P], ident)
                    ins.then_inc(h_T, 1)
            eng.wait_ge(hT_rest, 4)
            nproj[0] = PROJ["pw1"]
            w_off = SECOND_W - W_FIRST
            nw[0] = W_FIRST
            slot_n = [SECOND_W]

            def wpart2(n0, k, part, c0, width):
                tile = (whi, wlo)[part]
                return dense(tile, n0 + k // 4)[:, k % 4, c0:c0 + width]

            def conv(ch):
                eng.wait_ge(gate_set, ch + 1)
                for tap in range(PE_TAPS):
                    eng.wait_ge(diag_set, PE_TAPS * ch + tap + 1)
                    T.matmul(ps[:, ch, 0:SEQ], dg[:, (ch % 2) * PE_TAPS + tap, :], uT[:, ch, tap:tap + SEQ], start=(tap == 0),
                             stop=(tap == PE_TAPS - 1)).then_inc(diag_used, 1)

            def channel_sums(ch):
                for k in (ch, ch + 1):
                    eng.wait_ge(conv_set, k + 1)
                    ins = T.matmul(ps[:, 0, SEQ:2 * SEQ], ones[:], cT[:, k, :], start=(k == 0), stop=(k == KC - 1))
                if k == KC - 1:
                    ins.then_inc(ln_sum, 1)

            done_n = SECOND_W
            for j in range(4):
                for part_i in range(2):
                    eng.wait_ge(unit_done, done_count(SECOND_U + (done_n - SECOND_W) + 1))
                    for m in range(2):
                        dst = ps[:, 2 * j + m, part_i * SEQ:(part_i + 1) * SEQ]
                        for k in range(KC):
                            a0, a1 = fThi[:, k, :], fTlo[:, k, :]
                            T.matmul(dst, wpart2(done_n, k, 0, m * P, P), a0, start=(k == 0), stop=False)
                            T.matmul(dst, wpart2(done_n, k, 1, m * P, P), a0, start=False, stop=False)
                            ins = T.matmul(dst, wpart2(done_n, k, 0, m * P, P), a1, start=False, stop=(k == KC - 1))
                            if m == 1 and k == 3:
                                ins.then_inc(w_used, 1)
                        ins.then_inc(w_used if m == 1 else proj, 1)
                    done_n += DENSE
                if j:
                    conv(2 * j - 2)
                    conv(2 * j - 1)
                if j >= 2:
                    channel_sums(2 * j - 4)
            conv(6)
            conv(7)
            channel_sums(4)
            channel_sums(6)
            for k in range(KC):
                if k % 2 == 0:
                    eng.wait_ge(sq_set, k // 2 + 1)
                ins = T.matmul(ps[:, 1, 0:SEQ], ones[:], sq[:, k, :], start=(k == 0), stop=(k == KC - 1))
            ins.then_inc(ln_sum, 1)
            npj = 0
            for b in range(4):
                eng.wait_ge(unit_done, done_count(SECOND_U + (done_n - SECOND_W) + 1))
                for t in range(NT):
                    if npj >= 4:
                        eng.wait_ge(x_mixed, 8 + npj - 3)
                    dst = ps[:, npj % 4, 0:BLOCK]
                    for k in range(KC):
                        if npj == 0 and k % 2 == 0:
                            eng.wait_ge(s_rest, k // 2 + 1)
                        a0, a1 = sThi[:, k, t * P:(t + 1) * P], sTlo[:, k, t * P:(t + 1) * P]
                        T.matmul(dst, a0, wpart2(done_n, k, 0, 0, BLOCK), start=(k == 0), stop=False)
                        T.matmul(dst, a0, wpart2(done_n, k, 1, 0, BLOCK), start=False, stop=False)
                        ins = T.matmul(dst, a1, wpart2(done_n, k, 0, 0, BLOCK), start=False, stop=(k == KC - 1))
                        if t == NT - 1 and k == 3:
                            ins.then_inc(w_used, 1)
                    ins.then_inc(w_used if t == NT - 1 else proj, 1)
                    npj += 1
                done_n += DENSE
            experts(1)


W13 = [expert_order().index((e, "w1")) * 4 for e in range(PER_GROUP)]
HID_T = [12, 20, 32, 44]
SCATTER = [10, 13, 16, 19]
XG_AT = 2
XBANK = [BX] * 4
MOD_PE = [34, 38, 42, 46]
MOD_DVE = [30, 38]
def spread_count(b):
    return 2 * (b - 1) if b < 6 else 8 + b - 5


SPREADS = spread_count(MODS - 1)
ACC_USES = (5, 4)
PROJ = {"out": 28, "pw1": 36, "pw2": 36 + 16}


def tile_ends():
    out, tiles, units = [], 0, 0
    for per, blocks in ((2, 2), (4, 2), (2, 2), (2, 2), (2, 2), (2, 2), (2, 4), (2, 8), (2, 4)):
        for _ in range(blocks):
            if units == W_FIRST:
                units = SECOND_W
            units += DENSE
            for i in range(per - 1):
                tiles += 1
                out.append(("proj", tiles))
            out.append(("w_used", units))
    return out


TILE_END = tile_ends()

_INS = ["x", "c", "ctx", "c_ctx", "norm1_g", "norm2_g", "w_mod", "b_mod", "na_w_in", "na_rpb", "sc_conv_w", "ab_w_out",
        "cf_pw1_w", "cf_pw1_b", "cf_dw_w", "cf_dw_b", "cf_ln_g", "cf_ln_b", "cf_pw2_w", "cf_pw2_b", "router_w",
        "router_b", "moe_w1", "moe_w3", "moe_w2", "final_g"]


def shape_constants():
    import numpy as np

    k = np.zeros((P, C_N), np.float32)
    k[:, C_ID:C_ID + P] = np.eye(P)
    k[:, C_TRI:C_TRI + P] = np.triu(np.ones((P, P)), 1)
    k[:, C_ROW:C_ROW + TILES * P] = np.arange(TILES * P)
    k[:, C_SLOT:C_SLOT + TILES] = np.arange(P)[:, None] + P * np.arange(TILES)
    q = np.arange(GRID_W)
    start = np.clip(q - KCOL // 2, 0, GRID_W - KCOL)
    inside = (q[None, :] >= start[:, None]) & (q[None, :] < start[:, None] + KCOL)
    k[:, C_MASK:C_MASK + GRID_W] = np.tile(np.where(inside, 0.0, -1e30)[::-1], (2, 1))
    k[:, C_FLIP:C_FLIP + P] = np.eye(P)[::-1]
    k[:, C_PRIO:C_PRIO + GROUPS] = GROUPS - np.arange(GROUPS)
    i, j = np.divmod(np.arange(PER_GROUP ** 2), PER_GROUP)
    k[:, C_LOW:C_LOW + PER_GROUP ** 2] = j < i
    k[:, C_OFF:C_OFF + PER_GROUP ** 2] = np.where(i == j, -1e30, 0.0)
    return k


def kernel(**inputs):
    import numpy as np
    import concourse.bacc as bacc
    from concourse.bass_utils import run_bass_kernel_spmd

    nc = bacc.Bacc("TRN2", target_bir_lowering=False, num_devices=1)
    arrays, args = {}, []
    for name in _INS:
        a = np.ascontiguousarray(inputs[name])
        arrays[f"in_{name}"] = a
        args.append(nc.dram_tensor(f"in_{name}", a.shape, mybir.dt.from_np(a.dtype), kind="ExternalInput").ap())
    arrays["in_consts"] = shape_constants()
    args.append(nc.dram_tensor("in_consts", [P, C_N], F32, kind="ExternalInput").ap())
    args.append(nc.dram_tensor("bias_scratch", [HEADS * 7, P], F32, kind="Internal").ap())
    args.append(nc.dram_tensor("out_0", [1, SEQ, D], F32, kind="ExternalOutput").ap())
    program(nc, *args)
    r = run_bass_kernel_spmd(nc, [arrays], core_ids=[0])
    return r.results[0]["out_0"]
```
